# Optimizing a Trainium2 kernel written in Bass

```python
import jax
import jax.numpy as jnp
from jax import lax
import numpy as np

D_MODEL = 1024
BATCH = 1
SEQ = 512
DEPTH = 2

CTX_LEN = 256
GRID_W = 64
N_MOD = 6
EPS = 1e-6
N_EVEN = (DEPTH + 1) // 2
N_ODD = DEPTH // 2
LRU_WIDTH = D_MODEL
LRU_HEADS = 8
LRU_HEAD_DIM = LRU_WIDTH // LRU_HEADS
LRU_C = 8.0
CONV_W = 4
GLA_HEADS = 4
GLA_DK = D_MODEL // 2
GLA_DV = D_MODEL
GLA_RANK = 16
GLA_TAU = 16.0
HGRN_HEADS = 8
HGRN_DIM = D_MODEL
CHUNK = 64
N_EXPERTS = 64
TOP_K = 8
N_GROUPS = 8
TOPK_GROUPS = 4
EXPERT_FF = D_MODEL // 4
SHARED_FF = D_MODEL // 4
ROUTED_SCALE = 2.5
MOE_BLOCK = 128
AB_SIZES = (LRU_WIDTH, LRU_WIDTH, GLA_DK, GLA_DK, GLA_DV, GLA_DV, 2 * GLA_RANK)
C_SIZES = (HGRN_DIM,) * 5

kernel_name = 'hybrid_rglru_gla_hgrn2_moe_prefix_dit'

def split_cols(u, sizes):
    out, off = [], 0
    for s in sizes:
        out.append(u[..., off:off + s])
        off += s
    return out

def rmsnorm(t, gain):
    tf = t.astype(jnp.float32)
    tf = tf * lax.rsqrt(jnp.mean(tf * tf, axis=-1, keepdims=True) + EPS)
    return tf.astype(t.dtype) * gain

def head_rmsnorm(t):
    return t * lax.rsqrt(jnp.mean(t * t, axis=-1, keepdims=True) + EPS)

def to_heads(t, n_heads):
    b, s, _ = t.shape
    return t.reshape(b, s, n_heads, -1).transpose(0, 2, 1, 3)

def from_heads(t):
    b, h, s, d = t.shape
    return t.transpose(0, 2, 1, 3).reshape(b, s, h * d)

def grid_transpose(t, rows, cols):
    b, n, d = t.shape
    return t.reshape(b, rows, cols, d).transpose(0, 2, 1, 3).reshape(b, n, d)

def prefix_order(t_ctx, t_lat, reverse, axis):
    if reverse:
        t_ctx, t_lat = jnp.flip(t_ctx, axis), jnp.flip(t_lat, axis)
    return jnp.concatenate([t_ctx, t_lat], axis=axis)

def split_order(t, n_ctx, reverse, axis):
    t_ctx, t_lat = jnp.split(t, [n_ctx], axis=axis)
    if reverse:
        t_ctx, t_lat = jnp.flip(t_ctx, axis), jnp.flip(t_lat, axis)
    return t_ctx, t_lat

def centred_dwconv(t, w, b):
    s = t.shape[1]
    left = CONV_W // 2
    tp = jnp.pad(t, ((0, 0), (left, CONV_W - 1 - left), (0, 0)))
    return b + sum(tp[:, j:j + s] * w[j] for j in range(CONV_W))

def rglru_gates(xc, wa, ba, wi, bi, lam):
    b, s, _ = xc.shape
    xf = xc.astype(jnp.float32)
    xh = xf.reshape(b, s, LRU_HEADS, LRU_HEAD_DIM)
    r = jax.nn.sigmoid(jnp.einsum('bshd,hde->bshe', xh, wa.astype(jnp.float32)).reshape(b, s, LRU_WIDTH) + ba.astype(jnp.float32))
    i = jax.nn.sigmoid(jnp.einsum('bshd,hde->bshe', xh, wi.astype(jnp.float32)).reshape(b, s, LRU_WIDTH) + bi.astype(jnp.float32))
    log_a = -LRU_C * r * jax.nn.softplus(-lam.astype(jnp.float32))
    return jnp.exp(log_a), jnp.sqrt(-jnp.expm1(2.0 * log_a)) * (i * xf)

def linear_scan(a, u):
    def combine(l, r):
        return l[0] * r[0], r[0] * l[1] + r[1]
    return lax.associative_scan(combine, (a, u), axis=1)[1]

def chunked_gated_linear(q, k, v, log_a):
    bsz, nh, s, dk = q.shape
    dv = v.shape[-1]
    n = s // CHUNK
    qc = q.astype(jnp.float32).reshape(bsz, nh, n, CHUNK, dk)
    kc = k.astype(jnp.float32).reshape(bsz, nh, n, CHUNK, dk)
    vc = v.astype(jnp.float32).reshape(bsz, nh, n, CHUNK, dv)
    b = jnp.cumsum(log_a.astype(jnp.float32).reshape(bsz, nh, n, CHUNK, dk), axis=3)
    b_ref = b[:, :, :, CHUNK // 2 - 1:CHUNK // 2]
    b_last = b[:, :, :, -1:]
    scores = jnp.einsum('bhncd,bhnsd->bhncs', qc * jnp.exp(b - b_ref), kc * jnp.exp(b_ref - b))
    scores = jnp.where(jnp.tril(jnp.ones((CHUNK, CHUNK), dtype=bool)), scores, 0.0)
    o_intra = jnp.einsum('bhncs,bhnsv->bhncv', scores, vc)
    q_dec = qc * jnp.exp(b)
    k_dec = kc * jnp.exp(b_last - b)
    chunk_decay = jnp.exp(b[:, :, :, -1])

    def step(state, inp):
        qd, kd, vv, dec = inp
        o = jnp.einsum('bhcd,bhdv->bhcv', qd, state)
        state = dec[..., None] * state + jnp.einsum('bhcd,bhcv->bhdv', kd, vv)
        return state, o

    xs = tuple(jnp.moveaxis(t, 2, 0) for t in (q_dec, k_dec, vc, chunk_decay))
    _, o_inter = lax.scan(step, jnp.zeros((bsz, nh, dk, dv), jnp.float32), xs)
    return (o_intra + jnp.moveaxis(o_inter, 0, 2)).reshape(bsz, nh, s, dv)

def directional_chunked(q, k, v, g, n_ctx, reverse):
    ordered = [prefix_order(t_c, t_l, reverse, 2) for t_c, t_l in (q, k, v, g)]
    return split_order(chunked_gated_linear(*ordered), n_ctx, reverse, 2)

def gla_log_alpha(alr, wa2, ba):
    z = alr.astype(jnp.float32) @ wa2.astype(jnp.float32) + ba.astype(jnp.float32)
    return to_heads(jax.nn.log_sigmoid(z) / GLA_TAU, GLA_HEADS)

def mixer_ab(h_ctx, h_lat, w_in, conv_w, conv_b, lru_wa, lru_ba, lru_wi, lru_bi, lru_lambda,
             gla_wa2, gla_ba, w_out):
    n_ctx = h_ctx.shape[1]
    dt = h_lat.dtype
    cols = [split_cols(h @ w_in, AB_SIZES) for h in (h_ctx, h_lat)]
    conv = [centred_dwconv(cl[1], conv_w, conv_b) for cl in cols]
    rec = [0.0, 0.0]
    for d in range(2):
        rev = d == 1
        gates = [rglru_gates(xc, lru_wa[d], lru_ba[d], lru_wi[d], lru_bi[d], lru_lambda[d]) for xc in conv]
        a = prefix_order(gates[0][0], gates[1][0], rev, 1)
        u = prefix_order(gates[0][1], gates[1][1], rev, 1)
        hs = split_order(linear_scan(a, u), n_ctx, rev, 1)
        rec = [rec[j] + hs[j] for j in range(2)]
    y_a = [jax.nn.gelu(cl[0]) * r.astype(dt) for cl, r in zip(cols, rec)]
    q = tuple(to_heads(cl[2] * (GLA_DK // GLA_HEADS) ** -0.5, GLA_HEADS) for cl in cols)
    k = tuple(to_heads(cl[3], GLA_HEADS) for cl in cols)
    v = tuple(to_heads(cl[4], GLA_HEADS) for cl in cols)
    att = [0.0, 0.0]
    for d in range(2):
        g = tuple(gla_log_alpha(cl[6][..., d * GLA_RANK:(d + 1) * GLA_RANK], gla_wa2[d], gla_ba[d]) for cl in cols)
        o = directional_chunked(q, k, v, g, n_ctx, d == 1)
        att = [att[j] + o[j] for j in range(2)]
    y_b = [from_heads(head_rmsnorm(o)).astype(dt) * jax.nn.silu(cl[5]) for cl, o in zip(cols, att)]
    out_ctx = jnp.concatenate([y_a[0], y_b[0]], axis=-1) @ w_out
    out_lat = jnp.concatenate([y_a[1], y_b[1]], axis=-1) @ w_out
    return out_ctx, out_lat

def mixer_c(h_ctx, h_lat, layer, w_in, lb_logits, w_out):
    n_ctx = h_ctx.shape[1]
    dt = h_lat.dtype
    rows = h_lat.shape[1] // GRID_W
    h_lat = grid_transpose(h_lat, rows, GRID_W)
    lb_cum = jnp.cumsum(jax.nn.softmax(lb_logits.astype(jnp.float32), axis=0), axis=0)
    lb = lb_cum[layer] - lb_cum[0]
    log_lb, log_ub = jnp.log(lb), jnp.log1p(-lb)

    def forget(z):
        zf = z.astype(jnp.float32)
        log_f = jnp.logaddexp(log_lb, log_ub + jax.nn.log_sigmoid(zf))
        one_minus_f = jnp.exp(log_ub) * jax.nn.sigmoid(-zf)
        return to_heads(log_f, HGRN_HEADS), to_heads(one_minus_f, HGRN_HEADS)

    cols = [split_cols(h @ w_in, C_SIZES) for h in (h_ctx, h_lat)]
    q = tuple(to_heads(cl[0], HGRN_HEADS) for cl in cols)
    v = tuple(to_heads(cl[3], HGRN_HEADS) for cl in cols)
    acc = [0.0, 0.0]
    for d in range(2):
        fg = [forget(cl[1 + d]) for cl in cols]
        o = directional_chunked(q, (fg[0][1], fg[1][1]), v, (fg[0][0], fg[1][0]), n_ctx, d == 1)
        acc = [acc[j] + o[j] for j in range(2)]
    y = [from_heads(head_rmsnorm(o)).astype(dt) * jax.nn.silu(cl[4]) for cl, o in zip(cols, acc)]
    out_ctx = y[0] @ w_out
    out_lat = grid_transpose(y[1] @ w_out, GRID_W, rows)
    return out_ctx, out_lat

def swiglu(t, w_gate, w_up, w_down):
    return (jax.nn.silu(t @ w_gate) * (t @ w_up)) @ w_down

def moe_ffn(h, router, bias, w_gate, w_up, w_down, ws_gate, ws_up, ws_down):
    n_tok = h.shape[0]
    affinity = jax.nn.sigmoid(jnp.dot(h.astype(jnp.float32), router.astype(jnp.float32)))
    biased = affinity + bias.astype(jnp.float32)
    per_group = N_EXPERTS // N_GROUPS
    group_score = lax.top_k(biased.reshape(n_tok, N_GROUPS, per_group), 2)[0].sum(-1)
    _, top_groups = lax.top_k(group_score, TOPK_GROUPS)
    group_keep = jax.nn.one_hot(top_groups, N_GROUPS).sum(1) > 0
    expert_keep = jnp.repeat(group_keep, per_group, axis=1)
    _, top_e = lax.top_k(jnp.where(expert_keep, biased, -jnp.inf), TOP_K)
    gate = jnp.take_along_axis(affinity, top_e, axis=1)
    gate = ROUTED_SCALE * gate / jnp.sum(gate, axis=-1, keepdims=True)
    n_rows = n_tok * TOP_K
    n_blocks = -(-n_rows // MOE_BLOCK) + N_EXPERTS
    flat_e = top_e.reshape(-1)
    order = jnp.argsort(flat_e)
    sorted_e = flat_e[order]
    counts = jnp.bincount(flat_e, length=N_EXPERTS)
    padded = (counts + MOE_BLOCK - 1) // MOE_BLOCK * MOE_BLOCK
    ends = jnp.cumsum(padded)
    dest = (ends - padded)[sorted_e] + jnp.arange(n_rows) - (jnp.cumsum(counts) - counts)[sorted_e]
    row_tok = jnp.zeros((n_blocks * MOE_BLOCK,), jnp.int32).at[dest].set((order // TOP_K).astype(jnp.int32))
    row_w = jnp.zeros((n_blocks * MOE_BLOCK,), h.dtype).at[dest].set(gate.reshape(-1)[order].astype(h.dtype))
    block_e = jnp.minimum(jnp.searchsorted(ends, jnp.arange(n_blocks) * MOE_BLOCK, side='right'), N_EXPERTS - 1)

    def block_step(acc, blk):
        tok, wt, e = blk
        y = swiglu(h[tok], w_gate[e], w_up[e], w_down[e])
        return acc.at[tok].add(y * wt[:, None]), None

    shared = swiglu(h, ws_gate, ws_up, ws_down)
    out, _ = lax.scan(block_step, shared, (row_tok.reshape(n_blocks, MOE_BLOCK), row_w.reshape(n_blocks, MOE_BLOCK), block_e))
    return out

def setup_inputs(seed: int = 0) -> dict:
    key = jax.random.key(seed)
    keys = iter(jax.random.split(key, 40))

    def nrm(shape, scale):
        return scale * jax.random.normal(next(keys), shape, jnp.float32)

    ab_cols = sum(AB_SIZES)
    c_cols = sum(C_SIZES)
    a_pow = jax.random.uniform(next(keys), (N_EVEN, 2, LRU_WIDTH), jnp.float32, 0.9, 0.999)
    a_base = a_pow ** (1.0 / LRU_C)
    lru_lambda = jnp.log(a_base) - jnp.log1p(-a_base)
    return {
        'x': nrm((BATCH, SEQ, D_MODEL), 1.0),
        'c': nrm((BATCH, D_MODEL), 1.0),
        'ctx': nrm((BATCH, CTX_LEN, D_MODEL), 1.0),
        'c_ctx': nrm((D_MODEL,), 1.0),
        'mod_w': nrm((DEPTH, D_MODEL, N_MOD * D_MODEL), 0.5 * D_MODEL ** -0.5),
        'mod_b': nrm((DEPTH, N_MOD * D_MODEL), 0.02),
        'pre_gain': 1.0 + nrm((DEPTH, 2, D_MODEL), 0.1),
        'post_gain': 1.0 + nrm((DEPTH, 2, D_MODEL), 0.1),
        'ab_w_in': nrm((N_EVEN, D_MODEL, ab_cols), D_MODEL ** -0.5),
        'ab_conv_w': nrm((N_EVEN, CONV_W, LRU_WIDTH), CONV_W ** -0.5),
        'ab_conv_b': nrm((N_EVEN, LRU_WIDTH), 0.02),
        'ab_lru_wa': nrm((N_EVEN, 2, LRU_HEADS, LRU_HEAD_DIM, LRU_HEAD_DIM), LRU_HEAD_DIM ** -0.5),
        'ab_lru_ba': nrm((N_EVEN, 2, LRU_WIDTH), 0.02),
        'ab_lru_wi': nrm((N_EVEN, 2, LRU_HEADS, LRU_HEAD_DIM, LRU_HEAD_DIM), LRU_HEAD_DIM ** -0.5),
        'ab_lru_bi': nrm((N_EVEN, 2, LRU_WIDTH), 0.02),
        'ab_lru_lambda': lru_lambda,
        'ab_gla_wa2': nrm((N_EVEN, 2, GLA_RANK, GLA_DK), GLA_RANK ** -0.5),
        'ab_gla_ba': nrm((N_EVEN, 2, GLA_DK), 0.02),
        'ab_w_out': nrm((N_EVEN, LRU_WIDTH + GLA_DV, D_MODEL), (LRU_WIDTH + GLA_DV) ** -0.5),
        'c_w_in': nrm((N_ODD, D_MODEL, c_cols), D_MODEL ** -0.5),
        'hgrn_lb_logits': nrm((DEPTH, HGRN_DIM), 0.5),
        'c_w_out': nrm((N_ODD, HGRN_DIM, D_MODEL), HGRN_DIM ** -0.5),
        'moe_router': nrm((DEPTH, D_MODEL, N_EXPERTS), D_MODEL ** -0.5),
        'moe_bias': nrm((DEPTH, N_EXPERTS), 0.01),
        'moe_w_gate': nrm((DEPTH, N_EXPERTS, D_MODEL, EXPERT_FF), D_MODEL ** -0.5),
        'moe_w_up': nrm((DEPTH, N_EXPERTS, D_MODEL, EXPERT_FF), D_MODEL ** -0.5),
        'moe_w_down': nrm((DEPTH, N_EXPERTS, EXPERT_FF, D_MODEL), EXPERT_FF ** -0.5),
        'moe_ws_gate': nrm((DEPTH, D_MODEL, SHARED_FF), D_MODEL ** -0.5),
        'moe_ws_up': nrm((DEPTH, D_MODEL, SHARED_FF), D_MODEL ** -0.5),
        'moe_ws_down': nrm((DEPTH, SHARED_FF, D_MODEL), SHARED_FF ** -0.5),
    }

def reference(x, c, ctx, c_ctx, mod_w, mod_b, pre_gain, post_gain,
              ab_w_in, ab_conv_w, ab_conv_b, ab_lru_wa, ab_lru_ba, ab_lru_wi, ab_lru_bi, ab_lru_lambda,
              ab_gla_wa2, ab_gla_ba, ab_w_out, c_w_in, hgrn_lb_logits, c_w_out,
              moe_router, moe_bias, moe_w_gate, moe_w_up, moe_w_down, moe_ws_gate, moe_ws_up, moe_ws_down):
    silu_c = jax.nn.silu(c)
    silu_cc = jax.nn.silu(c_ctx)
    n_tok_ctx = ctx.shape[0] * ctx.shape[1]
    for layer in range(DEPTH):
        last = layer == DEPTH - 1
        p = layer // 2
        m_l = jnp.split((silu_c @ mod_w[layer] + mod_b[layer])[:, None, :], N_MOD, axis=-1)
        m_c = jnp.split(silu_cc @ mod_w[layer] + mod_b[layer], N_MOD, axis=-1)
        h_c = rmsnorm(ctx, pre_gain[layer, 0]) * (1.0 + m_c[1]) + m_c[0]
        h_l = rmsnorm(x, pre_gain[layer, 0]) * (1.0 + m_l[1]) + m_l[0]
        if layer % 2 == 0:
            o_c, o_l = mixer_ab(h_c, h_l, ab_w_in[p], ab_conv_w[p], ab_conv_b[p], ab_lru_wa[p], ab_lru_ba[p],
                                ab_lru_wi[p], ab_lru_bi[p], ab_lru_lambda[p], ab_gla_wa2[p], ab_gla_ba[p], ab_w_out[p])
        else:
            o_c, o_l = mixer_c(h_c, h_l, layer, c_w_in[p], hgrn_lb_logits, c_w_out[p])
        x = x + m_l[2] * rmsnorm(o_l, post_gain[layer, 0])
        moe_p = (moe_router[layer], moe_bias[layer], moe_w_gate[layer], moe_w_up[layer], moe_w_down[layer],
                 moe_ws_gate[layer], moe_ws_up[layer], moe_ws_down[layer])
        h_l = rmsnorm(x, pre_gain[layer, 1]) * (1.0 + m_l[4]) + m_l[3]
        if last:
            f_l = moe_ffn(h_l.reshape(-1, D_MODEL), *moe_p).reshape(x.shape)
        else:
            ctx = ctx + m_c[2] * rmsnorm(o_c, post_gain[layer, 0])
            h_c = rmsnorm(ctx, pre_gain[layer, 1]) * (1.0 + m_c[4]) + m_c[3]
            f = moe_ffn(jnp.concatenate([h_c.reshape(-1, D_MODEL), h_l.reshape(-1, D_MODEL)], axis=0), *moe_p)
            ctx = ctx + m_c[5] * rmsnorm(f[:n_tok_ctx].reshape(ctx.shape), post_gain[layer, 1])
            f_l = f[n_tok_ctx:].reshape(x.shape)
        x = x + m_l[5] * rmsnorm(f_l, post_gain[layer, 1])
    return x


_drawn_inputs = setup_inputs


def setup_inputs(seed=0):
    import zlib

    import numpy as np

    out = dict(_drawn_inputs(seed))
    spreads = {}
    factors = {'ab_lru_ba': 5.067, 'ab_lru_bi': 3.288, 'ab_gla_ba': 12.813}
    for name, (base, spread) in spreads.items():
        noise = np.random.default_rng([zlib.crc32(name.encode()), seed]).standard_normal(out[name].shape)
        drawn = base * np.exp(spread * noise) if base else spread * noise
        out[name] = jnp.asarray(drawn.astype(out[name].dtype))
    for name, factor in factors.items():
        out[name] = (out[name] * factor).astype(out[name].dtype)
    return out
```

```python
import concourse.bass as bass
from concourse import mybir
from contextlib import ExitStack

fp32 = mybir.dt.float32
i32 = mybir.dt.int32
u32 = mybir.dt.uint32
ALU = mybir.AluOpType
ACT = mybir.ActivationFunctionType
AX = mybir.AxisListType

P = 128
D = 1024
KD = D // P
CTX, LAT = 256, 512
T = CTX + LAT
TT = T // P
CT = CTX // P
EPS = 1e-6
GRID_W = 64
GRID_H = LAT // GRID_W
CHUNK = 64
NCH = T // CHUNK
CCH = CTX // CHUNK
E = 64
TOPK = 8
FF = 256
KF = FF // P
ROUTED_SCALE = 2.5
LRU_C = 8.0
GLA_TAU = 16.0
GLA_RANK = 16


class Link:

    def __init__(self, eng, sem):
        self.eng, self.sem, self.n, self.trip, self.per = eng, sem, 0, None, 0

    def value(self):
        return self.n if self.trip is None else self.trip * self.per + self.n

    def mark(self, ins):
        ins.then_inc(self.sem, 1)
        self.n += 1

    def wait(self):
        self.eng.wait_ge(self.sem, self.value())

    def __call__(self, ins):
        self.mark(ins)
        self.wait()

    def enter(self, trip, per):
        self.trip, self.per, self.before = trip, per, self.n

    def leave(self, trips):
        assert self.n - self.before == self.per, (self.n - self.before, self.per)
        self.n = self.before + trips * self.per
        self.trip = None


class Core:
    pass


def stage_constants(nc, g):
    with nc.Block() as block:
        made = g.sem("const_made")

        @block.gpsimd
        def _(pool):
            link = Link(pool, made)
            pool.sem_inc(g.settled, 4)
            link.mark(nc.gpsimd.memset(g.ones[:, :], 1.0))
            link.mark(nc.gpsimd.memset(g.eps[:, :], EPS))
            link.mark(nc.gpsimd.memset(g.ident[:, :], 0.0))
            link.mark(nc.gpsimd.memset(g.before[:, :], 0.0))
            link.mark(nc.gpsimd.iota(g.token_id[:, :], pattern=[[P, TT]], base=0, channel_multiplier=1))
            link(nc.gpsimd.memset(g.mask[:, :, :], 0.0))
            link.mark(nc.gpsimd.affine_select(out=g.ident[:, :], in_=g.ident[:, :], compare_op=ALU.not_equal,
                                              fill=1.0, base=0, pattern=[[-1, P]], channel_multiplier=1))
            link.mark(nc.gpsimd.affine_select(out=g.before[:, :], in_=g.before[:, :], compare_op=ALU.is_ge,
                                              fill=1.0, base=0, pattern=[[-1, P]], channel_multiplier=1))
            for h in range(2):
                rows = slice(h * CHUNK, (h + 1) * CHUNK)
                link.mark(nc.gpsimd.affine_select(out=g.mask[rows, 0, rows], in_=g.mask[rows, 0, rows],
                                                  compare_op=ALU.is_gt, fill=1.0, base=0, pattern=[[-1, CHUNK]],
                                                  channel_multiplier=1))
                link(nc.gpsimd.affine_select(out=g.mask[rows, 1, rows], in_=g.mask[rows, 1, rows],
                                             compare_op=ALU.is_gt, fill=1.0, base=0, pattern=[[1, CHUNK]],
                                             channel_multiplier=-1))


def stage_modulation(nc, g):
    NS = 6 * D // 512
    with ExitStack() as s:
        cc = g.sb(s, "cc", [16, P])
        cs = g.sb(s, "cs", [16, P])
        cT = g.sb(s, "cT", [P, 16])
        w = [g.sb(s, f"modw{i}", [P, KD, 512]) for i in range(2)]
        m = g.sb(s, "m", [2, 6, D])
        mb = g.sb(s, "mb", [2, 6, D])
        gain = g.sb(s, "gain", [2, 4, D])
        vec = g.sb(s, "vec", [2, 6, D])
        mf, mbf = (t[:, :, :].rearrange("s r d -> s (r d)") for t in (m, mb))
        c_loaded, silu_done, cT_ps, cT_done = g.sems("mod", "c_loaded silu_done cT_ps cT_done")
        w_loaded = g.sems("mod", "w_loaded0 w_loaded1")
        w_used = g.sems("mod", "w_used0 w_used1")
        evacuated = g.sems("mod", "evacuated0 evacuated1")
        bias_loaded, vec_ready, vec_stored, chain = g.sems("mod", "bias_loaded vec_ready vec_stored chain")

        block = s.enter_context(nc.Block())

        @block.sync
        def _(sp):
            sp.dma_start(cc[0:8, :], g.io["c"].rearrange("a (k p) -> (a k) p", p=P)).then_inc(c_loaded, 16)
            sp.dma_start(cc[8:16, :], g.io["c_ctx"].rearrange("(k p) -> k p", p=P)).then_inc(c_loaded, 16)
            for layer in range(2):
                wl = g.io["mod_w"][layer].rearrange("(k p) n -> p k n", p=P)
                if layer:
                    sp.wait_ge(vec_ready, layer)
                sp.dma_start(mb[:, :, :].rearrange("s r d -> s (r d)"),
                             g.io["mod_b"][layer].partition_broadcast(2)).then_inc(bias_loaded, 16)
                sp.dma_start(gain[:, 0:2, :].rearrange("s r d -> s (r d)"),
                             g.io["pre_gain"][layer].rearrange("r d -> (r d)").partition_broadcast(2)).then_inc(bias_loaded, 16)
                sp.dma_start(gain[:, 2:4, :].rearrange("s r d -> s (r d)"),
                             g.io["post_gain"][layer].rearrange("r d -> (r d)").partition_broadcast(2)).then_inc(bias_loaded, 16)
                for b in range(2):
                    if layer:
                        sp.wait_ge(w_used[b], layer * NS // 2)
                    sp.dma_start(w[b][:, :, :], wl[:, :, b * 512:(b + 1) * 512]).then_inc(w_loaded[b], 16)
                with sp.Fori(0, NS // 2 - 1) as i:
                    for b in range(2):
                        sp.wait_ge(w_used[b], i + (layer * NS // 2 + 1))
                        sp.dma_start(w[b][:, :, :], wl[:, :, bass.ds(i * 1024 + (1024 + b * 512), 512)]).then_inc(w_loaded[b], 16)
                if layer == 0:
                    sp.wait_ge(vec_ready, 1)
                    sp.dma_start(g.mod_vecs[0], vec[:, :, :]).then_inc(vec_stored, 16)
            sp.wait_ge(vec_ready, 2)
            sp.dma_start(g.mod_vecs[1], vec[:, :, :]).then_inc(vec_stored, 16)
            sp.wait_ge(vec_stored, 32)

        @block.scalar
        def _(act):
            act.wait_ge(c_loaded, 32)
            nc.scalar.activation(cs[:, :], cc[:, :], ACT.Silu).then_inc(silu_done, 1)

        @block.tensor
        def _(pe):
            pe.wait_ge(silu_done, 1)
            nc.tensor.transpose(g.ps[:, 2, 0:16], cs[:, :], g.ident[0:16, 0:16]).then_inc(cT_ps, 1)
            pe.wait_ge(cT_done, 1)
            for layer in range(2):
                with pe.Fori(0, NS // 2) as i:
                    for b in range(2):
                        pe.wait_ge(evacuated[b], i + (layer * NS // 2 + 1))
                        pe.wait_ge(w_loaded[b], i * 16 + (layer * NS // 2 + 1) * 16)
                        for k in range(KD):
                            last = nc.tensor.matmul(g.ps[0:2, b, :], cT[:, k:k + 9:8], w[b][:, k, :],
                                                    start=(k == 0), stop=(k == KD - 1))
                        last.then_inc(w_used[b], 1)

        @block.vector
        def _(dve):
            link = Link(dve, chain)
            for b in range(2):
                dve.sem_inc(evacuated[b], 1)
            dve.wait_ge(cT_ps, 1)
            nc.vector.tensor_copy(cT[:, :], g.ps[:, 2, 0:16]).then_inc(cT_done, 1)
            for layer in range(2):
                dve.wait_ge(bias_loaded, 48 * (layer + 1))
                with dve.Fori(0, NS // 2) as i:
                    for b in range(2):
                        at = bass.ds(i * 1024 + b * 512, 512)
                        dve.wait_ge(w_used[b], i + (layer * NS // 2 + 1))
                        nc.vector.tensor_tensor(mf[:, at], g.ps[0:2, b, :], mbf[:, at], ALU.add).then_inc(evacuated[b], 1)
                for b in range(2):
                    dve.wait_ge(evacuated[b], (layer + 1) * NS // 2 + 1)
                if layer:
                    dve.wait_ge(vec_stored, 16)
                nc.vector.scalar_tensor_tensor(vec[:, 0, :], m[:, 1, :], 1.0, gain[:, 0, :], ALU.add, ALU.mult)
                nc.vector.tensor_copy(vec[:, 1, :], m[:, 0, :])
                nc.vector.tensor_tensor(vec[:, 2, :], m[:, 2, :], gain[:, 2, :], ALU.mult)
                nc.vector.scalar_tensor_tensor(vec[:, 3, :], m[:, 4, :], 1.0, gain[:, 1, :], ALU.add, ALU.mult)
                nc.vector.tensor_copy(vec[:, 4, :], m[:, 3, :])
                nc.vector.tensor_tensor(vec[:, 5, :], m[:, 5, :], gain[:, 3, :], ALU.mult).then_inc(vec_ready, 1)


def load_vectors(nc, g, sp, layer, row, dst, loaded, streams=(0, 1)):
    for st in streams:
        sp.dma_start(dst[:, st, :], g.mod_vecs[layer, st, row].partition_broadcast(P)).then_inc(loaded, 16)


def tile_rows(ap, t):
    return ap[t * P:(t + 1) * P, :]


def stage_norm(nc, g, name, layer, sub, X, hT, load_x=None, store_rows=False, lat_only=False, column_major=False):
    tiles = list(range(CT if lat_only else 0, TT))
    N = len(tiles)
    streams = (0,) if lat_only else (0, 1)
    with ExitStack() as s:
        A = g.sb(s, "A", [P, 2, D])
        B = g.sb(s, "B", [P, 2, D])
        H = g.sb(s, "H", [P, 2, D])
        sq = g.sb(s, "sq", [P, D])
        st = g.sb(s, "st", [P, 4, 8])
        x_loaded, vec_loaded, squared, var_ready, root_ready, rstd_ready = g.sems(
            name, "x_loaded vec_loaded squared var_ready root_ready rstd_ready")
        h_ready, transposed, copied, chain, achain = g.sems(name, "h_ready transposed copied chain achain")
        stored = g.sems(name, "stored0 stored1")
        block = s.enter_context(nc.Block())

        @block.sync
        def _(sp):
            if load_x:
                for t in tiles:
                    sp.dma_start(X[:, t, :], load_x(t)).then_inc(x_loaded, 16)
            load_vectors(nc, g, sp, layer, 3 * sub, A, vec_loaded, streams)
            load_vectors(nc, g, sp, layer, 3 * sub + 1, B, vec_loaded, streams)
            if store_rows:
                for n, t in enumerate(tiles):
                    sp.wait_ge(h_ready, n + 1)
                    sp.dma_start(tile_rows(g.h_rows, t), H[:, n % 2, :]).then_inc(stored[n % 2], 16)
                for b in range(2):
                    sp.wait_ge(stored[b], 16 * (N // 2))

        @block.scalar
        def _(act):
            link = Link(act, achain)
            for n, t in enumerate(tiles):
                if load_x:
                    act.wait_ge(x_loaded, 16 * N if n == 0 else 16 * N)
                link(nc.scalar.activation(sq[:, :], X[:, t, :], ACT.Square, accum_out=st[:, 0, t:t + 1]))
            act.sem_inc(squared, 1)
            act.wait_ge(var_ready, 1)
            nc.scalar.activation(st[:, 2, 0:TT], st[:, 1, 0:TT], ACT.Sqrt).then_inc(root_ready, 1)
            for n, t in enumerate(tiles):
                act.wait_ge(transposed, n + 1)
                src = g.ps[:, 2 * (n % 2):2 * (n % 2) + 2, :].rearrange("p a (k q) -> p (a k) q", q=P)
                if column_major and t >= CT:
                    r0 = (t - CT) * (P // GRID_W)
                    lat = hT[:, :, CTX:T].rearrange("p k (w r) -> p k r w", r=GRID_H)
                    for r in range(P // GRID_W):
                        last = nc.scalar.activation(lat[:, :, r0 + r, :], src[:, :, r * GRID_W:(r + 1) * GRID_W], ACT.Copy)
                else:
                    last = nc.scalar.activation(hT[:, :, t * P:(t + 1) * P], src, ACT.Copy)
                last.then_inc(copied, 1)

        @block.vector
        def _(dve):
            link = Link(dve, chain)
            if lat_only:
                link(nc.vector.memset(st[:, 0, 0:CT], 1.0))
            dve.wait_ge(squared, 1)
            nc.vector.tensor_scalar(st[:, 1, 0:TT], st[:, 0, 0:TT], 1.0 / D, EPS, ALU.mult, ALU.add).then_inc(var_ready, 1)
            dve.wait_ge(root_ready, 1)
            link(nc.vector.reciprocal(st[:, 3, 0:TT], st[:, 2, 0:TT]))
            dve.wait_ge(vec_loaded, 32 * len(streams))
            for n, t in enumerate(tiles):
                k = 1 if t < CT else 0
                if n >= 2:
                    dve.wait_ge(transposed, n - 1)
                    if store_rows:
                        dve.wait_ge(stored[n % 2], 16 * (n // 2))
                link(nc.vector.scalar_tensor_tensor(H[:, n % 2, :], X[:, t, :], st[:, 3, t:t + 1], A[:, k, :], ALU.mult, ALU.mult))
                nc.vector.tensor_tensor(H[:, n % 2, :], H[:, n % 2, :], B[:, k, :], ALU.add).then_inc(h_ready, 1)

        @block.tensor
        def _(pe):
            for n, t in enumerate(tiles):
                pe.wait_ge(h_ready, n + 1)
                if n >= 2:
                    pe.wait_ge(copied, n - 1)
                for k in range(KD):
                    last = nc.tensor.transpose(g.ps[:, 2 * (n % 2) + k // 4, (k % 4) * P:(k % 4 + 1) * P],
                                               H[:, n % 2, k * P:(k + 1) * P], g.ident[:, :])
                last.then_inc(transposed, 1)


SEGS = ((0, CTX), (CTX, LAT))


def token_row(g, bank):
    return g.ps[:, bank:bank + 2, :].rearrange("p b c -> p (b c)")[:, 512 - CTX:512 + LAT]


def project(nc, out, lhsT, hT):
    for o, n in SEGS:
        for k in range(KD):
            last = nc.tensor.matmul(out[:, o:o + n], lhsT(k), hT[:, k, o:o + n], start=(k == 0), stop=(k == KD - 1))
    return last


AB_LRU_IN = D
AB_Q, AB_K, AB_V, AB_OG, AB_ALR = 2048, 2560, 3072, 4096, 5120


def stage_lru(nc, g, hT):
    io = g.io
    NP = 11
    LEFT, GAP = 2, 3
    XP = CTX + LAT + 2 * GAP
    XC = CTX + GAP + LAT
    with ExitStack() as s:
        wx = g.sb(s, "wx", [P, KD, P])
        wg = g.sb(s, "wg", [P, KD, P])
        w4 = g.sb(s, "w4", [P, 4, P])
        par = g.sb(s, "par", [P, P])
        table = g.sb(s, "table", [P, 13, 8])
        tmp = g.sb(s, "tmp", [P, 8, 16])
        cur = g.sb(s, "cur", [P, 13])
        xp = g.sb(s, "xp", [P, XP])
        xc = g.sb(s, "xc", [P, XC])
        gel = g.sb(s, "gel", [P, T])
        Rg = g.sb(s, "Rg", [P, 2, T])
        Ig = g.sb(s, "Ig", [P, 2, T])
        Ag = g.sb(s, "Ag", [P, 2, T])
        Th = g.sb(s, "Th", [P, 2, T])
        V = g.sb(s, "V", [P, 2, T])
        S2 = g.sb(s, "S2", [P, 2, T])
        ya = g.sb(s, "ya", [P, KD, T])
        par_loaded, par_ps, lam_ready, lam_exp, lam_w, lam_ln, chain, achain = g.sems(
            "lru", "par_loaded par_ps lam_ready lam_exp lam_w lam_ln chain achain")
        wx_loaded, wg_loaded, w4_loaded = g.sems("lru", "wx_loaded wg_loaded w4_loaded")
        x_ready, xp_ready, xc_ready, g_ready, gel_ready, ri_ready, ri_copied = g.sems(
            "lru", "x_ready xp_ready xc_ready g_ready gel_ready ri_ready ri_copied")
        decay_ready, v_ready, s_ready, y_ready, stored = g.sems("lru", "decay_ready v_ready s_ready y_ready stored")
        wx_d = io["ab_w_in"][0].rearrange("(k p) n -> p k n", p=P)
        zero = g.sb(s, "zero", [P, D])
        zero_made, zero_stored = g.sems("lru", "zero_made zero_stored")
        block = s.enter_context(nc.Block())

        @block.gpsimd
        def _(pool):
            sure, most, step = TT * TOPK, n_blocks(TT), 8
            nc.gpsimd.memset(zero[:, :], 0.0).then_inc(zero_made, 1)
            pool.wait_ge(zero_made, 1)
            for b in range(sure, most, step):
                pool.dma_start(g.y_rows[b * P:(b + step) * P, :].rearrange("(b p) d -> p b d", p=P),
                               zero[:, :].unsqueeze(1).broadcast_to([P, step, D])).then_inc(zero_stored, 16)
            pool.wait_ge(zero_stored, 16 * ((most - sure) // step))

        @block.sync
        def _(sp):
            rows = lambda ap: ap.rearrange("r (j p) -> (r j) p", p=P)
            for r, name in ((0, "ab_conv_w"), (5, "ab_lru_ba"), (7, "ab_lru_bi"), (9, "ab_lru_lambda")):
                src = rows(io[name][0])
                sp.dma_start(par[8 * r:8 * r + src.shape[0], :], src).then_inc(par_loaded, 16)
            sp.dma_start(par[32:40, :], rows(io["ab_conv_b"])).then_inc(par_loaded, 16)

            def load_x(col):
                sp.dma_start(wx[:, :, :], wx_d[:, :, col(AB_LRU_IN)]).then_inc(wx_loaded, 16)

            def load_g(col):
                sp.dma_start(wg[:, :, :], wx_d[:, :, col(0)]).then_inc(wg_loaded, 16)

            def load_4(head):
                for n, name in enumerate(("ab_lru_wa", "ab_lru_wi")):
                    sp.dma_start(w4[:, n:n + 3:2, :].rearrange("p d e -> p d e"),
                                 io[name][0][:, head, :, :].rearrange("d h p e -> p (d h) e")).then_inc(w4_loaded, 16)

            load_x(lambda o: slice(o, o + P))
            load_g(lambda o: slice(o, o + P))
            load_4(slice(0, 1))
            with sp.Fori(0, KD - 1) as i:
                sp.wait_ge(x_ready, i + 1)
                load_x(lambda o: bass.ds(i * P + (o + P), P))
                sp.wait_ge(g_ready, i + 1)
                load_g(lambda o: bass.ds(i * P + (o + P), P))
                sp.wait_ge(ri_ready, i * 2 + 2)
                load_4(bass.ds(i + 1, 1))
            sp.wait_ge(y_ready, KD + 1)
            sp.dma_start(g.ya_rows, ya[:, :, :]).then_inc(stored, 16)
            sp.wait_ge(stored, 16)

        @block.tensor
        def _(pe):
            pe.wait_ge(par_loaded, 80)
            nc.tensor.transpose(g.ps[:, 7, 0:8 * NP], par[0:8 * NP, :], g.ident[0:8 * NP, 0:8 * NP]).then_inc(par_ps, 1)
            with pe.Fori(0, KD) as i:
                pe.wait_ge(wx_loaded, i * 16 + 16)
                pe.wait_ge(xp_ready, i + 1)
                project(nc, token_row(g, 0), lambda k: wx[:, k, :], hT).then_inc(x_ready, 1)
                pe.wait_ge(wg_loaded, i * 16 + 16)
                pe.wait_ge(gel_ready, i + 1)
                project(nc, token_row(g, 2), lambda k: wg[:, k, :], hT).then_inc(g_ready, 1)
                pe.wait_ge(w4_loaded, i * 32 + 32)
                pe.wait_ge(xc_ready, i + 2)
                for d in range(2):
                    pe.wait_ge(ri_copied, i * 2 + (d + 1))
                    for n in range(2):
                        out = token_row(g, 4 + 2 * n)
                        nc.tensor.matmul(out[:, 0:CTX], w4[:, 2 * d + n, :], xc[:, 0:CTX], start=True, stop=True)
                        last = nc.tensor.matmul(out[:, CTX:T], w4[:, 2 * d + n, :], xc[:, CTX + GAP:XC], start=True, stop=True)
                    last.then_inc(ri_ready, 1)

        @block.scalar
        def _(act):
            link = Link(act, achain)
            act.wait_ge(lam_ready, 1)
            nc.scalar.activation(tmp[:, 1, :], tmp[:, 0, :], ACT.Exp, scale=-1.0).then_inc(lam_exp, 1)
            act.wait_ge(lam_w, 1)
            nc.scalar.activation(tmp[:, 3, :], tmp[:, 2, :], ACT.Ln).then_inc(lam_ln, 1)
            for credit in (xp_ready, gel_ready, ri_copied):
                act.sem_inc(credit, 1)
            with act.Fori(0, KD) as i:
                link.enter(i, 2)
                act.wait_ge(x_ready, i + 1)
                act.wait_ge(xc_ready, i + 1)
                src = token_row(g, 0)
                nc.scalar.activation(xp[:, LEFT:LEFT + CTX], src[:, 0:CTX], ACT.Copy)
                nc.scalar.activation(xp[:, LEFT + CTX + GAP:LEFT + CTX + GAP + LAT], src[:, CTX:T], ACT.Copy).then_inc(xp_ready, 1)
                act.wait_ge(g_ready, i + 1)
                act.wait_ge(y_ready, i + 1)
                nc.scalar.activation(gel[:, :], token_row(g, 2), ACT.Gelu_apprx_tanh).then_inc(gel_ready, 1)
                for d in range(2):
                    act.wait_ge(ri_ready, i * 2 + (d + 1))
                    link.mark(nc.scalar.activation(Rg[:, d, :], token_row(g, 4), ACT.Sigmoid, bias=cur[:, 5 + d:6 + d]))
                    nc.scalar.activation(Ig[:, d, :], token_row(g, 6), ACT.Sigmoid, bias=cur[:, 7 + d:8 + d]).then_inc(ri_copied, 1)
                link.wait()
                for d in range(2):
                    nc.scalar.activation(Th[:, d, :], Rg[:, d, :], ACT.Tanh, scale=cur[:, 11 + d:12 + d])
                    nc.scalar.activation(Ag[:, d, :], Rg[:, d, :], ACT.Exp, scale=cur[:, 9 + d:10 + d]).then_inc(decay_ready, 1)
                for d in range(2):
                    act.wait_ge(v_ready, i * 2 + (d + 1))
                    nc.scalar.activation(S2[:, d, :], V[:, d, :], ACT.Sqrt).then_inc(s_ready, 1)
                link.leave(KD)

        @block.vector
        def _(dve):
            link = Link(dve, chain)
            dve.wait_ge(par_ps, 1)
            link.mark(nc.vector.memset(xp[:, :], 0.0))
            tf = table[:, :, :].rearrange("p r j -> p (r j)")
            link(nc.vector.tensor_copy(tf[:, 0:88], g.ps[:, 7, 0:88]))
            lam = tf[:, 72:88]
            nc.vector.scalar_tensor_tensor(tmp[:, 0, :], lam, -1.0, lam, ALU.mult, ALU.max).then_inc(lam_ready, 1)
            dve.wait_ge(lam_exp, 1)
            nc.vector.tensor_scalar(tmp[:, 2, :], tmp[:, 1, :], 1.0, None, ALU.add).then_inc(lam_w, 1)
            dve.wait_ge(lam_w, 1)
            link.mark(nc.vector.tensor_scalar(tmp[:, 4, :], tmp[:, 2, :], 1.0, None, ALU.is_equal))
            link(nc.vector.tensor_scalar(tmp[:, 5, :], tmp[:, 2, :], -1.0, None, ALU.add))
            link(nc.vector.tensor_tensor(tmp[:, 5, :], tmp[:, 5, :], tmp[:, 4, :], ALU.add))
            link(nc.vector.reciprocal(tmp[:, 6, :], tmp[:, 5, :]))
            dve.wait_ge(lam_ln, 1)
            link(nc.vector.tensor_tensor(tmp[:, 6, :], tmp[:, 6, :], tmp[:, 3, :], ALU.mult))
            link(nc.vector.tensor_tensor(tmp[:, 6, :], tmp[:, 6, :], tmp[:, 4, :], ALU.add))
            link(nc.vector.tensor_tensor(tmp[:, 6, :], tmp[:, 6, :], tmp[:, 1, :], ALU.mult))
            link(nc.vector.tensor_scalar(tmp[:, 7, :], lam, -1.0, 0.0, ALU.mult, ALU.max))
            link(nc.vector.tensor_tensor(tmp[:, 7, :], tmp[:, 7, :], tmp[:, 6, :], ALU.add))
            link.mark(nc.vector.tensor_scalar(tf[:, 72:88], tmp[:, 7, :], -LRU_C, None, ALU.mult))
            link(nc.vector.tensor_scalar(tf[:, 88:104], tmp[:, 7, :], LRU_C, None, ALU.mult))
            for credit in (xc_ready, y_ready):
                dve.sem_inc(credit, 1)
            with dve.Fori(0, KD) as i:
                link.enter(i, 14)
                dve.wait_ge(xp_ready, i + 2)
                g.hold(dve)
                link(nc.vector.tensor_copy(cur[:, :], table[:, :, bass.ds(i, 1)].rearrange("p r j -> p (r j)")))
                link(nc.vector.tensor_scalar(xc[:, :], xp[:, 0:XC], cur[:, 0:1], cur[:, 4:5], ALU.mult, ALU.add))
                for j in (1, 2):
                    link(nc.vector.scalar_tensor_tensor(xc[:, :], xp[:, j:j + XC], cur[:, j:j + 1], xc[:, :], ALU.mult, ALU.add))
                nc.vector.scalar_tensor_tensor(xc[:, :], xp[:, 3:3 + XC], cur[:, 3:4], xc[:, :], ALU.mult, ALU.add).then_inc(xc_ready, 1)
                dve.wait_ge(xc_ready, i + 2)
                for d in range(2):
                    dve.wait_ge(decay_ready, i * 2 + (d + 1))
                    link(nc.vector.tensor_tensor(V[:, d, :], Ag[:, d, :], Ag[:, d, :], ALU.mult))
                    nc.vector.scalar_tensor_tensor(V[:, d, :], V[:, d, :], 1.0, Th[:, d, :], ALU.add, ALU.mult).then_inc(v_ready, 1)
                    nc.vector.tensor_tensor(Ig[:, d, 0:CTX], Ig[:, d, 0:CTX], xc[:, 0:CTX], ALU.mult)
                    link.mark(nc.vector.tensor_tensor(Ig[:, d, CTX:T], Ig[:, d, CTX:T], xc[:, CTX + GAP:XC], ALU.mult))
                for d in range(2):
                    dve.wait_ge(s_ready, i * 2 + (d + 1))
                    if d == 0:
                        link.wait()
                    link(nc.vector.tensor_tensor(Ig[:, d, :], Ig[:, d, :], S2[:, d, :], ALU.mult))
                    if d == 0:
                        link(nc.vector.tensor_tensor_scan(V[:, 0, :], Ag[:, 0, :], Ig[:, 0, :], 0.0, ALU.mult, ALU.add))
                    else:
                        link(nc.vector.tensor_tensor_scan(V[:, 1, 0:CTX][:, ::-1], Ag[:, 1, 0:CTX][:, ::-1],
                                                          Ig[:, 1, 0:CTX][:, ::-1], 0.0, ALU.mult, ALU.add))
                        link(nc.vector.tensor_tensor_scan(V[:, 1, CTX:T][:, ::-1], Ag[:, 1, CTX:T][:, ::-1],
                                                          Ig[:, 1, CTX:T][:, ::-1], V[:, 1, 0:1], ALU.mult, ALU.add))
                link(nc.vector.tensor_tensor(V[:, 0, :], V[:, 0, :], V[:, 1, :], ALU.add))
                nc.vector.tensor_tensor(ya[:, bass.ds(i, 1), :].rearrange("p a t -> p (a t)"), V[:, 0, :], gel[:, :],
                                        ALU.mult).then_inc(y_ready, 1)
                link.leave(KD)


def scan_chunks(d):
    if d == 0:
        return list(range(NCH))
    return list(range(CCH - 1, -1, -1)) + list(range(NCH - 1, CCH - 1, -1))


def stage_attention(nc, g, name, hT, gla):
    io = g.io
    heads, NV = (4, 2) if gla else (8, 1)
    DV = NV * P
    first_tile = 0 if gla else CT
    gate_scale = 1.0 / GLA_TAU if gla else 1.0
    w_in = io["ab_w_in" if gla else "c_w_in"][0].rearrange("(k p) n -> p k n", p=P)
    if gla:
        parts = [("v", AB_V, DV), ("k", AB_K, P), ("q", AB_Q, P), ("o", AB_OG, DV)]
        n_dma, n_par = 6, 8
    else:
        parts = [("v", 3 * D, DV), ("f0", D, P), ("f1", 2 * D, P), ("q", 0, P), ("o", 4 * D, DV)]
        n_dma, n_par = 5, 16
    at, width = {}, 0
    for what, _, n in parts:
        at[what] = width
        width += n
    out_segs = SEGS if gla else SEGS[1:]
    out_at = first_tile * P
    with ExitStack() as s:
        W = g.sb(s, "W", [P, KD, width])
        par = g.sb(s, "par", [16, P])
        table = g.sb(s, "table", [P, 3, 8])
        cur = g.sb(s, "cur", [P, 4])
        q = g.sb(s, "q", [P, T])
        K = g.sb(s, "K", [P, 2, T])
        vt = g.sb(s, "vt", [P, TT, DV])
        OG = g.sb(s, "OG", [P, NV, T])
        Z = g.sb(s, "Z", [P, 2, T])
        B = g.sb(s, "B", [P, 2, T])
        D1 = g.sb(s, "D1", [P, 2, T])
        D2 = g.sb(s, "D2", [P, 2, T])
        Es = g.sb(s, "Es", [P, 2, 4, T])
        dec = g.sb(s, "dec", [P, 2, NCH])
        kdT = g.sb(s, "kdT", [P, 2, TT, P])
        sc = g.sb(s, "sc", [P, 2, TT, P])
        ST = g.sb(s, "ST", [P, 2, NCH, DV])
        start = g.sb(s, "start", [P, 2, T])
        if gla:
            walr = g.sb(s, "walr", [P, KD, 2 * GLA_RANK])
            wa2 = g.sb(s, "wa2", [GLA_RANK, 2, P])
            alr = g.sb(s, "alr", [GLA_RANK, 2, T])
            Y = g.sb(s, "Y", [P, KD, T])
        else:
            Y = g.sb(s, "Y", [P, KD, LAT])
        names = ("par_loaded par_ps par_ready par_act w_loaded alr_loaded alr_ps alr_copied proj_ready proj_copied "
                 "abs_ready soft_ready d_ready e_ready qk_ready kd_ready kdT_ps kdT_copied s_ps sc_ready kv_ps "
                 "kv_used o_ready sq_ready n_ready root_ready silu_ready head_done stored chain achain masks")
        S = dict(zip(names.split(), g.sems(name, names)))
        block = s.enter_context(nc.Block())
        items = (["z0", "z1", "v", "k", "q", "o0", "o1"] if gla else ["v", "f0", "f1", "q", "o0"])
        bank_of = (dict(z0=4, z1=6, v=0, k=4, q=6, o0=0, o1=2) if gla else dict(v=0, f0=4, f1=6, q=2, o0=4))
        NI = len(items)
        freed_by = ({"k": "z0", "q": "z1", "o0": "v", "o1": "v"} if gla else {"o0": "f0"})
        rows = lambda ap: ap.rearrange("r (j p) -> (r j) p", p=P)

        @block.sync
        def _(sp):
            if gla:
                sp.dma_start(par[0:8, :], rows(io["ab_gla_ba"][0])).then_inc(S["par_loaded"], 16)
                sp.dma_start(walr[:, :, :], w_in[:, :, AB_ALR:AB_ALR + 2 * GLA_RANK]).then_inc(S["alr_loaded"], 16)
            else:
                sp.dma_start(par[0:16, :], rows(io["hgrn_lb_logits"])).then_inc(S["par_loaded"], 16)

            def load(col):
                for what, first, n in parts:
                    sp.dma_start(W[:, :, at[what]:at[what] + n], w_in[:, :, col(first, n)]).then_inc(S["w_loaded"], 16)
                if gla:
                    for d in range(2):
                        sp.dma_start(wa2[:, d, :], io["ab_gla_wa2"][0, d][:, col(0, P)]).then_inc(S["w_loaded"], 16)

            load(lambda first, n: slice(first, first + n))
            with sp.Fori(0, heads - 1) as i:
                sp.wait_ge(S["proj_ready"], i * NI + NI)
                load(lambda first, n: bass.ds(i * n + (first + n), n))
            sp.wait_ge(S["head_done"], heads + 1)
            if gla:
                sp.dma_start(g.yb_rows, Y[:, :, :]).then_inc(S["stored"], 16)
            else:
                sp.dma_start(g.yb_rows[:, :, CTX:T], Y[:, :, :]).then_inc(S["stored"], 16)
            sp.wait_ge(S["stored"], 16)

        @block.tensor
        def _(pe):
            pe.wait_ge(S["par_loaded"], 16)
            nc.tensor.transpose(g.ps[:, 7, 0:n_par], par[0:n_par, :], g.ident[0:n_par, 0:n_par]).then_inc(S["par_ps"], 1)
            if gla:
                pe.wait_ge(S["alr_loaded"], 16)
                for d in range(2):
                    cols = slice(d * GLA_RANK, (d + 1) * GLA_RANK)
                    project(nc, token_row(g, 2 * d)[0:GLA_RANK], lambda k: walr[:, k, cols], hT).then_inc(S["alr_ps"], 1)
                pe.wait_ge(S["alr_copied"], 2)
            with pe.Fori(0, heads) as i:
                pe.wait_ge(S["head_done"], i + 1)
                pe.wait_ge(S["w_loaded"], i * (16 * n_dma) + 16 * n_dma)
                for m, item in enumerate(items):
                    if item in freed_by:
                        pe.wait_ge(S["proj_copied"], i * NI + items.index(freed_by[item]) + 1)
                    bank = bank_of[item]
                    if item in ("z0", "z1"):
                        for o, n in SEGS:
                            last = nc.tensor.matmul(token_row(g, bank)[:, o:o + n], wa2[:, int(item[1]), :],
                                                    alr[:, int(item[1]), o:o + n], start=True, stop=True)
                    elif item == "v":
                        flat = g.ps[:, bank:bank + 3, :].rearrange("p b c -> p (b c)")
                        for t in range(TT):
                            for k in range(KD):
                                last = nc.tensor.matmul(flat[:, t * DV:(t + 1) * DV], hT[:, k, t * P:(t + 1) * P],
                                                        W[:, k, at["v"]:at["v"] + DV],
                                                        start=(k == 0), stop=(k == KD - 1))
                    else:
                        c = at[item[0]] + P * int(item[1]) if item[0] == "o" else at[item]
                        last = project(nc, token_row(g, bank), lambda k: W[:, k, c:c + P], hT)
                    last.then_inc(S["proj_ready"], 1)
                pe.wait_ge(S["proj_copied"], i * NI + NI)
                for d in range(2):
                    pe.wait_ge(S["kd_ready"], i * 2 + (d + 1))
                    if d:
                        pe.wait_ge(S["kv_used"], i * (2 * NCH - 2) + (NCH - 1))
                    for t in range(TT):
                        last = nc.tensor.transpose(token_row(g, 0)[:, t * P:(t + 1) * P], Es[:, d, 3, t * P:(t + 1) * P], g.ident[:, :])
                    last.then_inc(S["kdT_ps"], 1)
                    pe.wait_ge(S["qk_ready"], i * 2 + (d + 1))
                    if d:
                        pe.wait_ge(S["sc_ready"], i * 2 + 1)
                    for t in range(first_tile, TT):
                        last = nc.tensor.matmul(token_row(g, 2)[:, t * P:(t + 1) * P], Es[:, d, 1, t * P:(t + 1) * P],
                                                Es[:, d, 0, t * P:(t + 1) * P], start=True, stop=True)
                    last.then_inc(S["s_ps"], 1)
                    pe.wait_ge(S["kdT_copied"], i * 2 + (d + 1))
                    for n, c in enumerate(scan_chunks(d)[:-1]):
                        if n >= 2:
                            pe.wait_ge(S["kv_used"], i * (2 * NCH - 2) + (d * (NCH - 1) + n - 1))
                        half = slice(CHUNK * (c % 2), CHUNK * (c % 2) + CHUNK)
                        nc.tensor.matmul(g.ps[:, n % 2, 0:DV], kdT[half, d, c // 2, :], vt[half, c // 2, :],
                                         start=True, stop=True).then_inc(S["kv_ps"], 1)
                    pe.wait_ge(S["sc_ready"], i * 2 + (d + 1))
                    pe.wait_ge(S["kv_used"], i * (2 * NCH - 2) + (d + 1) * (NCH - 1))
                    order = scan_chunks(d)
                    for v in range(NV):
                        out = token_row(g, 4 + 2 * v)
                        cols = slice(v * P, (v + 1) * P)
                        for t in range(first_tile, TT):
                            opens = d == 0 and t in (0, CT)
                            nc.tensor.matmul(out[:, t * P:(t + 1) * P], vt[:, t, cols], sc[:, d, t, :], start=opens,
                                             stop=False, skip_group_check=True)
                            for c in (2 * t, 2 * t + 1):
                                if order[0] == c:
                                    continue
                                closes = d == 1 and c in (2 * CT - 1, NCH - 1)
                                last = nc.tensor.matmul(out[:, c * CHUNK:(c + 1) * CHUNK], ST[:, d, order.index(c), cols],
                                                        Es[:, d, 2, c * CHUNK:(c + 1) * CHUNK], start=False,
                                                        stop=closes, skip_group_check=True)
                last.then_inc(S["o_ready"], 1)
                pe.wait_ge(S["sq_ready"], i + 1)
                for o, n in out_segs:
                    for v in range(NV):
                        last = nc.tensor.matmul(token_row(g, 2)[:, o:o + n], g.ones[:, :], D1[:, v, o:o + n],
                                                start=(v == 0), stop=(v == NV - 1))
                last.then_inc(S["n_ready"], 1)

        @block.scalar
        def _(act):
            link = Link(act, S["achain"])
            if gla:
                for d in range(2):
                    act.wait_ge(S["alr_ps"], d + 1)
                    nc.scalar.activation(alr[:, d, :], token_row(g, 2 * d)[0:GLA_RANK], ACT.Copy).then_inc(S["alr_copied"], 1)
            else:
                act.wait_ge(S["par_ready"], 1)
                nc.scalar.activation(table[:, 0, :], table[:, 2, :], ACT.Sigmoid)
                nc.scalar.activation(table[:, 1, :], table[:, 2, :], ACT.Sigmoid, scale=-1.0).then_inc(S["par_act"], 1)
            with act.Fori(0, heads) as i:
                link.enter(i, 1 if gla else 2)

                def copied(ins):
                    ins.then_inc(S["proj_copied"], 1)

                def await_item(item):
                    act.wait_ge(S["proj_ready"], i * NI + items.index(item) + 1)

                act.wait_ge(S["head_done"], i + 1)
                act.wait_ge(S["par_ready"], i + 2)
                if gla:
                    for d in range(2):
                        await_item(f"z{d}")
                        copied(nc.scalar.activation(Z[:, d, :], token_row(g, 4 + 2 * d), ACT.Identity, bias=cur[:, d:d + 1]))
                await_item("v")
                flat = g.ps[:, 0:3, :].rearrange("p b c -> p (b c)")
                copied(nc.scalar.activation(vt[:, :, :].rearrange("p t v -> p (t v)"), flat[:, 0:TT * DV], ACT.Copy))
                if gla:
                    act.wait_ge(S["abs_ready"], i + 1)
                    link(nc.scalar.activation(D1[:, :, :], D1[:, :, :], ACT.Exp, scale=-1.0))
                    nc.scalar.activation(D1[:, :, :], D1[:, :, :], ACT.Ln, bias=1.0).then_inc(S["soft_ready"], 1)
                    await_item("k")
                    copied(nc.scalar.activation(K[:, 0, :], token_row(g, 4), ACT.Copy))
                else:
                    for d in range(2):
                        await_item(f"f{d}")
                        link(nc.scalar.activation(D1[:, d, :], token_row(g, 4 + 2 * d), ACT.Sigmoid))
                        copied(nc.scalar.activation(K[:, d, :], token_row(g, 4 + 2 * d), ACT.Sigmoid, scale=-1.0))
                    for d in range(2):
                        nc.scalar.activation(Z[:, d, :], D1[:, d, :], ACT.Ln, scale=cur[:, 1:2],
                                             bias=cur[:, 0:1]).then_inc(S["soft_ready"], 1)
                await_item("q")
                copied(nc.scalar.activation(q[:, :], token_row(g, bank_of["q"]), ACT.Copy,
                                            scale=float(P) ** -0.5 if gla else 1.0))
                for d in range(2):
                    act.wait_ge(S["d_ready"], i * 2 + (d + 1))
                    nc.scalar.activation(Es[:, d, 0, :], D1[:, d, :], ACT.Exp, scale=gate_scale)
                    nc.scalar.activation(Es[:, d, 1, :], D1[:, d, :], ACT.Exp, scale=-gate_scale)
                    nc.scalar.activation(Es[:, d, 2, :], B[:, d, :], ACT.Exp, scale=gate_scale)
                    nc.scalar.activation(Es[:, d, 3, :], D2[:, d, :], ACT.Exp, scale=-gate_scale).then_inc(S["e_ready"], 1)
                for v in range(NV):
                    await_item(f"o{v}")
                    ins = nc.scalar.activation(OG[:, v, :], token_row(g, bank_of[f"o{v}"]), ACT.Silu)
                    copied(ins)
                for d in range(2):
                    act.wait_ge(S["kdT_ps"], i * 2 + (d + 1))
                    nc.scalar.activation(kdT[:, d, :, :].rearrange("p t k -> p (t k)"), token_row(g, 0), ACT.Copy)\
                        .then_inc(S["kdT_copied"], 1)
                act.wait_ge(S["o_ready"], i + 1)
                for v in range(NV):
                    last = nc.scalar.activation(D1[:, v, out_at:T], token_row(g, 4 + 2 * v)[:, out_at:T], ACT.Square)
                last.then_inc(S["sq_ready"], 1)
                act.wait_ge(S["n_ready"], i + 1)
                nc.scalar.activation(D2[:, 0, out_at:T], token_row(g, 2)[:, out_at:T], ACT.Sqrt, scale=1.0 / DV,
                                     bias=g.eps[:, 0:1]).then_inc(S["root_ready"], 1)
                link.leave(heads)

        @block.gpsimd
        def _(pool):
            nc.gpsimd.memset(start[:, :, :], 1.0).then_inc(S["masks"], 1)
            pool.wait_ge(S["masks"], 1)
            chunks = start[:, :, :].rearrange("p d (c s) -> p d c s", s=CHUNK)
            nc.gpsimd.memset(chunks[:, 0, :, 0:1], 0.0)
            nc.gpsimd.memset(chunks[:, 1, :, CHUNK - 1:CHUNK], 0.0)
            nc.gpsimd.memset(sc[:, :, :, :], 0.0).then_inc(S["masks"], 1)
            with pool.Fori(0, heads) as i:
                for d in range(2):
                    key = K[:, 0 if gla else d, :]
                    pool.wait_ge(S["e_ready"], i * 2 + (d + 1))
                    nc.gpsimd.tensor_tensor(Es[:, d, 3, :], Es[:, d, 3, :], key, ALU.mult).then_inc(S["kd_ready"], 1)

        @block.vector
        def _(dve):
            link = Link(dve, S["chain"])
            dve.wait_ge(S["par_ps"], 1)
            tf = table[:, :, :].rearrange("p r j -> p (r j)")
            if gla:
                link(nc.vector.memset(table[:, :, :], 0.0))
                nc.vector.tensor_copy(table[:, 0:2, 0:4], g.ps[:, 7, 0:8].rearrange("p (r j) -> p r j", r=2)).then_inc(S["par_ready"], 1)
                dve.wait_ge(S["par_ready"], 1)
            else:
                link(nc.vector.tensor_copy(tf[:, 0:16], g.ps[:, 7, 0:16]))
                nc.vector.tensor_tensor(table[:, 2, :], table[:, 1, :], table[:, 0, :], ALU.subtract).then_inc(S["par_ready"], 1)
                dve.wait_ge(S["par_act"], 1)
            dve.sem_inc(S["head_done"], 1)
            dve.wait_ge(S["masks"], 2)
            with dve.Fori(0, heads) as i:
                link.enter(i, PER_GLA if gla else PER_HGRN)
                dve.wait_ge(S["head_done"], i + 1)
                g.hold(dve)
                nc.vector.tensor_copy(cur[:, 0:3], table[:, :, bass.ds(i, 1)].rearrange("p r j -> p (r j)"))\
                    .then_inc(S["par_ready"], 1)
                if gla:
                    dve.wait_ge(S["proj_copied"], i * NI + 2)
                    nc.vector.scalar_tensor_tensor(D1[:, :, :], Z[:, :, :], -1.0, Z[:, :, :], ALU.mult, ALU.max)\
                        .then_inc(S["abs_ready"], 1)
                    dve.wait_ge(S["soft_ready"], i + 1)
                    link(nc.vector.scalar_tensor_tensor(Z[:, :, :], Z[:, :, :], 0.0, D1[:, :, :], ALU.min, ALU.subtract))
                else:
                    dve.wait_ge(S["proj_copied"], i * NI + 3)
                    dve.wait_ge(S["par_ready"], i + 2)
                    link(nc.vector.tensor_scalar(K[:, :, :], K[:, :, :], cur[:, 1:2], None, ALU.mult))
                    dve.wait_ge(S["soft_ready"], i * 2 + 2)
                for d in range(2):
                    turn = (lambda a: a) if d == 0 else (lambda a: a[:, ::-1])
                    ref, end = (CHUNK // 2 - 1, CHUNK - 1) if d == 0 else (CHUNK // 2, 0)
                    link(nc.vector.tensor_tensor_scan(turn(B[:, d, :]), turn(start[:, d, :]), turn(Z[:, d, :]), 0.0, ALU.mult, ALU.add))
                    b3 = B[:, d, :].rearrange("p (c s) -> p c s", s=CHUNK)
                    sub = lambda out, col: nc.vector.tensor_tensor(
                        out.rearrange("p (c s) -> p c s", s=CHUNK), b3,
                        b3[:, :, col:col + 1].broadcast_to([P, NCH, CHUNK]), ALU.subtract)
                    sub(D1[:, d, :], ref)
                    sub(D2[:, d, :], end).then_inc(S["d_ready"], 1)
                dve.wait_ge(S["proj_copied"], i * NI + (5 if gla else 4))
                for d in range(2):
                    key = K[:, 0 if gla else d, :]
                    end = CHUNK - 1 if d == 0 else 0
                    dve.wait_ge(S["e_ready"], i * 2 + (d + 1))
                    link(nc.vector.tensor_scalar(dec[:, d, :], Es[:, d, 2, :].rearrange("p (c s) -> p c s", s=CHUNK)[:, :, end],
                                                 1.0, None, ALU.mult))
                    nc.vector.tensor_tensor(Es[:, d, 0, :], Es[:, d, 0, :], q[:, :], ALU.mult)
                    nc.vector.tensor_tensor(Es[:, d, 2, :], Es[:, d, 2, :], q[:, :], ALU.mult)
                    nc.vector.tensor_tensor(Es[:, d, 1, :], Es[:, d, 1, :], key, ALU.mult).then_inc(S["qk_ready"], 1)
                for d in range(2):
                    dve.wait_ge(S["s_ps"], i * 2 + (d + 1))
                    nc.vector.memset(cur[:, 3:4], 0.0)
                    NS = TT - first_tile
                    nc.vector.copy_predicated(sc[:, d, first_tile:TT, :], g.mask[:, d:d + 1, :].broadcast_to([P, NS, P]),
                                              token_row(g, 2)[:, out_at:T].rearrange("p (t c) -> p t c", c=P))\
                        .then_inc(S["sc_ready"], 1)
                    for n, c in enumerate(scan_chunks(d)[:-1]):
                        dve.wait_ge(S["kv_ps"], i * (2 * NCH - 2) + (d * (NCH - 1) + n + 1))
                        if n == 0:
                            ins = nc.vector.tensor_scalar(ST[:, d, 1, :], g.ps[:, 0, 0:DV], 1.0, None, ALU.mult)
                        else:
                            ins = nc.vector.scalar_tensor_tensor(ST[:, d, n + 1, :], ST[:, d, n, :], dec[:, d, c:c + 1],
                                                                 g.ps[:, n % 2, 0:DV], ALU.mult, ALU.add)
                        ins.then_inc(S["kv_used"], 1)
                        dve.wait_ge(S["kv_used"], i * (2 * NCH - 2) + (d * (NCH - 1) + n + 1))
                dve.wait_ge(S["proj_copied"], i * NI + NI)
                dve.wait_ge(S["sq_ready"], i + 1)
                for v in range(NV):
                    link.mark(nc.vector.tensor_tensor(OG[:, v, out_at:T], token_row(g, 4 + 2 * v)[:, out_at:T], OG[:, v, out_at:T], ALU.mult))
                dve.wait_ge(S["root_ready"], i + 1)
                link(nc.vector.reciprocal(D2[:, 1, out_at:T], D2[:, 0, out_at:T]))
                for v in range(NV):
                    row = Y[:, bass.ds(i * NV + v, 1), :].rearrange("p a t -> p (a t)")
                    if gla:
                        last = nc.vector.tensor_tensor(row, OG[:, v, :], D2[:, 1, :], ALU.mult)
                    else:
                        back = lambda a: a.rearrange("p (w r) -> p w r", r=GRID_H)
                        last = nc.vector.tensor_tensor(row.rearrange("p (r w) -> p w r", w=GRID_W), back(OG[:, v, CTX:T]),
                                                       back(D2[:, 1, CTX:T]), ALU.mult)
                last.then_inc(S["head_done"], 1)
                link.leave(heads)


PER_GLA = 1 + 2 + 2 + 2 + 1
PER_HGRN = 1 + 2 + 2 + 1 + 1


def stage_mix_out(nc, g, name, w_out, sources, F, tiles):
    KY = sum(n for _, n in sources)
    NC, SL = 256, D // 256
    N = len(tiles)
    with ExitStack() as s:
        Y = g.sb(s, "Yin", [P, KY, T])
        W = [g.sb(s, f"Wout{b}", [P, KY, NC]) for b in range(2)]
        y_loaded, = g.sems(name, "y_loaded")
        w_loaded = g.sems(name, "w_loaded0 w_loaded1")
        o_ps = g.sems(name, "o_ps0 o_ps1")
        o_copied = g.sems(name, "o_copied0 o_copied1")
        first = tiles[0] * P
        wv = w_out.rearrange("(k p) n -> p k n", p=P)
        block = s.enter_context(nc.Block())

        @block.sync
        def _(sp):
            sp.dma_start(W[0][:, :, :], wv[:, :, 0:NC]).then_inc(w_loaded[0], 16)
            k = 0
            for rows, n in sources:
                sp.dma_start(Y[:, k:k + n, first:T], rows[:, :, first:T]).then_inc(y_loaded, 16)
                k += n
            sp.dma_start(W[1][:, :, :], wv[:, :, NC:2 * NC]).then_inc(w_loaded[1], 16)
            for b in range(2):
                sp.wait_ge(o_ps[b], 1)
                sp.dma_start(W[b][:, :, :], wv[:, :, (2 + b) * NC:(3 + b) * NC]).then_inc(w_loaded[b], 16)

        @block.tensor
        def _(pe):
            pe.wait_ge(y_loaded, 16 * len(sources))
            with pe.Fori(0, SL // 2) as i:
                for b in range(2):
                    pe.wait_ge(w_loaded[b], i * 16 + 16)
                    pe.wait_ge(o_copied[b], i + 1)
                    out = g.ps[:, 4 * b:4 * b + 4, :].rearrange("p b c -> p (b c)")
                    for n, t in enumerate(tiles):
                        for k in range(KY):
                            last = nc.tensor.matmul(out[:, n * NC:(n + 1) * NC], Y[:, k, t * P:(t + 1) * P], W[b][:, k, :],
                                                    start=(k == 0), stop=(k == KY - 1))
                    last.then_inc(o_ps[b], 1)

        @block.vector
        def _(dve):
            for b in range(2):
                dve.sem_inc(o_copied[b], 1)
            with dve.Fori(0, SL // 2) as i:
                for b in range(2):
                    dve.wait_ge(o_ps[b], i + 1)
                    src = g.ps[:, 4 * b:4 * b + 4, :].rearrange("p b c -> p (b c)")[:, 0:N * NC]
                    nc.vector.tensor_scalar(F[:, tiles[0]:TT, bass.ds(i * (2 * NC) + b * NC, NC)],
                                            src.rearrange("p (t c) -> p t c", c=NC), 1.0, None, ALU.mult)\
                        .then_inc(o_copied[b], 1)


def stage_residual(nc, g, name, layer, sub, F, X, tiles, load_x=None, store=None):
    lat_only = tiles[0] == CT
    streams = (0,) if lat_only else (0, 1)
    N = len(tiles)
    with ExitStack() as s:
        G = g.sb(s, "G", [P, 2, D])
        sq = g.sb(s, "sq", [P, D])
        st = g.sb(s, "st", [P, 4, 8])
        x_loaded, vec_loaded, squared, var_ready, root_ready, x_ready, stored, chain, achain = g.sems(
            name, "x_loaded vec_loaded squared var_ready root_ready x_ready stored chain achain")
        block = s.enter_context(nc.Block())

        @block.sync
        def _(sp):
            load_vectors(nc, g, sp, layer, 3 * sub + 2, G, vec_loaded, streams)
            if load_x:
                for t in tiles:
                    sp.dma_start(X[:, t, :], load_x(t)).then_inc(x_loaded, 16)
            if store:
                for n, t in enumerate(tiles):
                    sp.wait_ge(x_ready, n + 1)
                    sp.dma_start(store(t), X[:, t, :]).then_inc(stored, 16)
                sp.wait_ge(stored, 16 * N)

        @block.scalar
        def _(act):
            link = Link(act, achain)
            for t in tiles:
                link(nc.scalar.activation(sq[:, :], F[:, t, :], ACT.Square, accum_out=st[:, 0, t:t + 1]))
            act.sem_inc(squared, 1)
            act.wait_ge(var_ready, 1)
            nc.scalar.activation(st[:, 2, tiles[0]:TT], st[:, 1, tiles[0]:TT], ACT.Sqrt).then_inc(root_ready, 1)

        @block.vector
        def _(dve):
            link = Link(dve, chain)
            cols = slice(tiles[0], TT)
            dve.wait_ge(squared, 1)
            nc.vector.tensor_scalar(st[:, 1, cols], st[:, 0, cols], 1.0 / D, EPS, ALU.mult, ALU.add).then_inc(var_ready, 1)
            dve.wait_ge(root_ready, 1)
            link(nc.vector.reciprocal(st[:, 3, cols], st[:, 2, cols]))
            dve.wait_ge(vec_loaded, 16 * len(streams))
            if load_x:
                dve.wait_ge(x_loaded, 16 * N)
            for t in tiles:
                k = 1 if t < CT else 0
                link(nc.vector.scalar_tensor_tensor(F[:, t, :], F[:, t, :], st[:, 3, t:t + 1], G[:, k, :], ALU.mult, ALU.mult))
                nc.vector.tensor_tensor(X[:, t, :], X[:, t, :], F[:, t, :], ALU.add).then_inc(x_ready, 1)


def n_blocks(n_tiles):
    return n_tiles * TOPK + E


def stage_route(nc, g, name, layer, hT, tiles, R):
    t0, N = tiles[0], len(tiles)
    NB = n_blocks(N)
    BIG = 1e30
    with ExitStack() as s:
        wr = g.sb(s, "wr", [P, KD, E])
        bias = g.sb(s, "bias", [P, E])
        iota_i = g.sb(s, "iota_i", [P, P], i32)
        iota = g.sb(s, "iota", [P, P])
        tok = g.sb(s, "tok", [P, TT])
        aff = g.sb(s, "aff", [P, N, E])
        biased = g.sb(s, "biased", [P, N, E])
        m8 = g.sb(s, "m8", [P, N * 8, 8])
        gs = g.sb(s, "gs", [P, N, 8])
        g8 = g.sb(s, "g8", [P, N, 8])
        gi = g.sb(s, "gi", [P, N, 8], u32)
        gif = g.sb(s, "gif", [P, N, 8])
        eq = g.sb(s, "eq", [P, N, 8, 4])
        keep = g.sb(s, "keep", [P, N, 8])
        pen = g.sb(s, "pen", [P, N, 8])
        masked = g.sb(s, "masked", [P, N, E])
        e8 = g.sb(s, "e8", [P, N, 8])
        ei = g.sb(s, "ei", [P, N, 8], u32)
        eif = g.sb(s, "eif", [P, N, 8])
        OH = g.sb(s, "OH", [P, N * 8, E])
        OX = g.sb(s, "OX", [P, N * 8, E])
        Sel = g.sb(s, "Sel", [P, N, E])
        gk = g.sb(s, "gk", [P, N, 8])
        gsum = g.sb(s, "gsum", [P, N])
        cnt = g.sb(s, "cnt", [P, E])
        nb = g.sb(s, "nb", [P, E])
        ends = g.sb(s, "ends", [P, E])
        off = g.sb(s, "off", [P, E])
        cmp_ = g.sb(s, "cmp", [P, E])
        posm = g.sb(s, "posm", [P, N, E])
        posf = g.sb(s, "posf", [P, N * 8])
        posi = g.sb(s, "posi", [P, N * 8], i32)
        slot_i = g.sb(s, "slot_i", [P, N * 8], i32)
        blk_i = g.sb(s, "blk_i", [P, N * 8], i32)
        slot = g.sb(s, "slot", [P, N * 8])
        blk = g.sb(s, "blk", [P, N * 8])
        OS = g.sb(s, "OS", [P, 2, 8, P])
        OB = g.sb(s, "OB", [P, 2, 8, NB])
        eb = g.sb(s, "eb", [P, 1])
        npf = g.sb(s, "npf", [1, 1])
        w_loaded, logits_ps, aff_ready, sel_ready, rank_ps, eb_ready, eb_ps, oh_ready, rows_used, chain, iotas = g.sems(
            name, "w_loaded logits_ps aff_ready sel_ready rank_ps eb_ready eb_ps oh_ready rows_used chain iotas")
        block = s.enter_context(nc.Block())

        @block.sync
        def _(sp):
            sp.dma_start(wr[:, :, :], g.io["moe_router"][layer].rearrange("(k p) e -> p k e", p=P)).then_inc(w_loaded, 16)
            sp.dma_start(bias[:, :], g.io["moe_bias"][layer].partition_broadcast(P)).then_inc(w_loaded, 16)

        @block.gpsimd
        def _(pool):
            nc.gpsimd.iota(iota_i[:, :], pattern=[[1, P]], base=0, channel_multiplier=0).then_inc(iotas, 1)

        @block.tensor
        def _(pe):
            pe.wait_ge(w_loaded, 32)
            for n, t in enumerate(tiles):
                for k in range(KD):
                    last = nc.tensor.matmul(g.ps[:, 0, n * E:(n + 1) * E], hT[:, k, t * P:(t + 1) * P], wr[:, k, :],
                                            start=(k == 0), stop=(k == KD - 1))
            last.then_inc(logits_ps, 1)
            pe.wait_ge(sel_ready, 1)
            for n in range(N):
                for m in range(n + 1):
                    nc.tensor.matmul(g.ps[:, 1, n * E:(n + 1) * E], (g.before if m == n else g.ones)[:, :], Sel[:, m, :],
                                     start=(m == 0), stop=(m == n))
            for m in range(N):
                last = nc.tensor.matmul(g.ps[:, 2, 0:E], g.ones[:, :], Sel[:, m, :], start=(m == 0), stop=(m == N - 1))
            last.then_inc(rank_ps, 1)
            pe.wait_ge(eb_ready, 1)
            nc.tensor.matmul(g.ps[0:1, 3, 0:P], eb[:, :], g.ident[:, :], start=True, stop=True).then_inc(eb_ps, 1)
            for n in range(N):
                pe.wait_ge(oh_ready, n + 1)
                for k in range(TOPK):
                    last = nc.tensor.matmul(g.ps[:, 4, 0:NB], OS[:, n % 2, k, :], OB[:, n % 2, k, :],
                                            start=(n == 0 and k == 0), stop=(n == N - 1 and k == TOPK - 1))
                last.then_inc(rows_used, 1)

        @block.scalar
        def _(act):
            act.wait_ge(logits_ps, 1)
            nc.scalar.activation(aff[:, :, :].rearrange("p n e -> p (n e)"), g.ps[:, 0, 0:N * E], ACT.Sigmoid).then_inc(aff_ready, 1)

        @block.vector
        def _(dve):
            v = nc.vector
            link = Link(dve, chain)
            dve.wait_ge(iotas, 1)
            link.mark(v.tensor_copy(iota[:, :], iota_i[:, :]))
            link.mark(v.tensor_copy(tok[:, :], g.token_id[:, :]))
            dve.wait_ge(w_loaded, 32)
            dve.wait_ge(aff_ready, 1)
            link(v.tensor_tensor(biased[:, :, :], aff[:, :, :], bias[:, None, :].broadcast_to([P, N, E]), ALU.add))
            groups = biased[:, :, :].rearrange("p n (g e) -> p (n g) e", e=8)
            for j in range(N * 8):
                last = v.max(m8[:, j, :], groups[:, j, :])
            link(last)
            m8g = m8[:, :, :].rearrange("p (n g) e -> p n g e", g=8)
            link(v.tensor_tensor(gs[:, :, :], m8g[:, :, :, 0], m8g[:, :, :, 1], ALU.add))
            for n in range(N):
                last = v.max(g8[:, n, :], gs[:, n, :])
            link(last)
            for n in range(N):
                last = v.max_index(gi[:, n, :], g8[:, n, :], gs[:, n, :])
            link(last)
            link(v.tensor_copy(gif[:, :, :], gi[:, :, :]))
            for n in range(N):
                last = v.tensor_tensor(eq[:, n, :, :], iota[:, 0:8].unsqueeze(2).broadcast_to([P, 8, 4]),
                                       gif[:, n, 0:4].unsqueeze(1).broadcast_to([P, 8, 4]), ALU.is_equal)
            link(last)
            link(v.tensor_reduce(keep[:, :, :], eq[:, :, :, :], AX.X, ALU.add))
            link(v.tensor_scalar(pen[:, :, :], keep[:, :, :], -1.0, BIG, ALU.add, ALU.mult))
            over = lambda a: a[:, :, :].rearrange("p n g -> p (n g)").unsqueeze(2).broadcast_to([P, N * 8, 8])
            mg = masked[:, :, :].rearrange("p n (g e) -> p (n g) e", e=8)
            link(v.tensor_tensor(mg, groups, over(keep), ALU.mult))
            link(v.tensor_tensor(mg, mg, over(pen), ALU.add))
            for n in range(N):
                last = v.max(e8[:, n, :], masked[:, n, :])
            link(last)
            for n in range(N):
                last = v.max_index(ei[:, n, :], e8[:, n, :], masked[:, n, :])
            link(last)
            link(v.tensor_copy(eif[:, :, :], ei[:, :, :]))
            link(v.tensor_tensor(OH[:, :, :], iota[:, 0:E].unsqueeze(1).broadcast_to([P, N * 8, E]),
                                 eif[:, :, :].rearrange("p n k -> p (n k)").unsqueeze(2).broadcast_to([P, N * 8, E]), ALU.is_equal))
            v.tensor_reduce(Sel[:, :, :], OH[:, :, :].rearrange("p (n k) e -> p n e k", k=8), AX.X, ALU.add).then_inc(sel_ready, 1)
            for n in range(N):
                last = v.tensor_tensor(OX[:, n * 8:(n + 1) * 8, :], OH[:, n * 8:(n + 1) * 8, :],
                                       aff[:, n, :].unsqueeze(1).broadcast_to([P, 8, E]), ALU.mult)
            link(last)
            link(v.tensor_reduce(gk[:, :, :].rearrange("p n k -> p (n k)"), OX[:, :, :], AX.X, ALU.add))
            link(v.tensor_reduce(gsum[:, :], gk[:, :, :], AX.X, ALU.add))
            link(v.reciprocal(gsum[:, :], gsum[:, :]))
            for n in range(N):
                last = v.tensor_scalar(R.gates[:, n, :], gk[:, n, :], gsum[:, n:n + 1], ROUTED_SCALE, ALU.mult, ALU.mult)
            link(last)
            dve.wait_ge(rank_ps, 1)
            link.mark(v.memset(nb[:, :], 0.0))
            link.mark(v.memset(OS[:, 0, 0, 0:E], 1.0))
            link(v.tensor_copy(cnt[:, :], g.ps[:, 2, 0:E]))
            for j in range(TT):
                link(v.scalar_tensor_tensor(nb[:, :], cnt[:, :], float(P * j), nb[:, :], ALU.is_gt, ALU.add))
            link(v.tensor_tensor_scan(ends[:, :], OS[:, 0, 0, 0:E], nb[:, :], 0.0, ALU.mult, ALU.add))
            link(v.tensor_tensor(off[:, :], ends[:, :], nb[:, :], ALU.subtract))
            link(v.tensor_scalar(cmp_[:, :], ends[:, :], tok[:, 0:1], None, ALU.is_le))
            link(v.tensor_reduce(eb[:, :], cmp_[:, :], AX.X, ALU.add))
            v.tensor_scalar(eb[:, :], eb[:, :], float(E - 1), None, ALU.min).then_inc(eb_ready, 1)
            link(v.tensor_scalar(npf[:, :], ends[0:1, E - 1:E], 0.5, 0.25, ALU.mult, ALU.add))
            link(v.tensor_copy(R.pairs[:, :], npf[:, :]))
            for n in range(N):
                last = v.scalar_tensor_tensor(posm[:, n, :], off[:, :], float(P), g.ps[:, 1, n * E:(n + 1) * E], ALU.mult, ALU.add)
            link(last)
            for n in range(N):
                last = v.tensor_tensor(OX[:, n * 8:(n + 1) * 8, :], OH[:, n * 8:(n + 1) * 8, :],
                                       posm[:, n, :].unsqueeze(1).broadcast_to([P, 8, E]), ALU.mult)
            link(last)
            link(v.tensor_reduce(posf[:, :], OX[:, :, :], AX.X, ALU.add))
            link.mark(v.tensor_copy(posi[:, :], posf[:, :]))
            link(v.tensor_copy(R.pos[:, 0:N * 8], posf[:, :]))
            link.mark(v.tensor_scalar(slot_i[:, :], posi[:, :], P - 1, None, ALU.bitwise_and))
            link(v.tensor_scalar(blk_i[:, :], posi[:, :], 7, None, ALU.logical_shift_right))
            link.mark(v.tensor_copy(slot[:, :], slot_i[:, :]))
            link(v.tensor_copy(blk[:, :], blk_i[:, :]))
            for n, t in enumerate(tiles):
                if n >= 2:
                    dve.wait_ge(rows_used, n - 1)
                b = n % 2
                v.tensor_tensor(OS[:, b, :, :], iota[:, :].unsqueeze(1).broadcast_to([P, 8, P]),
                                slot[:, n * 8:(n + 1) * 8].unsqueeze(2).broadcast_to([P, 8, P]), ALU.is_equal)
                link(v.tensor_tensor(OB[:, b, :, :], iota[:, 0:NB].unsqueeze(1).broadcast_to([P, 8, NB]),
                                     blk[:, n * 8:(n + 1) * 8].unsqueeze(2).broadcast_to([P, 8, NB]), ALU.is_equal))
                v.tensor_scalar(OB[:, b, :, :], OB[:, b, :, :], tok[:, t:t + 1], None, ALU.mult).then_inc(oh_ready, 1)
            dve.wait_ge(eb_ps, 1)
            v.tensor_copy(R.block_expert[:, :], g.ps[0:1, 3, 0:P])
            dve.wait_ge(rows_used, N)
            link(v.memset(R.rows[:, :], 0))
            link(v.tensor_copy(R.rows[:, 0:NB], g.ps[:, 4, 0:NB]))


def stage_experts(nc, g, name, layer, hT, tiles, R, F):
    N = len(tiles)
    NB = n_blocks(N)
    io = g.io
    with ExitStack() as s:
        wgu = [g.sb(s, f"wgu{b}", [P, KD, 2 * FF]) for b in range(2)]
        wd = [g.sb(s, f"wd{b}", [P, KF, D]) for b in range(2)]
        idx = [g.sb(s, f"idx{b}", [P, 1], u32) for b in range(2)]
        xg = [g.sb(s, f"xg{b}", [P, D]) for b in range(2)]
        xT = [g.sb(s, f"xT{b}", [P, KD, P]) for b in range(2)]
        sg = [g.sb(s, f"sg{b}", [P, FF]) for b in range(2)]
        hm = [g.sb(s, f"hm{b}", [P, FF]) for b in range(2)]
        hmT = [g.sb(s, f"hmT{b}", [P, KF, P]) for b in range(2)]
        y = [g.sb(s, f"y{b}", [P, D]) for b in range(2)]
        tiny = g.sb(s, "tiny", [P, 3])
        tiny_made, = g.sems(name, "tiny_made")

        def pair(names):
            return {n: g.sems(name, f"{n}0 {n}1") for n in names.split()}

        A = pair("s_loaded s_gu s_silu s_h s_ht s_htc s_y s_yc")
        M = pair("wgu_loaded wd_loaded idx_ready gathered xT_ps xT_copied gu_ps silu_done h_ready ht_ps ht_copied "
                 "y_ps y_low y_copied y_stored passed")
        block = s.enter_context(nc.Block())

        def y_banks(b):
            return (6, 7) if b == 0 else (0, 1)

        def gate_up(b, lhsT):
            for k in range(KD):
                last = nc.tensor.matmul(g.ps[:, 4 + b, :], lhsT(k), wgu[b][:, k, :], start=(k == 0), stop=(k == KD - 1))
            return last

        def turn_h(b):
            for f in range(KF):
                last = nc.tensor.transpose(g.ps[:, 2 + b, f * P:(f + 1) * P], hm[b][:, f * P:(f + 1) * P], g.ident[:, :])
            return last

        def down(b):
            for o in range(2):
                for f in range(KF):
                    last = nc.tensor.matmul(g.ps[:, y_banks(b)[o], :], hmT[b][:, f, :], wd[b][:, f, o * 512:(o + 1) * 512],
                                            start=(f == 0), stop=(f == KF - 1))
            return last

        def y_half(o, b):
            return g.ps[:, y_banks(b)[o], :]

        @block.sync
        def _(sp):
            for b in range(2):
                sp.dma_start(wgu[b][:, :, 0:FF], io["moe_ws_gate"][layer].rearrange("(k p) f -> p k f", p=P)).then_inc(A["s_loaded"][b], 16)
                sp.dma_start(wgu[b][:, :, FF:2 * FF], io["moe_ws_up"][layer].rearrange("(k p) f -> p k f", p=P)).then_inc(A["s_loaded"][b], 16)
                sp.dma_start(wd[b][:, :, :], io["moe_ws_down"][layer].rearrange("(k p) n -> p k n", p=P)).then_inc(A["s_loaded"][b], 16)
            sp.wait_ge(A["s_y"][0], N // 2)
            sp.wait_ge(A["s_y"][1], N // 2)
            pairs = sp.value_load(R.pairs[0:1, 0:1], min_val=1, max_val=NB // 2)
            with sp.Fori(0, NB // 2) as i:
                with sp.If(i < pairs):
                    for b in range(2):
                        e = sp.value_load(R.block_expert[0:1, bass.ds(i * 2 + b, 1)], min_val=0, max_val=E - 1)
                        sp.wait_ge(M["gu_ps"][b], i + 1)
                        sp.dma_start(wgu[b][:, :, 0:FF], io["moe_w_gate"][layer, bass.ds(e, 1)].rearrange("e (p k) f -> p (e k) f", k=KD))\
                            .then_inc(M["wgu_loaded"][b], 16)
                        sp.dma_start(wgu[b][:, :, FF:2 * FF], io["moe_w_up"][layer, bass.ds(e, 1)].rearrange("e (p k) f -> p (e k) f", k=KD))\
                            .then_inc(M["wgu_loaded"][b], 16)
                        sp.wait_ge(M["y_ps"][b], i + 1)
                        sp.dma_start(wd[b][:, :, :], io["moe_w_down"][layer, bass.ds(e, 1)].rearrange("e (k p) n -> p (e k) n", p=P))\
                            .then_inc(M["wd_loaded"][b], 16)

        @block.gpsimd
        def _(pool):
            nc.gpsimd.memset(tiny[:, :], 0.0).then_inc(tiny_made, 1)
            pool.wait_ge(tiny_made, 1)
            for b in range(2):
                pool.sem_inc(M["passed"][b], 1)
            pairs = pool.value_load(R.pairs[0:1, 0:1], min_val=1, max_val=NB // 2)
            with pool.Fori(0, NB // 2) as i:
                with pool.If(i < pairs):
                    for b in range(2):
                        pool.wait_ge(M["xT_ps"][b], i + 1)
                        pool.wait_ge(M["idx_ready"][b], i + 1)
                        pool.wait_ge(M["passed"][b], i + 1)
                        nc.gpsimd.tensor_tensor(tiny[:, 1 + b:2 + b], tiny[:, 0:1], tiny[:, 0:1], ALU.add).then_inc(M["passed"][b], 1)
                        nc.gpsimd.indirect_dma_start(xg[b][:, :], None, g.h_rows, bass.IndirectOffsetOnAxis(ap=idx[b][:, 0:1], axis=0))\
                            .then_inc(M["gathered"][b], 16)

        @block.tensor
        def _(pe):
            for j in range(N // 2):
                for b in range(2):
                    t = tiles[2 * j + b]
                    pe.wait_ge(A["s_loaded"][b], 48)
                    gate_up(b, lambda k: hT[:, k, t * P:(t + 1) * P]).then_inc(A["s_gu"][b], 1)
                for b in range(2):
                    pe.wait_ge(A["s_h"][b], j + 1)
                    turn_h(b).then_inc(A["s_ht"][b], 1)
                    pe.wait_ge(A["s_htc"][b], j + 1)
                    if j:
                        pe.wait_ge(A["s_yc"][b], j)
                    down(b).then_inc(A["s_y"][b], 1)
            pe.wait_ge(A["s_yc"][1], N // 2)
            pe.wait_ge(A["s_yc"][0], N // 2)
            for b in range(2):
                for credit in ("gu_ps", "y_ps", "xT_ps"):
                    pe.sem_inc(M[credit][b], 1)
            pairs = pe.value_load(R.pairs[0:1, 0:1], min_val=1, max_val=NB // 2)
            with pe.Fori(0, NB // 2) as i:
                with pe.If(i < pairs):
                    for b in range(2):
                        pe.wait_ge(M["gathered"][b], i * 16 + 16)
                        if b == 0:
                            pe.wait_ge(M["y_copied"][1], i + 1)
                        cols = xg[b][:, :].rearrange("p (q k) -> p k q", k=KD)
                        for k in range(KD):
                            last = nc.tensor.transpose(g.ps[:, 2 * b + k // 4, (k % 4) * P:(k % 4 + 1) * P], cols[:, k, :], g.ident[:, :])
                        last.then_inc(M["xT_ps"][b], 1)
                    for b in range(2):
                        pe.wait_ge(M["xT_copied"][b], i + 1)
                        pe.wait_ge(M["wgu_loaded"][b], i * 32 + 32)
                        gate_up(b, lambda k: xT[b][:, k, :]).then_inc(M["gu_ps"][b], 1)
                    for b in range(2):
                        pe.wait_ge(M["h_ready"][b], i + 1)
                        turn_h(b).then_inc(M["ht_ps"][b], 1)
                        pe.wait_ge(M["ht_copied"][b], i + 1)
                        pe.wait_ge(M["wd_loaded"][b], i * 16 + 16)
                        if b == 0:
                            pe.wait_ge(M["y_copied"][0], i + 1)
                        down(b).then_inc(M["y_ps"][b], 1)

        @block.scalar
        def _(act):
            def silu(b, waited, at, done):
                act.wait_ge(waited[b], at)
                nc.scalar.activation(sg[b][:, :], g.ps[:, 4 + b, 0:FF], ACT.Silu).then_inc(done[b], 1)

            def take_ht(b, waited, at, done):
                act.wait_ge(waited[b], at)
                nc.scalar.activation(hmT[b][:, :, :].rearrange("p f r -> p (f r)"), g.ps[:, 2 + b, 0:FF], ACT.Copy).then_inc(done[b], 1)

            for j in range(N // 2):
                for b in range(2):
                    silu(b, A["s_gu"], j + 1, A["s_silu"])
                for b in range(2):
                    take_ht(b, A["s_ht"], j + 1, A["s_htc"])
            for b in range(2):
                act.sem_inc(M["y_stored"][b], 16)
            pairs = act.value_load(R.pairs[0:1, 0:1], min_val=1, max_val=NB // 2)
            with act.Fori(0, NB // 2) as i:
                with act.If(i < pairs):
                    for b in range(2):
                        act.wait_ge(M["xT_ps"][b], i + 2)
                        nc.scalar.activation(xT[b][:, :, :].rearrange("p k r -> p (k r)"),
                                             g.ps[:, 2 * b:2 * b + 2, :].rearrange("p a c -> p (a c)"), ACT.Copy)\
                            .then_inc(M["xT_copied"][b], 1)
                    for b in range(2):
                        silu(b, M["gu_ps"], i + 2, M["silu_done"])
                    for b in range(2):
                        take_ht(b, M["ht_ps"], i + 1, M["ht_copied"])
                        act.wait_ge(M["y_ps"][b], i + 2)
                        act.wait_ge(M["y_stored"][b], i * 16 + 16)
                        nc.scalar.activation(y[b][:, 0:512], y_half(0, b), ACT.Copy).then_inc(M["y_low"][b], 1)
                    for b in range(2):
                        act.wait_ge(M["y_low"][b], i + 1)
                        act.wait_ge(M["y_copied"][b], i + 2)
                        act.dma_start(g.y_rows[bass.ds(i * (2 * P) + b * P, P), :], y[b][:, :]).then_inc(M["y_stored"][b], 16)
            for b in range(2):
                act.wait_ge(M["y_stored"][b], pairs * 16 + 16)
                nc.scalar.activation(y[b][:, 0:1], y[b][:, 0:1], ACT.Copy)

        @block.vector
        def _(dve):
            def multiply(b, waited, at, done):
                dve.wait_ge(waited[b], at)
                nc.vector.tensor_tensor(hm[b][:, :], sg[b][:, :], g.ps[:, 4 + b, FF:2 * FF], ALU.mult).then_inc(done[b], 1)

            for j in range(N // 2):
                for b in range(2):
                    multiply(b, A["s_silu"], j + 1, A["s_h"])
                for b in range(2):
                    t = tiles[2 * j + b]
                    dve.wait_ge(A["s_y"][b], j + 1)
                    y0 = y_banks(b)[0]
                    nc.vector.tensor_copy(F[:, t, :], g.ps[:, y0:y0 + 2, :].rearrange("p a c -> p (a c)")).then_inc(A["s_yc"][b], 1)

            for b in range(2):
                dve.sem_inc(M["y_copied"][b], 1)
                nc.vector.tensor_copy(idx[b][:, :], R.rows[:, b:b + 1]).then_inc(M["idx_ready"][b], 1)
            pairs = dve.value_load(R.pairs[0:1, 0:1], min_val=1, max_val=NB // 2)
            with dve.Fori(0, NB // 2) as i:
                with dve.If(i < pairs):
                    for b in range(2):
                        dve.wait_ge(M["gathered"][b], i * 16 + 16)
                        nc.vector.tensor_copy(idx[b][:, :], R.rows[:, bass.ds(i * 2 + (2 + b), 1)]).then_inc(M["idx_ready"][b], 1)
                    for b in range(2):
                        multiply(b, M["silu_done"], i + 1, M["h_ready"])
                    for b in range(2):
                        dve.wait_ge(M["y_low"][b], i + 1)
                        nc.vector.tensor_copy(y[b][:, 512:D], y_half(1, b)).then_inc(M["y_copied"][b], 1)


def stage_combine(nc, g, name, tiles, R, F):
    NBUF = 6
    with ExitStack() as s:
        buf = g.sb(s, "buf", [P, NBUF, D])
        gathered = [g.sem(f"{name}_gathered{b}") for b in range(NBUF)]
        used, = g.sems(name, "used")
        block = s.enter_context(nc.Block())
        work = [(n, t, k) for n, t in enumerate(tiles) for k in range(TOPK)]
        work.sort(key=lambda w: (w[0] // 2, w[2], w[0]))

        @block.gpsimd
        def _(pool):
            for j, (n, t, k) in enumerate(work):
                if j >= NBUF:
                    pool.wait_ge(used, j - NBUF + 1)
                c = n * TOPK + k
                nc.gpsimd.indirect_dma_start(buf[:, j % NBUF, :], None, g.y_rows, bass.IndirectOffsetOnAxis(ap=R.pos[:, c:c + 1], axis=0))\
                    .then_inc(gathered[j % NBUF], 16)

        @block.vector
        def _(dve):
            for j, (n, t, k) in enumerate(work):
                if j >= 2:
                    dve.wait_ge(used, j - 1)
                dve.wait_ge(gathered[j % NBUF], 16 * (j // NBUF + 1))
                nc.vector.scalar_tensor_tensor(F[:, t, :], buf[:, j % NBUF, :], R.gates[:, n, k:k + 1], F[:, t, :], ALU.mult, ALU.add)\
                    .then_inc(used, 1)



def program(nc, io):
    g = Core()
    g.io = io
    g.names = {}
    outer = ExitStack()
    with outer:
        def sb(stack, name, shape, dt=fp32):
            g.names[name] = g.names.get(name, 0) + 1
            return stack.enter_context(nc.sbuf_tensor(f"{name}_{g.names[name]}", shape, dt))

        def sem(name):
            return nc.alloc_semaphore(name)

        def recycle():
            nc.clear_and_free_semaphores(nc.allocated_since(g.kept))
            nc.all_engine_barrier()

        g.sb, g.sem = sb, sem
        g.sems = lambda stage, names: [sem(f"{stage}_{n}") for n in names.split()]
        g.mod_vecs = nc.dram_tensor("mod_vecs", [2, 2, 6, D], fp32).ap()
        g.h_rows = nc.dram_tensor("h_rows", [T, D], fp32).ap()
        g.x_rows = nc.dram_tensor("x_rows", [T, D], fp32).ap()
        g.ps = outer.enter_context(nc.psum_tensor("ps", [P, 8, 512], fp32))
        g.ident = sb(outer, "ident", [P, P])
        g.ones = sb(outer, "ones", [P, P])
        g.before = sb(outer, "before", [P, P])
        g.token_id = sb(outer, "token_id", [P, TT], i32)
        g.mask = sb(outer, "mask", [P, 2, P], i32)
        g.eps = sb(outer, "eps", [P, 1])
        hT = sb(outer, "hT", [P, KD, T])
        g.y_rows = nc.dram_tensor("y_rows", [n_blocks(TT) * P, D], fp32).ap()
        g.ya_rows = nc.dram_tensor("ya_rows", [P, KD, T], fp32).ap()
        g.yb_rows = nc.dram_tensor("yb_rows", [P, KD, T], fp32).ap()
        settled = sem("settled")

        def hold(eng, n=1):
            eng.wait_ge(settled, n)
        g.hold = hold
        g.settled = settled

        stage_constants(nc, g)
        g.kept = nc.snapshot_sems()
        stage_modulation(nc, g)
        x0 = lambda t: tile_rows(io["ctx"][0], t) if t < CT else tile_rows(io["x"][0], t - CT)
        def moe(layer, X, tiles, F, store):
            name = f"moe{layer}"
            with ExitStack() as s:
                R = Core()
                R.gates = sb(s, "gates", [P, TT, TOPK])
                R.pos = sb(s, "pos", [P, TT * TOPK], u32)
                R.rows = sb(s, "rows", [P, n_blocks(TT) + 2], u32)
                R.block_expert = sb(s, "block_expert", [1, P], i32)
                R.pairs = sb(s, "pairs", [1, 1], i32)
                recycle()
                stage_route(nc, g, name + "r", layer, hT, tiles, R)
                stage_experts(nc, g, name + "e", layer, hT, tiles, R, F)
                stage_combine(nc, g, name + "c", tiles, R, F)
                stage_residual(nc, g, name + "x", layer, 1, F, X, tiles, store=store)

        every, latent = list(range(TT)), list(range(CT, TT))
        with ExitStack() as s:
            X = sb(s, "X", [P, TT, D])
            stage_norm(nc, g, "n00", 0, 0, X, hT, load_x=x0)
        stage_lru(nc, g, hT)
        stage_attention(nc, g, "gla", hT, True)
        with ExitStack() as s:
            F = sb(s, "F", [P, TT, D])
            X = sb(s, "X", [P, TT, D])
            stage_mix_out(nc, g, "mo0", io["ab_w_out"][0], ((g.ya_rows, KD), (g.yb_rows, KD)), F, every)
            stage_residual(nc, g, "r0", 0, 0, F, X, every, load_x=x0)
            stage_norm(nc, g, "n01", 0, 1, X, hT, store_rows=True)
            moe(0, X, every, F, lambda t: tile_rows(g.x_rows, t))
            recycle()
            stage_norm(nc, g, "n10", 1, 0, X, hT, column_major=True)
        stage_attention(nc, g, "hgrn", hT, False)
        with ExitStack() as s:
            F = sb(s, "F", [P, TT, D])
            X = sb(s, "X", [P, TT, D])
            stage_mix_out(nc, g, "mo1", io["c_w_out"][0], ((g.yb_rows, KD),), F, latent)
            stage_residual(nc, g, "r1", 1, 0, F, X, latent, load_x=lambda t: tile_rows(g.x_rows, t))
            stage_norm(nc, g, "n11", 1, 1, X, hT, store_rows=True, lat_only=True)
            moe(1, X, latent, F, lambda t: tile_rows(io["out"][0], t - CT))


_INPUTS = ["x", "c", "ctx", "c_ctx", "mod_w", "mod_b", "pre_gain", "post_gain", "ab_w_in", "ab_conv_w", "ab_conv_b",
           "ab_lru_wa", "ab_lru_ba", "ab_lru_wi", "ab_lru_bi", "ab_lru_lambda", "ab_gla_wa2", "ab_gla_ba", "ab_w_out",
           "c_w_in", "hgrn_lb_logits", "c_w_out", "moe_router", "moe_bias", "moe_w_gate", "moe_w_up", "moe_w_down",
           "moe_ws_gate", "moe_ws_up", "moe_ws_down"]


def kernel(**inputs):
    import numpy as np
    import concourse.bacc as bacc
    from concourse.bass_utils import run_bass_kernel_spmd

    nc = bacc.Bacc("TRN2", target_bir_lowering=False, num_devices=1)
    arrays, io = {}, {}
    for name in _INPUTS:
        a = np.ascontiguousarray(inputs[name])
        arrays[f"in_{name}"] = a
        io[name] = nc.dram_tensor(f"in_{name}", a.shape, mybir.dt.from_np(a.dtype), kind="ExternalInput").ap()
    io["out"] = nc.dram_tensor("out_0", (1, LAT, D), fp32, kind="ExternalOutput").ap()
    program(nc, io)
    r = run_bass_kernel_spmd(nc, [arrays], core_ids=[0])
    return r.results[0]["out_0"]
```

```python
import concourse.bass as bass
from concourse import mybir
from contextlib import ExitStack

fp32 = mybir.dt.float32
i32 = mybir.dt.int32
u32 = mybir.dt.uint32
ALU = mybir.AluOpType
ACT = mybir.ActivationFunctionType
AX = mybir.AxisListType

P = 128
D = 1024
KD = D // P
CTX, LAT = 256, 512
T = CTX + LAT
TT = T // P
CT = CTX // P
EPS = 1e-6
GRID_W = 64
GRID_H = LAT // GRID_W
CHUNK = 64
NCH = T // CHUNK
CCH = CTX // CHUNK
E = 64
TOPK = 8
FF = 256
KF = FF // P
ROUTED_SCALE = 2.5
LRU_C = 8.0
GLA_TAU = 16.0
GLA_RANK = 16


class Link:

    def __init__(self, eng, sem):
        self.eng, self.sem, self.n, self.trip, self.per = eng, sem, 0, None, 0

    def value(self):
        return self.n if self.trip is None else self.trip * self.per + self.n

    def mark(self, ins):
        ins.then_inc(self.sem, 1)
        self.n += 1

    def wait(self):
        self.eng.wait_ge(self.sem, self.value())

    def __call__(self, ins):
        self.mark(ins)
        self.wait()

    def enter(self, trip, per):
        self.trip, self.per, self.before = trip, per, self.n

    def leave(self, trips):
        assert self.n - self.before == self.per, (self.n - self.before, self.per)
        self.n = self.before + trips * self.per
        self.trip = None


class Core:
    pass


def stage_constants(nc, g):
    with nc.Block() as block:
        made = g.sem("const_made")

        @block.gpsimd
        def _(pool):
            link = Link(pool, made)
            pool.sem_inc(g.settled, 4)
            link.mark(nc.gpsimd.memset(g.ones[:, :], 1.0))
            link.mark(nc.gpsimd.memset(g.eps[:, :], EPS))
            link.mark(nc.gpsimd.memset(g.ident[:, :], 0.0))
            link.mark(nc.gpsimd.memset(g.before[:, :], 0.0))
            link.mark(nc.gpsimd.iota(g.token_id[:, :], pattern=[[P, TT]], base=0, channel_multiplier=1))
            link(nc.gpsimd.memset(g.mask[:, :, :], 0.0))
            link.mark(nc.gpsimd.affine_select(out=g.ident[:, :], in_=g.ident[:, :], compare_op=ALU.not_equal,
                                              fill=1.0, base=0, pattern=[[-1, P]], channel_multiplier=1))
            link.mark(nc.gpsimd.affine_select(out=g.before[:, :], in_=g.before[:, :], compare_op=ALU.is_ge,
                                              fill=1.0, base=0, pattern=[[-1, P]], channel_multiplier=1))
            for h in range(2):
                rows = slice(h * CHUNK, (h + 1) * CHUNK)
                link.mark(nc.gpsimd.affine_select(out=g.mask[rows, 0, rows], in_=g.mask[rows, 0, rows],
                                                  compare_op=ALU.is_gt, fill=1.0, base=0, pattern=[[-1, CHUNK]],
                                                  channel_multiplier=1))
                link(nc.gpsimd.affine_select(out=g.mask[rows, 1, rows], in_=g.mask[rows, 1, rows],
                                             compare_op=ALU.is_gt, fill=1.0, base=0, pattern=[[1, CHUNK]],
                                             channel_multiplier=-1))


def stage_modulation(nc, g, hT, load_x):
    NS = 6 * D // 512
    GROUPS = 4
    with ExitStack() as s:
        cc = g.sb(s, "cc", [16, P])
        cs = g.sb(s, "cs", [16, P])
        cT = g.sb(s, "cT", [P, 16])
        w = [g.sb(s, f"modw{i}", [P, KD, 512]) for i in range(2)]
        m = g.sb(s, "m", [2, 6, D])
        mb = g.sb(s, "mb", [2, 6, D])
        gain = g.sb(s, "gain", [2, 4, D])
        vec = g.sb(s, "vec", [2, 6, D])
        mf, mbf = (t[:, :, :].rearrange("s r d -> s (r d)") for t in (m, mb))
        X = g.sb(s, "X", [P, TT, D])
        sq = g.sb(s, "sq", [P, D])
        xn = g.sb(s, "xn", [P, 2, D])
        st = g.sb(s, "st", [P, 3, TT])
        ab = g.sb(s, "ab", [4 * KD, P])
        abT = g.sb(s, "abT", [P, 2, 2, KD])
        x_loaded, x_squared, x_root, rstd_ready, xn_ready, x_turned, x_taken, ab_loaded, ab_ps, ab_ready = g.sems(
            "mod", "x_loaded x_squared x_root rstd_ready xn_ready x_turned x_taken ab_loaded ab_ps ab_ready")
        c_loaded, silu_done, cT_ps, cT_done = g.sems("mod", "c_loaded silu_done cT_ps cT_done")
        w_loaded = g.sems("mod", "w_loaded0 w_loaded1")
        w_used = g.sems("mod", "w_used0 w_used1")
        evacuated = g.sems("mod", "evacuated0 evacuated1")
        bias_loaded, vec_ready, vec_stored, chain = g.sems("mod", "bias_loaded vec_ready vec_stored chain")

        turned = lambda t: g.ps[:, 4 + 2 * (t % 2):6 + 2 * (t % 2), :]
        block = s.enter_context(nc.Block())

        @block.sync
        def _(sp):
            sp.dma_start(cc[0:8, :], g.io["c"].rearrange("a (k p) -> (a k) p", p=P)).then_inc(c_loaded, 16)
            sp.dma_start(cc[8:16, :], g.io["c_ctx"].rearrange("(k p) -> k p", p=P)).then_inc(c_loaded, 16)
            for layer in range(2):
                wl = g.io["mod_w"][layer].rearrange("(k p) n -> p k n", p=P)
                if layer:
                    sp.wait_ge(vec_ready, layer)
                sp.dma_start(mb[:, :, :].rearrange("s r d -> s (r d)"),
                             g.io["mod_b"][layer].partition_broadcast(2)).then_inc(bias_loaded, 16)
                sp.dma_start(gain[:, 0:2, :].rearrange("s r d -> s (r d)"),
                             g.io["pre_gain"][layer].rearrange("r d -> (r d)").partition_broadcast(2)).then_inc(bias_loaded, 16)
                sp.dma_start(gain[:, 2:4, :].rearrange("s r d -> s (r d)"),
                             g.io["post_gain"][layer].rearrange("r d -> (r d)").partition_broadcast(2)).then_inc(bias_loaded, 16)
                for b in range(2):
                    if layer:
                        sp.wait_ge(w_used[b], layer * NS // 2)
                    sp.dma_start(w[b][:, :, :], wl[:, :, b * 512:(b + 1) * 512]).then_inc(w_loaded[b], 16)
                with sp.Fori(0, NS // 2 - 1) as i:
                    for b in range(2):
                        sp.wait_ge(w_used[b], i + (layer * NS // 2 + 1))
                        sp.dma_start(w[b][:, :, :], wl[:, :, bass.ds(i * 1024 + (1024 + b * 512), 512)]).then_inc(w_loaded[b], 16)
            sp.wait_ge(vec_ready, 2)
            sp.dma_start(g.mod_vecs[1], vec[:, :, :]).then_inc(vec_stored, 16)
            sp.wait_ge(vec_stored, 32)

        @block.scalar
        def _(act):
            act.wait_ge(c_loaded, 32)
            nc.scalar.activation(cs[:, :], cc[:, :], ACT.Silu).then_inc(silu_done, 1)
            act.wait_ge(x_loaded, 16 * TT)
            for t in range(TT):
                if t:
                    act.wait_ge(x_squared, t)
                nc.scalar.activation(sq[:, :], X[:, t, :], ACT.Square, accum_out=st[:, 0, t:t + 1]).then_inc(x_squared, 1)
            act.wait_ge(x_squared, TT)
            nc.scalar.activation(st[:, 1, :], st[:, 0, :], ACT.Sqrt, scale=1.0 / D, bias=g.eps[:, 0:1]).then_inc(x_root, 1)
            act.wait_ge(rstd_ready, 1)

            def take(t):
                act.wait_ge(x_turned, t + 1)
                nc.scalar.activation(hT[:, :, t * P:(t + 1) * P], turned(t).rearrange("p a (k q) -> p (a k) q", q=P), ACT.Copy)\
                    .then_inc(x_taken, 1)

            for t in range(TT):
                nc.scalar.activation(xn[:, t % 2, :], X[:, t, :], ACT.Copy, scale=st[:, 2, t:t + 1]).then_inc(xn_ready, 1)
                if t:
                    take(t - 1)
            take(TT - 1)
            act.wait_ge(vec_ready, 1)
            act.dma_start(g.mod_vecs[0], vec[:, :, :]).then_inc(vec_stored, 16)
            act.wait_ge(vec_stored, 16)
            act.dma_start(ab[:, :], g.mod_vecs[0, :, 0:2, :].rearrange("s r (k p) -> s (r k) p", p=P)).then_inc(ab_loaded, 16)
            act.wait_ge(x_taken, TT)
            act.wait_ge(ab_ready, 1)
            for k in range(KD // 2, KD):
                for o, n, stream in ((0, CTX, 1), (CTX, LAT, 0)):
                    nc.scalar.activation(hT[:, k, o:o + n], hT[:, k, o:o + n], ACT.Identity, scale=abT[:, stream, 0, k:k + 1],
                                         bias=abT[:, stream, 1, k:k + 1])

        @block.gpsimd
        def _(pool):
            for t in range(TT):
                pool.dma_start(X[:, t, :], load_x(t)).then_inc(x_loaded, 16)

        @block.tensor
        def _(pe):
            pe.wait_ge(silu_done, 1)
            nc.tensor.transpose(g.ps[:, 2, 0:16], cs[:, :], g.ident[0:16, 0:16]).then_inc(cT_ps, 1)
            pe.wait_ge(cT_done, 1)
            for layer in range(2):
                with pe.Fori(0, NS // 2) as i:
                    for b in range(2):
                        pe.wait_ge(evacuated[b], i + (layer * NS // 2 + 1))
                        pe.wait_ge(w_loaded[b], i * 16 + (layer * NS // 2 + 1) * 16)
                        for k in range(KD):
                            at = 32 * (k % GROUPS)
                            last = nc.tensor.matmul(g.ps[at:at + 2, b, :], cT[:, k:k + 9:8], w[b][:, k, :],
                                                    start=(k < GROUPS), stop=(k >= KD - GROUPS), tile_position=(0, at))
                        last.then_inc(w_used[b], 1)
                if layer == 0:
                    for t in range(TT):
                        pe.wait_ge(xn_ready, t + 1)
                        if t >= 2:
                            pe.wait_ge(x_taken, t - 1)
                        for k in range(KD):
                            last = nc.tensor.transpose(turned(t)[:, k // 4, (k % 4) * P:(k % 4 + 1) * P],
                                                       xn[:, t % 2, k * P:(k + 1) * P], g.ident[:, :])
                        last.then_inc(x_turned, 1)
            pe.wait_ge(ab_loaded, 16)
            nc.tensor.transpose(g.ps[:, 2, 0:4 * KD], ab[:, :], g.ident[0:4 * KD, 0:4 * KD]).then_inc(ab_ps, 1)

        @block.vector
        def _(dve):
            link = Link(dve, chain)
            for b in range(2):
                dve.sem_inc(evacuated[b], 1)
            dve.wait_ge(cT_ps, 1)
            nc.vector.tensor_copy(cT[:, :], g.ps[:, 2, 0:16]).then_inc(cT_done, 1)
            for layer in range(2):
                dve.wait_ge(bias_loaded, 48 * (layer + 1))
                with dve.Fori(0, NS // 2) as i:
                    link.enter(i, 2 * (GROUPS - 1))
                    for b in range(2):
                        at = bass.ds(i * 1024 + b * 512, 512)
                        dve.wait_ge(w_used[b], i + (layer * NS // 2 + 1))
                        for j in range(GROUPS):
                            so_far = mf if j else mbf
                            last = nc.vector.tensor_tensor(mf[:, at], g.ps[32 * j:32 * j + 2, b, :], so_far[:, at], ALU.add)
                            if j < GROUPS - 1:
                                link(last)
                        last.then_inc(evacuated[b], 1)
                    link.leave(NS // 2)
                if layer == 0:
                    dve.wait_ge(x_root, 1)
                    nc.vector.reciprocal(st[:, 2, :], st[:, 1, :]).then_inc(rstd_ready, 1)
                if layer:
                    dve.wait_ge(ab_ps, 1)
                    nc.vector.tensor_copy(abT[:, :, :, :].rearrange("p s r k -> p (s r k)"), g.ps[:, 2, 0:4 * KD]).then_inc(ab_ready, 1)
                    dve.wait_ge(ab_ready, 1)
                    dve.wait_ge(x_taken, TT)
                    for k in range(KD // 2):
                        for o, n, stream in ((0, CTX, 1), (CTX, LAT, 0)):
                            nc.vector.tensor_scalar(hT[:, k, o:o + n], hT[:, k, o:o + n], abT[:, stream, 0, k:k + 1],
                                                    abT[:, stream, 1, k:k + 1], ALU.mult, ALU.add)
                for b in range(2):
                    dve.wait_ge(evacuated[b], (layer + 1) * NS // 2 + 1)
                if layer:
                    dve.wait_ge(vec_stored, 16)
                nc.vector.scalar_tensor_tensor(vec[:, 0, :], m[:, 1, :], 1.0, gain[:, 0, :], ALU.add, ALU.mult)
                nc.vector.tensor_copy(vec[:, 1, :], m[:, 0, :])
                nc.vector.tensor_tensor(vec[:, 2, :], m[:, 2, :], gain[:, 2, :], ALU.mult)
                nc.vector.scalar_tensor_tensor(vec[:, 3, :], m[:, 4, :], 1.0, gain[:, 1, :], ALU.add, ALU.mult)
                nc.vector.tensor_copy(vec[:, 4, :], m[:, 3, :])
                nc.vector.tensor_tensor(vec[:, 5, :], m[:, 5, :], gain[:, 3, :], ALU.mult).then_inc(vec_ready, 1)


def load_vectors(nc, g, sp, layer, row, dst, loaded, streams=(0, 1)):
    for st in streams:
        sp.dma_start(dst[:, st, :], g.mod_vecs[layer, st, row].partition_broadcast(P)).then_inc(loaded, 16)


def tile_rows(ap, t):
    return ap[t * P:(t + 1) * P, :]


SEGS = ((0, CTX), (CTX, LAT))


def token_row(g, bank):
    return g.ps[:, bank:bank + 2, :].rearrange("p b c -> p (b c)")[:, 512 - CTX:512 + LAT]


def project(nc, out, lhsT, hT, segs=SEGS):
    for o, n in segs:
        for k in range(KD):
            last = nc.tensor.matmul(out[:, o - segs[0][0]:o - segs[0][0] + n], lhsT(k), hT[:, k, o:o + n],
                                    start=(k == 0), stop=(k == KD - 1))
    return last


AB_LRU_IN = D
AB_Q, AB_K, AB_V, AB_OG, AB_ALR = 2048, 2560, 3072, 4096, 5120


def stage_lru(nc, g, hT):
    io = g.io
    NP = 11
    LEFT, GAP = 2, 3
    XP = CTX + LAT + 2 * GAP
    XC = CTX + GAP + LAT
    with ExitStack() as s:
        wx = g.sb(s, "wx", [P, KD, P])
        wg = g.sb(s, "wg", [P, KD, P])
        w4 = g.sb(s, "w4", [P, 4, P])
        par = g.sb(s, "par", [P, P])
        table = g.sb(s, "table", [P, 13, 8])
        tmp = g.sb(s, "tmp", [P, 8, 16])
        cur = g.sb(s, "cur", [P, 13])
        xp = g.sb(s, "xp", [P, XP])
        xc = g.sb(s, "xc", [P, XC])
        gel = g.sb(s, "gel", [P, T])
        Rg = g.sb(s, "Rg", [P, 2, T])
        Ig = g.sb(s, "Ig", [P, 2, T])
        Ag = g.sb(s, "Ag", [P, 2, T])
        Th = g.sb(s, "Th", [P, 2, T])
        V = g.sb(s, "V", [P, 2, T])
        S2 = g.sb(s, "S2", [P, 2, T])
        ya = g.sb(s, "ya", [P, KD, T])
        par_loaded, par_ps, lam_ready, lam_exp, lam_w, lam_ln, chain, achain = g.sems(
            "lru", "par_loaded par_ps lam_ready lam_exp lam_w lam_ln chain achain")
        wx_loaded, wg_loaded, w4_loaded = g.sems("lru", "wx_loaded wg_loaded w4_loaded")
        x_ready, xp_ready, xc_ready, g_ready, gel_ready, ri_ready, ri_copied = g.sems(
            "lru", "x_ready xp_ready xc_ready g_ready gel_ready ri_ready ri_copied")
        decay_ready, v_ready, s_ready, y_ready, stored = g.sems("lru", "decay_ready v_ready s_ready y_ready stored")
        wx_d = io["ab_w_in"][0].rearrange("(k p) n -> p k n", p=P)
        block = s.enter_context(nc.Block())

        @block.sync
        def _(sp):
            rows = lambda ap: ap.rearrange("r (j p) -> (r j) p", p=P)
            for r, name in ((0, "ab_conv_w"), (5, "ab_lru_ba"), (7, "ab_lru_bi"), (9, "ab_lru_lambda")):
                src = rows(io[name][0])
                sp.dma_start(par[8 * r:8 * r + src.shape[0], :], src).then_inc(par_loaded, 16)
            sp.dma_start(par[32:40, :], rows(io["ab_conv_b"])).then_inc(par_loaded, 16)

            def load_x(col):
                sp.dma_start(wx[:, :, :], wx_d[:, :, col(AB_LRU_IN)]).then_inc(wx_loaded, 16)

            def load_g(col):
                sp.dma_start(wg[:, :, :], wx_d[:, :, col(0)]).then_inc(wg_loaded, 16)

            def load_4(head):
                for n, name in enumerate(("ab_lru_wa", "ab_lru_wi")):
                    sp.dma_start(w4[:, n:n + 3:2, :].rearrange("p d e -> p d e"),
                                 io[name][0][:, head, :, :].rearrange("d h p e -> p (d h) e")).then_inc(w4_loaded, 16)

            load_x(lambda o: slice(o, o + P))
            load_g(lambda o: slice(o, o + P))
            load_4(slice(0, 1))
            with sp.Fori(0, KD - 1) as i:
                sp.wait_ge(x_ready, i + 1)
                load_x(lambda o: bass.ds(i * P + (o + P), P))
                sp.wait_ge(g_ready, i + 1)
                load_g(lambda o: bass.ds(i * P + (o + P), P))
                sp.wait_ge(ri_ready, i * 2 + 2)
                load_4(bass.ds(i + 1, 1))
                sp.wait_ge(y_ready, i + 2)
                sp.dma_start(g.ya_rows[:, bass.ds(i, 1), :], ya[:, bass.ds(i, 1), :]).then_inc(stored, 16)
            sp.wait_ge(y_ready, KD + 1)
            sp.dma_start(g.ya_rows[:, KD - 1:KD, :], ya[:, KD - 1:KD, :]).then_inc(stored, 16)
            sp.wait_ge(stored, 16 * KD)

        @block.tensor
        def _(pe):
            pe.wait_ge(par_loaded, 80)
            nc.tensor.transpose(g.ps[:, 7, 0:8 * NP], par[0:8 * NP, :], g.ident[0:8 * NP, 0:8 * NP]).then_inc(par_ps, 1)
            with pe.Fori(0, KD) as i:
                pe.wait_ge(wx_loaded, i * 16 + 16)
                pe.wait_ge(xp_ready, i + 1)
                project(nc, token_row(g, 0), lambda k: wx[:, k, :], hT).then_inc(x_ready, 1)
                pe.wait_ge(wg_loaded, i * 16 + 16)
                pe.wait_ge(gel_ready, i + 1)
                project(nc, token_row(g, 2), lambda k: wg[:, k, :], hT).then_inc(g_ready, 1)
                pe.wait_ge(w4_loaded, i * 32 + 32)
                pe.wait_ge(xc_ready, i + 2)
                for d in range(2):
                    pe.wait_ge(ri_copied, i * 2 + (d + 1))
                    for n in range(2):
                        out = token_row(g, 4 + 2 * n)
                        nc.tensor.matmul(out[:, 0:CTX], w4[:, 2 * d + n, :], xc[:, 0:CTX], start=True, stop=True)
                        last = nc.tensor.matmul(out[:, CTX:T], w4[:, 2 * d + n, :], xc[:, CTX + GAP:XC], start=True, stop=True)
                    last.then_inc(ri_ready, 1)

        @block.scalar
        def _(act):
            link = Link(act, achain)
            act.wait_ge(lam_ready, 1)
            nc.scalar.activation(tmp[:, 1, :], tmp[:, 0, :], ACT.Exp, scale=-1.0).then_inc(lam_exp, 1)
            act.wait_ge(lam_w, 1)
            nc.scalar.activation(tmp[:, 3, :], tmp[:, 2, :], ACT.Ln).then_inc(lam_ln, 1)
            for credit in (xp_ready, gel_ready, ri_copied):
                act.sem_inc(credit, 1)
            with act.Fori(0, KD) as i:
                link.enter(i, 2)
                act.wait_ge(x_ready, i + 1)
                act.wait_ge(xc_ready, i + 1)
                src = token_row(g, 0)
                nc.scalar.activation(xp[:, LEFT:LEFT + CTX], src[:, 0:CTX], ACT.Copy)
                nc.scalar.activation(xp[:, LEFT + CTX + GAP:LEFT + CTX + GAP + LAT], src[:, CTX:T], ACT.Copy).then_inc(xp_ready, 1)
                act.wait_ge(g_ready, i + 1)
                act.wait_ge(y_ready, i + 1)
                nc.scalar.activation(gel[:, :], token_row(g, 2), ACT.Gelu_apprx_tanh).then_inc(gel_ready, 1)
                for d in range(2):
                    act.wait_ge(ri_ready, i * 2 + (d + 1))
                    link.mark(nc.scalar.activation(Rg[:, d, :], token_row(g, 4), ACT.Sigmoid, bias=cur[:, 5 + d:6 + d]))
                    nc.scalar.activation(Ig[:, d, :], token_row(g, 6), ACT.Sigmoid, bias=cur[:, 7 + d:8 + d]).then_inc(ri_copied, 1)
                link.wait()
                for d in range(2):
                    nc.scalar.activation(Th[:, d, :], Rg[:, d, :], ACT.Tanh, scale=cur[:, 11 + d:12 + d])
                    nc.scalar.activation(Ag[:, d, :], Rg[:, d, :], ACT.Exp, scale=cur[:, 9 + d:10 + d]).then_inc(decay_ready, 1)
                for d in range(2):
                    act.wait_ge(v_ready, i * 2 + (d + 1))
                    nc.scalar.activation(S2[:, d, :], V[:, d, :], ACT.Sqrt).then_inc(s_ready, 1)
                link.leave(KD)

        @block.vector
        def _(dve):
            link = Link(dve, chain)
            dve.wait_ge(par_ps, 1)
            link.mark(nc.vector.memset(xp[:, :], 0.0))
            tf = table[:, :, :].rearrange("p r j -> p (r j)")
            link(nc.vector.tensor_copy(tf[:, 0:88], g.ps[:, 7, 0:88]))
            lam = tf[:, 72:88]
            nc.vector.scalar_tensor_tensor(tmp[:, 0, :], lam, -1.0, lam, ALU.mult, ALU.max).then_inc(lam_ready, 1)
            dve.wait_ge(lam_exp, 1)
            nc.vector.tensor_scalar(tmp[:, 2, :], tmp[:, 1, :], 1.0, None, ALU.add).then_inc(lam_w, 1)
            dve.wait_ge(lam_w, 1)
            link.mark(nc.vector.tensor_scalar(tmp[:, 4, :], tmp[:, 2, :], 1.0, None, ALU.is_equal))
            link(nc.vector.tensor_scalar(tmp[:, 5, :], tmp[:, 2, :], -1.0, None, ALU.add))
            link(nc.vector.tensor_tensor(tmp[:, 5, :], tmp[:, 5, :], tmp[:, 4, :], ALU.add))
            link(nc.vector.reciprocal(tmp[:, 6, :], tmp[:, 5, :]))
            dve.wait_ge(lam_ln, 1)
            link(nc.vector.tensor_tensor(tmp[:, 6, :], tmp[:, 6, :], tmp[:, 3, :], ALU.mult))
            link(nc.vector.tensor_tensor(tmp[:, 6, :], tmp[:, 6, :], tmp[:, 4, :], ALU.add))
            link(nc.vector.tensor_tensor(tmp[:, 6, :], tmp[:, 6, :], tmp[:, 1, :], ALU.mult))
            link(nc.vector.tensor_scalar(tmp[:, 7, :], lam, -1.0, 0.0, ALU.mult, ALU.max))
            link(nc.vector.tensor_tensor(tmp[:, 7, :], tmp[:, 7, :], tmp[:, 6, :], ALU.add))
            link.mark(nc.vector.tensor_scalar(tf[:, 72:88], tmp[:, 7, :], -LRU_C, None, ALU.mult))
            link(nc.vector.tensor_scalar(tf[:, 88:104], tmp[:, 7, :], LRU_C, None, ALU.mult))
            for credit in (xc_ready, y_ready):
                dve.sem_inc(credit, 1)
            with dve.Fori(0, KD) as i:
                link.enter(i, 14)
                dve.wait_ge(xp_ready, i + 2)
                g.hold(dve)
                link(nc.vector.tensor_copy(cur[:, :], table[:, :, bass.ds(i, 1)].rearrange("p r j -> p (r j)")))
                link(nc.vector.tensor_scalar(xc[:, :], xp[:, 0:XC], cur[:, 0:1], cur[:, 4:5], ALU.mult, ALU.add))
                for j in (1, 2):
                    link(nc.vector.scalar_tensor_tensor(xc[:, :], xp[:, j:j + XC], cur[:, j:j + 1], xc[:, :], ALU.mult, ALU.add))
                nc.vector.scalar_tensor_tensor(xc[:, :], xp[:, 3:3 + XC], cur[:, 3:4], xc[:, :], ALU.mult, ALU.add).then_inc(xc_ready, 1)
                dve.wait_ge(xc_ready, i + 2)
                for d in range(2):
                    dve.wait_ge(decay_ready, i * 2 + (d + 1))
                    link(nc.vector.tensor_tensor(V[:, d, :], Ag[:, d, :], Ag[:, d, :], ALU.mult))
                    nc.vector.scalar_tensor_tensor(V[:, d, :], V[:, d, :], 1.0, Th[:, d, :], ALU.add, ALU.mult).then_inc(v_ready, 1)
                    nc.vector.tensor_tensor(Ig[:, d, 0:CTX], Ig[:, d, 0:CTX], xc[:, 0:CTX], ALU.mult)
                    link.mark(nc.vector.tensor_tensor(Ig[:, d, CTX:T], Ig[:, d, CTX:T], xc[:, CTX + GAP:XC], ALU.mult))
                for d in range(2):
                    dve.wait_ge(s_ready, i * 2 + (d + 1))
                    if d == 0:
                        link.wait()
                    link(nc.vector.tensor_tensor(Ig[:, d, :], Ig[:, d, :], S2[:, d, :], ALU.mult))
                    if d == 0:
                        link(nc.vector.tensor_tensor_scan(V[:, 0, :], Ag[:, 0, :], Ig[:, 0, :], 0.0, ALU.mult, ALU.add))
                    else:
                        link(nc.vector.tensor_tensor_scan(V[:, 1, 0:CTX][:, ::-1], Ag[:, 1, 0:CTX][:, ::-1],
                                                          Ig[:, 1, 0:CTX][:, ::-1], 0.0, ALU.mult, ALU.add))
                        link(nc.vector.tensor_tensor_scan(V[:, 1, CTX:T][:, ::-1], Ag[:, 1, CTX:T][:, ::-1],
                                                          Ig[:, 1, CTX:T][:, ::-1], V[:, 1, 0:1], ALU.mult, ALU.add))
                link(nc.vector.tensor_tensor(V[:, 0, :], V[:, 0, :], V[:, 1, :], ALU.add))
                nc.vector.tensor_tensor(ya[:, bass.ds(i, 1), :].rearrange("p a t -> p (a t)"), V[:, 0, :], gel[:, :],
                                        ALU.mult).then_inc(y_ready, 1)
                link.leave(KD)


def scan_chunks(d):
    if d == 0:
        return list(range(NCH))
    return list(range(CCH - 1, -1, -1)) + list(range(NCH - 1, CCH - 1, -1))


def stage_attention(nc, g, name, hT, gla):
    io = g.io
    heads, NV = (4, 2) if gla else (8, 1)
    DV = NV * P
    first_tile = 0 if gla else CT
    gate_scale = 1.0 / GLA_TAU if gla else 1.0
    w_in = io["ab_w_in" if gla else "c_w_in"][0].rearrange("(k p) n -> p k n", p=P)
    if gla:
        parts = [("v", AB_V, DV), ("k", AB_K, P), ("q", AB_Q, P), ("o", AB_OG, DV)]
        n_dma, n_par = 6, 8
    else:
        parts = [("v", 3 * D, DV), ("f0", D, P), ("f1", 2 * D, P), ("q", 0, P), ("o", 4 * D, DV)]
        n_dma, n_par = 5, 16
    at, width = {}, 0
    for what, _, n in parts:
        at[what] = width
        width += n
    out_segs = SEGS if gla else SEGS[1:]
    out_at = first_tile * P
    with ExitStack() as s:
        W = g.sb(s, "W", [P, KD, width])
        par = g.sb(s, "par", [16, P])
        table = g.sb(s, "table", [P, 3, 8])
        cur = g.sb(s, "cur", [P, 5])
        q = g.sb(s, "q", [P, T])
        K = g.sb(s, "K", [P, 1 if gla else 2, T])
        vt = g.sb(s, "vt", [P, TT, DV])
        OG = g.sb(s, "OG", [P, NV, T])
        Z = g.sb(s, "Z", [P, 2, T])
        B = g.sb(s, "B", [P, 2, T])
        D1 = g.sb(s, "D1", [P, 2, T])
        D2 = g.sb(s, "D2", [P, 2, T])
        Es = g.sb(s, "Es", [P, 2, 4, T])
        decay = g.sb(s, "decay", [P, 2, NCH])
        kdT = g.sb(s, "kdT", [P, 2, TT, P])
        sc = g.sb(s, "sc", [P, 2, TT, P])
        term = g.sb(s, "term", [P, P, NCH - 1])
        factor = g.sb(s, "factor", [P, 2, P, NCH - 1])
        ST = g.sb(s, "ST", [P, 2, NV, P, NCH - 1])
        start = g.sb(s, "start", [P, 2, T])
        if gla:
            walr = g.sb(s, "walr", [P, KD, 2 * GLA_RANK])
            wa2 = g.sb(s, "wa2", [2 * GLA_RANK, 2, P])
            alr = g.sb(s, "alr", [2 * GLA_RANK, T])
            Y = g.sb(s, "Y", [P, KD, T])
            zero = g.sb(s, "zero", [P, D // 2])
        else:
            Y = g.sb(s, "Y", [P, KD, LAT])
        names = ("par_loaded par_ps par_ready par_act w_loaded alr_loaded alr_ps alr_copied proj_ready proj_copied "
                 "abs_ready soft_ready d_ready e_ready qk_ready kd_ready kdT_ps kdT_copied s_ps sc_ready kv_ps "
                 "kv_half kv_taken decay_ready factor_ready state_ready o_ready o_taken sq_ready n_ready root_ready "
                 "head_done stored chain achain masks zero_made zero_stored wa2_zero")
        S = dict(zip(names.split(), g.sems(name, names)))
        block = s.enter_context(nc.Block())
        items = (["v", "z0", "z1", "k", "q", "o0", "o1"] if gla else ["v", "f0", "f1", "q", "o0"])
        NI = len(items)
        row = lambda bank: token_row(g, bank)
        flat = lambda bank: g.ps[:, bank:bank + 3, :].rearrange("p b c -> p (b c)")
        seg_of = {what: SEGS for what in items}
        if gla:
            bank_row = dict(z0=row(4), z1=row(6), k=row(4), q=row(6), o0=row(0), o1=row(2))
            turned, kv_bank = row(4), 0
            score_row = (row(6), row(6))
            out_row = (row(4), row(6))
        else:
            seg_of["q"] = seg_of["o0"] = SEGS[1:]
            bank_row = dict(f0=row(4), f1=row(6), q=g.ps[:, 3, :], o0=g.ps[:, 4, :])
            turned, kv_bank = row(0), 5
            score_row = (g.ps[:, 3, :], g.ps[:, 2, :])
            out_row = (g.ps[:, 4, :],)
        norm_row = row(2)[:, out_at:T]
        rows = lambda ap: ap.rearrange("r (j p) -> (r j) p", p=P)
        copied_at = lambda i, item: i * NI + (items.index(item) + 1)
        updates = [(d, v) for d in range(2) for v in range(NV)]
        NU = len(updates)

        @block.sync
        def _(sp):
            if gla:
                sp.dma_start(par[0:8, :], rows(io["ab_gla_ba"][0])).then_inc(S["par_loaded"], 16)
                sp.dma_start(walr[:, :, :], w_in[:, :, AB_ALR:AB_ALR + 2 * GLA_RANK]).then_inc(S["alr_loaded"], 16)
            else:
                sp.dma_start(par[0:16, :], rows(io["hgrn_lb_logits"])).then_inc(S["par_loaded"], 16)

            def load(col):
                for what, first, n in parts:
                    sp.dma_start(W[:, :, at[what]:at[what] + n], w_in[:, :, col(first, n)]).then_inc(S["w_loaded"], 16)
                if gla:
                    for d in range(2):
                        sp.dma_start(wa2[d * GLA_RANK:(d + 1) * GLA_RANK, d, :], io["ab_gla_wa2"][0, d][:, col(0, P)]).then_inc(S["w_loaded"], 16)

            def store(at):
                sp.dma_start(g.yb_rows[:, at, out_at:T], Y[:, at, :]).then_inc(S["stored"], 16)

            if gla:
                sp.wait_ge(S["wa2_zero"], 1)
            load(lambda first, n: slice(first, first + n))
            with sp.Fori(0, heads - 1) as i:
                sp.wait_ge(S["proj_ready"], i * NI + NI)
                load(lambda first, n: bass.ds(i * n + (first + n), n))
                sp.wait_ge(S["head_done"], i + 2)
                store(bass.ds(i * NV, NV))
            sp.wait_ge(S["head_done"], heads + 1)
            store(slice((heads - 1) * NV, heads * NV))
            sp.wait_ge(S["stored"], 16 * heads)

        @block.tensor
        def _(pe):
            def sums(ready):
                pe.wait_ge(S["sq_ready"], ready)
                for o, n in out_segs:
                    for v in range(NV):
                        last = nc.tensor.matmul(norm_row[:, o - out_at:o - out_at + n], g.ones[:, :], D1[:, v, o:o + n],
                                                start=(v == 0), stop=(v == NV - 1))
                last.then_inc(S["n_ready"], 1)

            pe.wait_ge(S["par_loaded"], 16)
            nc.tensor.transpose(g.ps[:, 7, 0:n_par], par[0:n_par, :], g.ident[0:n_par, 0:n_par]).then_inc(S["par_ps"], 1)
            if gla:
                pe.wait_ge(S["alr_loaded"], 16)
                project(nc, row(0)[0:2 * GLA_RANK], lambda k: walr[:, k, :], hT).then_inc(S["alr_ps"], 1)
                pe.wait_ge(S["alr_copied"], 1)
            with pe.Fori(0, heads) as i:
                def await_copy(item):
                    pe.wait_ge(S["proj_copied"], copied_at(i, item))

                pe.wait_ge(S["w_loaded"], i * (16 * n_dma) + 16 * n_dma)
                for item in items:
                    if item in ("z0", "f0"):
                        pe.wait_ge(S["o_taken"], i + 1)
                    if item in ("k", "q") and gla:
                        await_copy("z0" if item == "k" else "z1")
                    if item == "o0":
                        await_copy("v" if gla else "f0")
                    if item == ("o1" if gla else "q"):
                        pe.wait_ge(S["root_ready"], i + 1)
                    if item == "v":
                        for t in range(TT):
                            for k in range(KD):
                                last = nc.tensor.matmul(flat(0)[:, t * DV:(t + 1) * DV], hT[:, k, t * P:(t + 1) * P],
                                                        W[:, k, at["v"]:at["v"] + DV],
                                                        start=(k == 0), stop=(k == KD - 1))
                    elif item in ("z0", "z1"):
                        for o, n in SEGS:
                            last = nc.tensor.matmul(bank_row[item][:, o:o + n], wa2[:, int(item[1]), :],
                                                    alr[:, o:o + n], start=True, stop=True)
                    else:
                        c = at[item[0]] + P * int(item[1]) if item[0] == "o" else at[item]
                        last = project(nc, bank_row[item], lambda k: W[:, k, c:c + P], hT, seg_of[item])
                    last.then_inc(S["proj_ready"], 1)
                    if item == ("z1" if gla else "v"):
                        if gla:
                            await_copy("v")
                        sums(i + 1)

                def turn_keys(d):
                    pe.wait_ge(S["kd_ready"], i * 2 + (d + 1))
                    if d:
                        pe.wait_ge(S["kdT_copied"], i * 2 + 1)
                    for t in range(TT):
                        last = nc.tensor.transpose(turned[:, t * P:(t + 1) * P], Es[:, d, 3, t * P:(t + 1) * P], g.ident[:, :])
                    last.then_inc(S["kdT_ps"], 1)

                def scores(d):
                    pe.wait_ge(S["qk_ready"], i * 2 + (d + 1))
                    if d and gla:
                        pe.wait_ge(S["sc_ready"], i * 2 + 1)
                    for t in range(first_tile, TT):
                        last = nc.tensor.matmul(score_row[d][:, t * P - out_at:(t + 1) * P - out_at], Es[:, d, 1, t * P:(t + 1) * P],
                                                Es[:, d, 0, t * P:(t + 1) * P], start=True, stop=True)
                    last.then_inc(S["s_ps"], 1)

                def update(n):
                    d, v = updates[n]
                    if v == 0:
                        pe.wait_ge(S["kdT_copied"], i * 2 + (d + 1))
                    if n:
                        pe.wait_ge(S["kv_taken"], i * NU + n)
                    order, slot = scan_chunks(d)[:-1], 0
                    for every_other in (order[0::2], order[1::2]):
                        if slot:
                            pe.wait_ge(S["kv_half"], i * NU + (n + 1))
                        for c in every_other:
                            half = slice(CHUNK * (c % 2), CHUNK * (c % 2) + CHUNK)
                            last = nc.tensor.matmul(flat(kv_bank)[:, slot * P:(slot + 1) * P], kdT[half, d, c // 2, :],
                                                    vt[half, c // 2, v * P:(v + 1) * P], start=True, stop=True)
                            slot += 1
                        last.then_inc(S["kv_half" if slot < NCH - 1 else "kv_ps"], 1)

                def inside(d):
                    pe.wait_ge(S["sc_ready"], i * 2 + (2 if gla else d + 1))
                    for v in range(NV):
                        for t in range(first_tile, TT):
                            nc.tensor.matmul(out_row[v][:, t * P - out_at:(t + 1) * P - out_at], vt[:, t, v * P:(v + 1) * P],
                                             sc[:, d, t, :], start=(d == 0 and t in (0, CT)), stop=False,
                                             skip_group_check=True)

                def from_state(d, v):
                    pe.wait_ge(S["state_ready"], i * NU + (d * NV + v + 1))
                    order = scan_chunks(d)
                    for c in range(2 * first_tile, NCH):
                        if order[0] != c:
                            last = nc.tensor.matmul(out_row[v][:, c * CHUNK - out_at:(c + 1) * CHUNK - out_at],
                                                    ST[:, d, v, :, order.index(c) - 1],
                                                    Es[:, d, 2, c * CHUNK:(c + 1) * CHUNK], start=False,
                                                    stop=(d == 1 and c in (CCH - 2, NCH - 1)), skip_group_check=True)
                    return last

                await_copy("q")
                turn_keys(0)
                scores(0)
                turn_keys(1)
                if gla:
                    scores(1)
                await_copy(items[-1])
                update(0)
                if not gla:
                    scores(1)
                else:
                    pe.wait_ge(S["kdT_copied"], i * 2 + 2)
                inside(0)
                for n, (d, v) in enumerate(updates):
                    if n + 1 < NU:
                        update(n + 1)
                    if d and v == 0:
                        inside(1)
                    last = from_state(d, v)
                last.then_inc(S["o_ready"], 1)
            sums(heads + 1)

        @block.scalar
        def _(act):
            link = Link(act, S["achain"])

            def root(ready):
                act.wait_ge(S["n_ready"], ready)
                nc.scalar.activation(D2[:, 0, out_at:T], norm_row, ACT.Sqrt, scale=1.0 / DV,
                                     bias=g.eps[:, 0:1]).then_inc(S["root_ready"], 1)

            if gla:
                act.wait_ge(S["alr_ps"], 1)
                nc.scalar.activation(alr[:, :], row(0)[0:2 * GLA_RANK], ACT.Copy).then_inc(S["alr_copied"], 1)
            else:
                act.wait_ge(S["par_ready"], 1)
                nc.scalar.activation(table[:, 0, :], table[:, 2, :], ACT.Sigmoid)
                nc.scalar.activation(table[:, 1, :], table[:, 2, :], ACT.Sigmoid, scale=-1.0).then_inc(S["par_act"], 1)
            with act.Fori(0, heads) as i:
                link.enter(i, 1 if gla else 2)

                def copied(ins):
                    ins.then_inc(S["proj_copied"], 1)

                def await_item(item):
                    act.wait_ge(S["proj_ready"], copied_at(i, item))

                await_item("v")
                copied(nc.scalar.activation(vt[:, :, :].rearrange("p t v -> p (t v)"), flat(0)[:, 0:TT * DV], ACT.Copy))
                act.wait_ge(S["par_ready"], i + 2)
                if gla:
                    for d in range(2):
                        await_item(f"z{d}")
                        copied(nc.scalar.activation(Z[:, d, :], bank_row[f"z{d}"], ACT.Identity, bias=cur[:, d:d + 1]))
                root(i + 1)
                if gla:
                    act.wait_ge(S["abs_ready"], i + 1)
                    link(nc.scalar.activation(D1[:, :, :], D1[:, :, :], ACT.Exp, scale=-1.0))
                    nc.scalar.activation(D1[:, :, :], D1[:, :, :], ACT.Ln, bias=1.0).then_inc(S["soft_ready"], 1)
                    await_item("k")
                    copied(nc.scalar.activation(K[:, 0, :], bank_row["k"], ACT.Copy))
                else:
                    for d in range(2):
                        await_item(f"f{d}")
                        link(nc.scalar.activation(D1[:, d, :], bank_row[f"f{d}"], ACT.Sigmoid))
                        copied(nc.scalar.activation(K[:, d, :], bank_row[f"f{d}"], ACT.Sigmoid, scale=-1.0))
                    for d in range(2):
                        nc.scalar.activation(Z[:, d, :], D1[:, d, :], ACT.Ln, scale=cur[:, 1:2],
                                             bias=cur[:, 0:1]).then_inc(S["soft_ready"], 1)
                await_item("q")
                copied(nc.scalar.activation(q[:, out_at:T], bank_row["q"], ACT.Copy, scale=float(P) ** -0.5 if gla else 1.0))
                for d in range(2):
                    act.wait_ge(S["d_ready"], i * 2 + (d + 1))
                    nc.scalar.activation(Es[:, d, 0, out_at:T], D1[:, d, out_at:T], ACT.Exp, scale=gate_scale)
                    nc.scalar.activation(Es[:, d, 1, out_at:T], D1[:, d, out_at:T], ACT.Exp, scale=-gate_scale)
                    nc.scalar.activation(Es[:, d, 2, :], B[:, d, :], ACT.Exp, scale=gate_scale)
                    nc.scalar.activation(Es[:, d, 3, :], D2[:, d, :], ACT.Exp, scale=-gate_scale).then_inc(S["e_ready"], 1)
                act.wait_ge(S["head_done"], i + 1)
                for v in range(NV):
                    await_item(f"o{v}")
                    copied(nc.scalar.activation(OG[:, v, out_at:T], bank_row[f"o{v}"], ACT.Silu))
                for d in range(2):
                    act.wait_ge(S["kdT_ps"], i * 2 + (d + 1))
                    nc.scalar.activation(kdT[:, d, :, :].rearrange("p t k -> p (t k)"), turned, ACT.Copy)\
                        .then_inc(S["kdT_copied"], 1)
                for n in range(NU):
                    act.wait_ge(S["kv_ps"], i * NU + (n + 1))
                    if n:
                        act.wait_ge(S["state_ready"], i * NU + n)
                    for first, slots in ((0, slice(0, NCH // 2)), (1, slice(NCH // 2, NCH - 1))):
                        last = nc.scalar.activation(term[:, :, first::2].rearrange("p v n -> p n v"),
                                                    flat(kv_bank).rearrange("p (n v) -> p n v", v=P)[:, slots, :], ACT.Copy)
                    last.then_inc(S["kv_taken"], 1)
                act.wait_ge(S["o_ready"], i + 1)
                for v in range(NV):
                    last = nc.scalar.activation(D1[:, v, out_at:T], out_row[v], ACT.Square)
                last.then_inc(S["sq_ready"], 1)
                link.leave(heads)
            root(heads + 1)

        @block.gpsimd
        def _(pool):
            if gla:
                nc.gpsimd.memset(wa2[:, :, :], 0.0).then_inc(S["wa2_zero"], 1)
            nc.gpsimd.memset(D1[:, :, :], 0.0).then_inc(S["sq_ready"], 1)
            nc.gpsimd.memset(OG[:, :, :], 0.0)
            nc.gpsimd.memset(decay[:, :, :], 0.0)
            nc.gpsimd.memset(start[:, :, :], 1.0).then_inc(S["masks"], 1)
            pool.wait_ge(S["masks"], 1)
            chunks = start[:, :, :].rearrange("p d (c s) -> p d c s", s=CHUNK)
            nc.gpsimd.memset(chunks[:, 0, :, 0:1], 0.0)
            nc.gpsimd.memset(chunks[:, 1, :, CHUNK - 1:CHUNK], 0.0)
            nc.gpsimd.memset(sc[:, :, :, :], 0.0).then_inc(S["masks"], 1)
            if gla:
                sure, most, step = E, n_blocks(TT), 8
                nc.gpsimd.memset(zero[:, :], 0.0).then_inc(S["zero_made"], 1)
                pool.wait_ge(S["w_loaded"], 16 * n_dma)
                pool.wait_ge(S["zero_made"], 1)
                for b in range(sure, most, step):
                    pool.dma_start(g.y_rows[b * P:(b + step) * P, :].rearrange("(p b) (q d) -> p (b q) d", p=P, q=2),
                                   zero[:, :].unsqueeze(1).broadcast_to([P, step * 2, D // 2]))\
                        .then_inc(S["zero_stored"], 16)
            with pool.Fori(0, heads) as i:
                for d in range(2):
                    key = K[:, 0 if gla else d, :]
                    pool.wait_ge(S["e_ready"], i * 2 + (d + 1))
                    nc.gpsimd.tensor_tensor(Es[:, d, 3, :], Es[:, d, 3, :], key, ALU.mult).then_inc(S["kd_ready"], 1)
                for d in range(2):
                    ones = g.ones[:, 0:1].unsqueeze(1).broadcast_to([P, P, NCH - 1])
                    pool.wait_ge(S["decay_ready"], i * 2 + (d + 1))
                    every = decay[:, d, 0:NCH - 1].unsqueeze(1).broadcast_to([P, P, NCH - 1])
                    nc.gpsimd.tensor_tensor(factor[:, d, :, :], every, ones, ALU.mult).then_inc(S["factor_ready"], 1)
            if gla:
                pool.wait_ge(S["zero_stored"], 16 * ((n_blocks(TT) - E) // 8))

        @block.vector
        def _(dve):
            link = Link(dve, S["chain"])

            def tail(ready, head):
                dve.wait_ge(S["root_ready"], ready)
                link(nc.vector.reciprocal(D2[:, 1, out_at:T], D2[:, 0, out_at:T]))
                for v in range(NV):
                    y = Y[:, bass.ds(head * NV + v, 1), :].rearrange("p a t -> p (a t)")
                    if gla:
                        last = nc.vector.tensor_tensor(y, OG[:, v, :], D2[:, 1, :], ALU.mult)
                    else:
                        back = lambda a: a.rearrange("p (w r) -> p w r", r=GRID_H)
                        last = nc.vector.tensor_tensor(y.rearrange("p (r w) -> p w r", w=GRID_W), back(OG[:, v, CTX:T]),
                                                       back(D2[:, 1, CTX:T]), ALU.mult)
                last.then_inc(S["head_done"], 1)

            dve.wait_ge(S["par_ps"], 1)
            tf = table[:, :, :].rearrange("p r j -> p (r j)")
            if gla:
                link(nc.vector.memset(table[:, :, :], 0.0))
                nc.vector.tensor_copy(table[:, 0:2, 0:4], g.ps[:, 7, 0:8].rearrange("p (r j) -> p r j", r=2)).then_inc(S["par_ready"], 1)
                dve.wait_ge(S["par_ready"], 1)
            else:
                link(nc.vector.tensor_copy(tf[:, 0:16], g.ps[:, 7, 0:16]))
                nc.vector.tensor_tensor(table[:, 2, :], table[:, 1, :], table[:, 0, :], ALU.subtract).then_inc(S["par_ready"], 1)
                dve.wait_ge(S["par_act"], 1)
            dve.sem_inc(S["o_taken"], 1)
            dve.wait_ge(S["masks"], 2)
            g.hold(dve)
            with dve.Fori(0, heads) as i:
                link.enter(i, PER_HEAD)
                nc.vector.tensor_copy(cur[:, 0:3], table[:, :, bass.ds(i, 1)].rearrange("p r j -> p (r j)"))\
                    .then_inc(S["par_ready"], 1)
                tail(i + 1, (i + (heads - 1)) & (heads - 1))
                if gla:
                    dve.wait_ge(S["proj_copied"], copied_at(i, "z1"))
                    nc.vector.scalar_tensor_tensor(D1[:, :, :], Z[:, :, :], -1.0, Z[:, :, :], ALU.mult, ALU.max)\
                        .then_inc(S["abs_ready"], 1)
                    dve.wait_ge(S["soft_ready"], i + 1)
                    link(nc.vector.scalar_tensor_tensor(Z[:, :, :], Z[:, :, :], 0.0, D1[:, :, :], ALU.min, ALU.subtract))
                else:
                    dve.wait_ge(S["proj_copied"], copied_at(i, "f1"))
                    dve.wait_ge(S["par_ready"], i + 2)
                    link(nc.vector.tensor_scalar(K[:, :, :], K[:, :, :], cur[:, 1:2], None, ALU.mult))
                    dve.wait_ge(S["soft_ready"], i * 2 + 2)
                for d in range(2):
                    turn = (lambda a: a) if d == 0 else (lambda a: a[:, ::-1])
                    ref, end = (CHUNK // 2 - 1, CHUNK - 1) if d == 0 else (CHUNK // 2, 0)
                    link(nc.vector.tensor_tensor_scan(turn(B[:, d, :]), turn(start[:, d, :]), turn(Z[:, d, :]), 0.0, ALU.mult, ALU.add))

                    def sub(out, col, c0):
                        chunks = lambda a: a[:, c0 * CHUNK:T].rearrange("p (c s) -> p c s", s=CHUNK)
                        b3 = chunks(B[:, d, :])
                        return nc.vector.tensor_tensor(chunks(out), b3,
                                                       b3[:, :, col:col + 1].broadcast_to([P, NCH - c0, CHUNK]), ALU.subtract)
                    sub(D1[:, d, :], ref, 2 * first_tile)
                    sub(D2[:, d, :], end, 0).then_inc(S["d_ready"], 1)
                dve.wait_ge(S["proj_copied"], copied_at(i, "q"))
                for d in range(2):
                    key = K[:, 0 if gla else d, out_at:T]
                    dve.wait_ge(S["e_ready"], i * 2 + (d + 1))
                    at_end = Es[:, d, 2, :].rearrange("p (c s) -> p c s", s=CHUNK)[:, :, CHUNK - 1 if d == 0 else 0]
                    if d == 0:
                        nc.vector.tensor_scalar(decay[:, 0, 1:NCH], at_end[:, 1:NCH], 1.0, None, ALU.mult).then_inc(S["decay_ready"], 1)
                    else:
                        nc.vector.tensor_scalar(decay[:, 1, 1:CCH], at_end[:, 0:CCH - 1][:, ::-1], 1.0, None, ALU.mult)
                        nc.vector.tensor_scalar(decay[:, 1, CCH:NCH], at_end[:, CCH:NCH][:, ::-1], 1.0, None, ALU.mult)\
                            .then_inc(S["decay_ready"], 1)
                    dve.wait_ge(S["decay_ready"], i * 2 + (d + 1))
                    nc.vector.tensor_tensor(Es[:, d, 0, out_at:T], Es[:, d, 0, out_at:T], q[:, out_at:T], ALU.mult)
                    nc.vector.tensor_tensor(Es[:, d, 2, out_at:T], Es[:, d, 2, out_at:T], q[:, out_at:T], ALU.mult)
                    nc.vector.tensor_tensor(Es[:, d, 1, out_at:T], Es[:, d, 1, out_at:T], key, ALU.mult).then_inc(S["qk_ready"], 1)

                def mask_scores(d):
                    dve.wait_ge(S["s_ps"], i * 2 + (d + 1))
                    nc.vector.memset(cur[:, 3 + d:4 + d], 0.0)
                    NS = TT - first_tile
                    nc.vector.copy_predicated(sc[:, d, first_tile:TT, :], g.mask[:, d:d + 1, :].broadcast_to([P, NS, P]),
                                              score_row[d].rearrange("p (t c) -> p t c", c=P)).then_inc(S["sc_ready"], 1)

                def scan_states(n):
                    d, v = updates[n]
                    if v == 0:
                        dve.wait_ge(S["factor_ready"], i * 2 + (d + 1))
                    dve.wait_ge(S["kv_taken"], i * NU + (n + 1))
                    one_row = lambda a: a.rearrange("p v n -> p (v n)")
                    nc.vector.tensor_tensor_scan(one_row(ST[:, d, v, :, :]), one_row(factor[:, d, :, :]), one_row(term[:, :, :]),
                                                 0.0, ALU.mult, ALU.add).then_inc(S["state_ready"], 1)

                mask_scores(0)
                if gla:
                    mask_scores(1)
                scan_states(0)
                if not gla:
                    mask_scores(1)
                for n in range(1, NU):
                    scan_states(n)
                dve.wait_ge(S["proj_copied"], i * NI + NI)
                dve.wait_ge(S["sq_ready"], i + 2)
                for v in range(NV):
                    last = nc.vector.tensor_tensor(OG[:, v, out_at:T], out_row[v], OG[:, v, out_at:T], ALU.mult)
                last.then_inc(S["o_taken"], 1)
                dve.wait_ge(S["o_taken"], i + 2)
                link.leave(heads)
            tail(heads + 1, heads - 1)


PER_HEAD = 1 + 1 + 2


def stage_rows(nc, g, name, tiles, hT, X, mix=None, experts=None, residual=None, norm=None, load_x=None,
               store_x=None, store_h=False, column_major=False):
    lat_only = tiles[0] == CT
    streams = (0,) if lat_only else (0, 1)
    N = len(tiles)
    NBUF = 6
    with ExitStack() as s:
        if mix:
            w_out, sources = mix
            KY = sum(n for _, n in sources)
            first = tiles[0] * P
            Y = g.sb(s, "Yin", [P, KY, T])
            W = g.sb(s, "Wout", [P, KY, D])
        if experts:
            R, F = experts
            buf = g.sb(s, "buf", [P, NBUF, D])
            gathered = g.sems(name, " ".join(f"gathered{b}" for b in range(NBUF)))
        G, A, B = (g.sb(s, v, [P, 2, D]) if use else None for v, use in (("G", residual), ("A", norm), ("B", norm)))
        H = g.sb(s, "H", [P, 2, D]) if norm else None
        U = g.sb(s, "U", [P, D])
        sq = g.sb(s, "sq", [P, D])
        st = g.sb(s, "st", [P, 2, 4, TT])
        names = ("x_loaded vec_loaded f_ready f_squared f_var f_root x_ready x_squared x_var x_root "
                 "h_ready transposed copied chain summed")
        S = dict(zip(names.split(), g.sems(name, names)))
        if mix:
            w_loaded = g.sems(name, " ".join(f"w_loaded{c}" for c in range(KY // 2)))
            y_loaded = g.sems(name, " ".join(f"y_loaded{n}" for n in range(N)))
        h_stored = g.sems(name, "h_stored0 h_stored1")
        x_stored, = g.sems(name, "x_stored")
        block = s.enter_context(nc.Block())

        def f_tile(n, t):
            if experts:
                return F[:, t, :]
            return g.ps[:, 2 * (n % 2):2 * (n % 2) + 2, :].rearrange("p a c -> p (a c)")

        @block.sync
        def _(sp):
            if mix:
                wv = w_out.rearrange("(k p) n -> p k n", p=P)

                def load_y(n):
                    k, at = 0, slice(tiles[n] * P, (tiles[n] + 1) * P)
                    for rows, count in sources:
                        sp.dma_start(Y[:, k:k + count, at], rows[:, :, at]).then_inc(y_loaded[n], 16)
                        k += count

                load_y(0)
                for c in range(KY // 2):
                    sp.dma_start(W[:, 2 * c:2 * c + 2, :], wv[:, 2 * c:2 * c + 2, :]).then_inc(w_loaded[c], 16)
                load_y(1)
            if load_x:
                for t in tiles:
                    sp.dma_start(X[:, t, :], load_x(t)).then_inc(S["x_loaded"], 16)
            if residual:
                load_vectors(nc, g, sp, residual[0], 3 * residual[1] + 2, G, S["vec_loaded"], streams)
            if norm:
                load_vectors(nc, g, sp, norm[0], 3 * norm[1], A, S["vec_loaded"], streams)
                load_vectors(nc, g, sp, norm[0], 3 * norm[1] + 1, B, S["vec_loaded"], streams)
            if mix:
                for n in range(2, N):
                    load_y(n)
            for n, t in enumerate(tiles):
                if store_x:
                    sp.wait_ge(S["x_ready"], n + 1)
                    sp.dma_start(store_x(t), X[:, t, :]).then_inc(x_stored, 16)
                if store_h:
                    sp.wait_ge(S["h_ready"], n + 1)
                    sp.dma_start(tile_rows(g.h_rows, t), H[:, n % 2, :]).then_inc(h_stored[n % 2], 16)
            if store_x:
                sp.wait_ge(x_stored, 16 * N)
            if store_h:
                for b in range(2):
                    sp.wait_ge(h_stored[b], 16 * (N // 2))

        @block.gpsimd
        def _(pool):
            if experts:
                j = 0
                for n in range(N):
                    for k in range(TOPK):
                        if j >= NBUF:
                            pool.wait_ge(S["summed"], j - NBUF + 1)
                        c = n * TOPK + k
                        nc.gpsimd.indirect_dma_start(buf[:, j % NBUF, :], None, g.y_rows,
                                                     bass.IndirectOffsetOnAxis(ap=R.pos[:, c:c + 1], axis=0))\
                            .then_inc(gathered[j % NBUF], 16)
                        j += 1

        @block.tensor
        def _(pe):
            def turn(n):
                pe.wait_ge(S["h_ready"], n + 1)
                if n >= 2:
                    pe.wait_ge(S["copied"], n - 1)
                for k in range(KD):
                    last = nc.tensor.transpose(g.ps[:, 4 + 2 * (n % 2) + k // 4, (k % 4) * P:(k % 4 + 1) * P],
                                               H[:, n % 2, k * P:(k + 1) * P], g.ident[:, :])
                last.then_inc(S["transposed"], 1)

            for n, t in enumerate(tiles):
                if mix:
                    if n >= 2:
                        pe.wait_ge(S["x_ready"], n - 1)
                    pe.wait_ge(y_loaded[n], 16 * len(sources))
                    for k in range(KY):
                        if n == 0 and k % 2 == 0:
                            pe.wait_ge(w_loaded[k // 2], 16)
                        for o in range(2):
                            last = nc.tensor.matmul(g.ps[:, 2 * (n % 2) + o, :], Y[:, k, t * P:(t + 1) * P],
                                                    W[:, k, o * 512:(o + 1) * 512], start=(k == 0), stop=(k == KY - 1))
                    last.then_inc(S["f_ready"], 1)
                if norm and n:
                    turn(n - 1)
            if norm:
                turn(N - 1)

        @block.scalar
        def _(act):
            def norms(n, t):
                if residual:
                    act.wait_ge(S["f_var"], n + 1)
                    nc.scalar.activation(st[:, 0, 2, t:t + 1], st[:, 0, 1, t:t + 1], ACT.Sqrt).then_inc(S["f_root"], 1)
                    act.wait_ge(S["x_ready"], n + 1)
                if not norm:
                    return
                if n:
                    act.wait_ge(S["x_squared"], n)
                if residual:
                    act.wait_ge(S["f_squared"], n + 1)
                elif load_x:
                    act.wait_ge(S["x_loaded"], 16 * N)
                nc.scalar.activation(sq[:, :], X[:, t, :], ACT.Square, accum_out=st[:, 1, 0, t:t + 1]).then_inc(S["x_squared"], 1)
                act.wait_ge(S["x_var"], n + 1)
                nc.scalar.activation(st[:, 1, 2, t:t + 1], st[:, 1, 1, t:t + 1], ACT.Sqrt).then_inc(S["x_root"], 1)

            def take(n, t):
                act.wait_ge(S["transposed"], n + 1)
                src = g.ps[:, 4 + 2 * (n % 2):6 + 2 * (n % 2), :].rearrange("p a (k q) -> p (a k) q", q=P)
                if column_major and t >= CT:
                    r0 = (t - CT) * (P // GRID_W)
                    lat = hT[:, :, CTX:T].rearrange("p k (w r) -> p k r w", r=GRID_H)
                    for r in range(P // GRID_W):
                        last = nc.scalar.activation(lat[:, :, r0 + r, :], src[:, :, r * GRID_W:(r + 1) * GRID_W], ACT.Copy)
                else:
                    last = nc.scalar.activation(hT[:, :, t * P:(t + 1) * P], src, ACT.Copy)
                last.then_inc(S["copied"], 1)

            for n, t in enumerate(tiles):
                if residual:
                    if n and norm:
                        norms(n - 1, tiles[n - 1])
                    elif n:
                        norms(n - 1, tiles[n - 1])
                    act.wait_ge(S["f_ready"], n + 1)
                    if n:
                        act.wait_ge(S["f_squared"], n)
                        if norm:
                            act.wait_ge(S["x_squared"], n)
                    nc.scalar.activation(sq[:, :], f_tile(n, t), ACT.Square, accum_out=st[:, 0, 0, t:t + 1]).then_inc(S["f_squared"], 1)
                    if n and norm:
                        take(n - 1, tiles[n - 1])
                else:
                    norms(n, t)
                    if n:
                        take(n - 1, tiles[n - 1])
            if residual:
                norms(N - 1, tiles[N - 1])
            if norm:
                take(N - 1, tiles[N - 1])

        @block.vector
        def _(dve):
            link = Link(dve, S["chain"])
            done = [0]

            def combine(n, k):
                if not experts:
                    return
                t = tiles[n]
                j = n * TOPK + k
                if k:
                    dve.wait_ge(S["summed"], j)
                dve.wait_ge(gathered[j % NBUF], 16 * (j // NBUF + 1))
                nc.vector.scalar_tensor_tensor(F[:, t, :], buf[:, j % NBUF, :], R.gates[:, n, k:k + 1], F[:, t, :],
                                               ALU.mult, ALU.add).then_inc(S["summed"], 1)
                if k == TOPK - 1:
                    dve.wait_ge(S["summed"], j + 1)
                    dve.sem_inc(S["f_ready"], 1)

            def variance(n, which, waited, ready):
                t = tiles[n]
                dve.wait_ge(S[waited], n + 1)
                nc.vector.tensor_scalar(st[:, which, 1, t:t + 1], st[:, which, 0, t:t + 1], 1.0 / D, EPS, ALU.mult, ALU.add)\
                    .then_inc(S[ready], 1)

            def new_x(n):
                t = tiles[n]
                k = 1 if t < CT else 0
                dve.wait_ge(S["f_root"], n + 1)
                link(nc.vector.reciprocal(st[:, 0, 3, t:t + 1], st[:, 0, 2, t:t + 1]))
                if n == 0:
                    dve.wait_ge(S["vec_loaded"], 16 * len(streams) * (1 + 2 * bool(norm)))
                    if load_x:
                        dve.wait_ge(S["x_loaded"], 16 * N)
                link(nc.vector.scalar_tensor_tensor(U[:, :], f_tile(n, t), st[:, 0, 3, t:t + 1], G[:, k, :], ALU.mult, ALU.mult))
                nc.vector.tensor_tensor(X[:, t, :], X[:, t, :], U[:, :], ALU.add).then_inc(S["x_ready"], 1)
                dve.wait_ge(S["x_ready"], n + 1)

            def new_h(n):
                t = tiles[n]
                k = 1 if t < CT else 0
                dve.wait_ge(S["x_root"], n + 1)
                link(nc.vector.reciprocal(st[:, 1, 3, t:t + 1], st[:, 1, 2, t:t + 1]))
                if n == 0 and not residual:
                    dve.wait_ge(S["vec_loaded"], 32 * len(streams))
                if n >= 2:
                    dve.wait_ge(S["transposed"], n - 1)
                    if store_h:
                        dve.wait_ge(h_stored[n % 2], 16 * (n // 2))
                link(nc.vector.scalar_tensor_tensor(H[:, n % 2, :], X[:, t, :], st[:, 1, 3, t:t + 1], A[:, k, :], ALU.mult, ALU.mult))
                nc.vector.tensor_tensor(H[:, n % 2, :], H[:, n % 2, :], B[:, k, :], ALU.add).then_inc(S["h_ready"], 1)

            for n in range(N + 1):
                if not residual:
                    if n < N:
                        variance(n, 1, "x_squared", "x_var")
                        new_h(n)
                    continue
                if n < N:
                    for k in range(0, 3):
                        combine(n, k)
                if n:
                    variance(n - 1, 0, "f_squared", "f_var")
                if n < N:
                    combine(n, 3)
                    combine(n, 4)
                if n:
                    new_x(n - 1)
                if n < N:
                    combine(n, 5)
                    combine(n, 6)
                if n and norm:
                    variance(n - 1, 1, "x_squared", "x_var")
                if n < N:
                    combine(n, 7)
                if n and norm:
                    new_h(n - 1)


def n_blocks(n_tiles):
    return n_tiles * TOPK + E


def stage_route(nc, g, name, layer, hT, tiles, R, F):
    t0, N = tiles[0], len(tiles)
    NB = n_blocks(N)
    BIG = 1e30
    with ExitStack() as s:
        wr = g.sb(s, "wr", [P, KD, E])
        bias = g.sb(s, "bias", [P, E])
        iota_i = g.sb(s, "iota_i", [P, P], i32)
        iota = g.sb(s, "iota", [P, P])
        tok = g.sb(s, "tok", [P, TT])
        aff = g.sb(s, "aff", [P, N, E])
        biased = g.sb(s, "biased", [P, N, E])
        m8 = g.sb(s, "m8", [P, N * 8, 8])
        gs = g.sb(s, "gs", [P, N, 8])
        g8 = g.sb(s, "g8", [P, N, 8])
        gi = g.sb(s, "gi", [P, N, 8], u32)
        gif = g.sb(s, "gif", [P, N, 8])
        eq = g.sb(s, "eq", [P, N, 8, 4])
        keep = g.sb(s, "keep", [P, N, 8])
        pen = g.sb(s, "pen", [P, N, 8])
        masked = g.sb(s, "masked", [P, N, E])
        e8 = g.sb(s, "e8", [P, N, 8])
        ei = g.sb(s, "ei", [P, N, 8], u32)
        eif = g.sb(s, "eif", [P, N, 8])
        OH = g.sb(s, "OH", [P, N * 8, E])
        OX = g.sb(s, "OX", [P, N * 8, E])
        Sel = g.sb(s, "Sel", [P, N, E])
        gk = g.sb(s, "gk", [P, N, 8])
        gsum = g.sb(s, "gsum", [P, N])
        cnt = g.sb(s, "cnt", [P, E])
        nb = g.sb(s, "nb", [P, E])
        ends = g.sb(s, "ends", [P, E])
        off = g.sb(s, "off", [P, E])
        cmp_ = g.sb(s, "cmp", [P, E])
        posm = g.sb(s, "posm", [P, N, E])
        posf = g.sb(s, "posf", [P, N * 8])
        posi = g.sb(s, "posi", [P, N * 8], i32)
        slot_i = g.sb(s, "slot_i", [P, N * 8], i32)
        blk_i = g.sb(s, "blk_i", [P, N * 8], i32)
        slot = g.sb(s, "slot", [P, N * 8])
        blk = g.sb(s, "blk", [P, N * 8])
        OS = g.sb(s, "OS", [P, 2, 8, P])
        OB = g.sb(s, "OB", [P, 2, 8, NB])
        eb = g.sb(s, "eb", [P, 1])
        npf = g.sb(s, "npf", [1, 1])
        w_loaded, logits_ps, aff_ready, sel_ready, rank_ps, eb_ready, eb_ps, oh_ready, rows_used, chain, iotas = g.sems(
            name, "w_loaded logits_ps aff_ready sel_ready rank_ps eb_ready eb_ps oh_ready rows_used chain iotas")
        wgu = g.sb(s, "ws_gu", [P, KD, 2 * FF])
        wd = g.sb(s, "ws_down", [P, KF, D])
        sg, up, hm = (g.sb(s, what, [P, 2, FF]) for what in ("s_gate", "s_up", "s_hm"))
        hmT = g.sb(s, "s_hmT", [P, 2, KF, P])
        A = dict(zip("loaded gu taken h ht htc y yc".split(),
                     g.sems(name, "s_loaded s_gu s_taken s_h s_ht s_htc s_y s_yc")))
        gu_bank = lambda n: 5 if n % 2 == 0 else 0
        block = s.enter_context(nc.Block())

        @block.sync
        def _(sp):
            sp.dma_start(wr[:, :, :], g.io["moe_router"][layer].rearrange("(k p) e -> p k e", p=P)).then_inc(w_loaded, 16)
            sp.dma_start(bias[:, :], g.io["moe_bias"][layer].partition_broadcast(P)).then_inc(w_loaded, 16)
            sp.dma_start(wgu[:, :, 0:FF], g.io["moe_ws_gate"][layer].rearrange("(k p) f -> p k f", p=P)).then_inc(A["loaded"], 16)
            sp.dma_start(wgu[:, :, FF:2 * FF], g.io["moe_ws_up"][layer].rearrange("(k p) f -> p k f", p=P)).then_inc(A["loaded"], 16)
            sp.dma_start(wd[:, :, :], g.io["moe_ws_down"][layer].rearrange("(k p) n -> p k n", p=P)).then_inc(A["loaded"], 16)

        @block.gpsimd
        def _(pool):
            nc.gpsimd.iota(iota_i[:, :], pattern=[[1, P]], base=0, channel_multiplier=0).then_inc(iotas, 1)
            for n in range(N):
                pool.wait_ge(A["taken"], n + 1)
                nc.gpsimd.tensor_tensor(hm[:, n % 2, :], sg[:, n % 2, :], up[:, n % 2, :], ALU.mult).then_inc(A["h"], 1)

        @block.tensor
        def _(pe):
            def gate_up(n):
                if n == 1:
                    pe.wait_ge(aff_ready, 1)
                if n >= 2:
                    pe.wait_ge(A["htc"], n - 1)
                t = tiles[n]
                for k in range(KD):
                    last = nc.tensor.matmul(g.ps[:, gu_bank(n), :], hT[:, k, t * P:(t + 1) * P], wgu[:, k, :],
                                            start=(k == 0), stop=(k == KD - 1))
                last.then_inc(A["gu"], 1)

            def shared(n):
                if n + 1 < N:
                    gate_up(n + 1)
                pe.wait_ge(A["h"], n + 1)
                for f in range(KF):
                    last = nc.tensor.transpose(g.ps[:, gu_bank(n), f * P:(f + 1) * P], hm[:, n % 2, f * P:(f + 1) * P], g.ident[:, :])
                last.then_inc(A["ht"], 1)
                if n:
                    pe.wait_ge(A["yc"], n)
                pe.wait_ge(A["htc"], n + 1)
                for o in range(2):
                    for f in range(KF):
                        last = nc.tensor.matmul(g.ps[:, 6 + o, :], hmT[:, n % 2, f, :], wd[:, f, o * 512:(o + 1) * 512],
                                                start=(f == 0), stop=(f == KF - 1))
                last.then_inc(A["y"], 1)

            pe.wait_ge(w_loaded, 32)
            for n, t in enumerate(tiles):
                for k in range(KD):
                    last = nc.tensor.matmul(g.ps[:, 0, n * E:(n + 1) * E], hT[:, k, t * P:(t + 1) * P], wr[:, k, :],
                                            start=(k == 0), stop=(k == KD - 1))
            last.then_inc(logits_ps, 1)
            pe.wait_ge(A["loaded"], 48)
            gate_up(0)
            shared(0)
            pe.wait_ge(sel_ready, 1)
            for n in range(N):
                for m in range(n + 1):
                    nc.tensor.matmul(g.ps[:, 1, n * E:(n + 1) * E], (g.before if m == n else g.ones)[:, :], Sel[:, m, :],
                                     start=(m == 0), stop=(m == n))
            for m in range(N):
                last = nc.tensor.matmul(g.ps[:, 2, 0:E], g.ones[:, :], Sel[:, m, :], start=(m == 0), stop=(m == N - 1))
            last.then_inc(rank_ps, 1)
            shared(1)
            pe.wait_ge(eb_ready, 1)
            nc.tensor.matmul(g.ps[0:1, 3, 0:P], eb[:, :], g.ident[:, :], start=True, stop=True).then_inc(eb_ps, 1)
            for n in range(N):
                pe.wait_ge(oh_ready, n + 1)
                for k in range(TOPK):
                    last = nc.tensor.matmul(g.ps[:, 4, 0:NB], OS[:, n % 2, k, :], OB[:, n % 2, k, :],
                                            start=(n == 0 and k == 0), stop=(n == N - 1 and k == TOPK - 1))
                last.then_inc(rows_used, 1)
                if n >= 2:
                    shared(n)

        @block.scalar
        def _(act):
            def take(n):
                act.wait_ge(A["gu"], n + 1)
                nc.scalar.activation(sg[:, n % 2, :], g.ps[:, gu_bank(n), 0:FF], ACT.Silu)
                nc.scalar.activation(up[:, n % 2, :], g.ps[:, gu_bank(n), FF:2 * FF], ACT.Copy).then_inc(A["taken"], 1)

            act.wait_ge(logits_ps, 1)
            nc.scalar.activation(aff[:, :, :].rearrange("p n e -> p (n e)"), g.ps[:, 0, 0:N * E], ACT.Sigmoid).then_inc(aff_ready, 1)
            take(0)
            for n, t in enumerate(tiles):
                if n + 1 < N:
                    take(n + 1)
                act.wait_ge(A["ht"], n + 1)
                nc.scalar.activation(hmT[:, n % 2, :, :].rearrange("p f r -> p (f r)"), g.ps[:, gu_bank(n), 0:FF], ACT.Copy)\
                    .then_inc(A["htc"], 1)
                act.wait_ge(A["y"], n + 1)
                nc.scalar.activation(F[:, t, :], g.ps[:, 6:8, :].rearrange("p a c -> p (a c)"), ACT.Copy).then_inc(A["yc"], 1)

        @block.vector
        def _(dve):
            v = nc.vector
            link = Link(dve, chain)
            dve.wait_ge(iotas, 1)
            link.mark(v.tensor_copy(iota[:, :], iota_i[:, :]))
            link.mark(v.tensor_copy(tok[:, :], g.token_id[:, :]))
            dve.wait_ge(w_loaded, 32)
            dve.wait_ge(aff_ready, 1)
            link(v.tensor_tensor(biased[:, :, :], aff[:, :, :], bias[:, None, :].broadcast_to([P, N, E]), ALU.add))
            groups = biased[:, :, :].rearrange("p n (g e) -> p (n g) e", e=8)
            for j in range(N * 8):
                last = v.max(m8[:, j, :], groups[:, j, :])
            link(last)
            m8g = m8[:, :, :].rearrange("p (n g) e -> p n g e", g=8)
            link(v.tensor_tensor(gs[:, :, :], m8g[:, :, :, 0], m8g[:, :, :, 1], ALU.add))
            for n in range(N):
                last = v.max(g8[:, n, :], gs[:, n, :])
            link(last)
            for n in range(N):
                last = v.max_index(gi[:, n, :], g8[:, n, :], gs[:, n, :])
            link(last)
            link(v.tensor_copy(gif[:, :, :], gi[:, :, :]))
            for n in range(N):
                last = v.tensor_tensor(eq[:, n, :, :], iota[:, 0:8].unsqueeze(2).broadcast_to([P, 8, 4]),
                                       gif[:, n, 0:4].unsqueeze(1).broadcast_to([P, 8, 4]), ALU.is_equal)
            link(last)
            link(v.tensor_reduce(keep[:, :, :], eq[:, :, :, :], AX.X, ALU.add))
            link(v.tensor_scalar(pen[:, :, :], keep[:, :, :], -1.0, BIG, ALU.add, ALU.mult))
            over = lambda a: a[:, :, :].rearrange("p n g -> p (n g)").unsqueeze(2).broadcast_to([P, N * 8, 8])
            mg = masked[:, :, :].rearrange("p n (g e) -> p (n g) e", e=8)
            link(v.tensor_tensor(mg, groups, over(keep), ALU.mult))
            link(v.tensor_tensor(mg, mg, over(pen), ALU.add))
            for n in range(N):
                last = v.max(e8[:, n, :], masked[:, n, :])
            link(last)
            for n in range(N):
                last = v.max_index(ei[:, n, :], e8[:, n, :], masked[:, n, :])
            link(last)
            link(v.tensor_copy(eif[:, :, :], ei[:, :, :]))
            link(v.tensor_tensor(OH[:, :, :], iota[:, 0:E].unsqueeze(1).broadcast_to([P, N * 8, E]),
                                 eif[:, :, :].rearrange("p n k -> p (n k)").unsqueeze(2).broadcast_to([P, N * 8, E]), ALU.is_equal))
            v.tensor_reduce(Sel[:, :, :], OH[:, :, :].rearrange("p (n k) e -> p n e k", k=8), AX.X, ALU.add).then_inc(sel_ready, 1)
            for n in range(N):
                last = v.tensor_tensor(OX[:, n * 8:(n + 1) * 8, :], OH[:, n * 8:(n + 1) * 8, :],
                                       aff[:, n, :].unsqueeze(1).broadcast_to([P, 8, E]), ALU.mult)
            link(last)
            link(v.tensor_reduce(gk[:, :, :].rearrange("p n k -> p (n k)"), OX[:, :, :], AX.X, ALU.add))
            link(v.tensor_reduce(gsum[:, :], gk[:, :, :], AX.X, ALU.add))
            link(v.reciprocal(gsum[:, :], gsum[:, :]))
            for n in range(N):
                last = v.tensor_scalar(R.gates[:, n, :], gk[:, n, :], gsum[:, n:n + 1], ROUTED_SCALE, ALU.mult, ALU.mult)
            link(last)
            dve.wait_ge(rank_ps, 1)
            link.mark(v.memset(nb[:, :], 1.0))
            link.mark(v.memset(OS[:, 0, 0, 0:E], 1.0))
            link(v.tensor_copy(cnt[:, :], g.ps[:, 2, 0:E]))
            for j in range(1, TT):
                link(v.scalar_tensor_tensor(nb[:, :], cnt[:, :], float(P * j), nb[:, :], ALU.is_gt, ALU.add))
            link(v.tensor_tensor_scan(ends[:, :], OS[:, 0, 0, 0:E], nb[:, :], 0.0, ALU.mult, ALU.add))
            link(v.tensor_tensor(off[:, :], ends[:, :], nb[:, :], ALU.subtract))
            link(v.tensor_scalar(cmp_[:, :], ends[:, :], tok[:, 0:1], None, ALU.is_le))
            link(v.tensor_reduce(eb[:, :], cmp_[:, :], AX.X, ALU.add))
            v.tensor_scalar(eb[:, :], eb[:, :], float(E - 1), None, ALU.min).then_inc(eb_ready, 1)
            link(v.tensor_scalar(npf[:, :], ends[0:1, E - 1:E], 0.5, 0.25, ALU.mult, ALU.add))
            link(v.tensor_copy(R.pairs[:, :], npf[:, :]))
            link(v.tensor_copy(R.ends[:, :], ends[0:1, :]))
            for n in range(N):
                last = v.scalar_tensor_tensor(posm[:, n, :], off[:, :], float(P), g.ps[:, 1, n * E:(n + 1) * E], ALU.mult, ALU.add)
            link(last)
            for n in range(N):
                last = v.tensor_tensor(OX[:, n * 8:(n + 1) * 8, :], OH[:, n * 8:(n + 1) * 8, :],
                                       posm[:, n, :].unsqueeze(1).broadcast_to([P, 8, E]), ALU.mult)
            link(last)
            link(v.tensor_reduce(posf[:, :], OX[:, :, :], AX.X, ALU.add))
            link.mark(v.tensor_copy(posi[:, :], posf[:, :]))
            link(v.tensor_copy(R.pos[:, 0:N * 8], posf[:, :]))
            link.mark(v.tensor_scalar(slot_i[:, :], posi[:, :], P - 1, None, ALU.bitwise_and))
            link(v.tensor_scalar(blk_i[:, :], posi[:, :], 7, None, ALU.logical_shift_right))
            link.mark(v.tensor_copy(slot[:, :], slot_i[:, :]))
            link(v.tensor_copy(blk[:, :], blk_i[:, :]))
            for n, t in enumerate(tiles):
                if n >= 2:
                    dve.wait_ge(rows_used, n - 1)
                b = n % 2
                v.tensor_tensor(OS[:, b, :, :], iota[:, :].unsqueeze(1).broadcast_to([P, 8, P]),
                                slot[:, n * 8:(n + 1) * 8].unsqueeze(2).broadcast_to([P, 8, P]), ALU.is_equal)
                link(v.tensor_tensor(OB[:, b, :, :], iota[:, 0:NB].unsqueeze(1).broadcast_to([P, 8, NB]),
                                     blk[:, n * 8:(n + 1) * 8].unsqueeze(2).broadcast_to([P, 8, NB]), ALU.is_equal))
                v.tensor_scalar(OB[:, b, :, :], OB[:, b, :, :], tok[:, t:t + 1], None, ALU.mult).then_inc(oh_ready, 1)
            dve.wait_ge(eb_ps, 1)
            v.tensor_copy(R.block_expert[:, :], g.ps[0:1, 3, 0:P])
            dve.wait_ge(rows_used, N)
            link(v.memset(R.rows[:, :], 0))
            link(v.tensor_copy(R.rows[:, 0:NB], g.ps[:, 4, 0:NB]))


RING = 4


def stage_experts(nc, g, name, layer, tiles, R):
    N = len(tiles)
    NB = n_blocks(N)
    io = g.io
    with ExitStack() as s:
        wgu = g.sb(s, "wgu", [P, RING, KD, 2 * FF])
        wd = g.sb(s, "wd", [P, RING, KF, D])
        idx = [g.sb(s, f"idx{b}", [P, 1], u32) for b in range(2)]
        xg = [g.sb(s, f"xg{b}", [P, D]) for b in range(2)]
        xT = [g.sb(s, f"xT{b}", [P, KD, P]) for b in range(2)]
        sg = [g.sb(s, f"sg{b}", [P, FF]) for b in range(2)]
        hm = [g.sb(s, f"hm{b}", [P, FF]) for b in range(2)]
        hmT = [g.sb(s, f"hmT{b}", [P, KF, P]) for b in range(2)]
        y = [g.sb(s, f"y{b}", [P, D]) for b in range(2)]
        tiny = g.sb(s, "tiny", [P, 3])
        tiny_made, = g.sems(name, "tiny_made")
        names = "gu_ps silu_done h_ready ht_ps ht_copied y_ps y_low y_high"
        M = dict(zip(names.split(), g.sems(name, names)))
        TW = {n: g.sems(name, f"{n}0 {n}1") for n in "idx_ready gathered xT_ps xT_copied y_stored passed".split()}
        w_loaded = g.sems(name, " ".join(f"w_loaded{r}" for r in range(RING)))
        block = s.enter_context(nc.Block())

        def gate_up(b, lhsT, rhs):
            for k in range(KD):
                last = nc.tensor.matmul(g.ps[:, 4 + b, :], lhsT(k), rhs(k), start=(k == 0), stop=(k == KD - 1))
            return last

        def turn_h(b):
            for f in range(KF):
                last = nc.tensor.transpose(g.ps[:, 4 + b, f * P:(f + 1) * P], hm[b][:, f * P:(f + 1) * P], g.ident[:, :])
            return last

        def down(b, bank, rhs):
            for o in range(2):
                for f in range(KF):
                    last = nc.tensor.matmul(g.ps[:, bank + o, :], hmT[b][:, f, :], rhs(f, o),
                                            start=(f == 0), stop=(f == KF - 1))
            return last

        @block.sync
        def _(sp):
            def load(e, r):
                sp.dma_start(wgu[:, r, :, 0:FF], io["moe_w_gate"][layer, e].rearrange("e (p k) f -> p (e k) f", k=KD)).then_inc(w_loaded[r], 16)
                sp.dma_start(wgu[:, r, :, FF:2 * FF], io["moe_w_up"][layer, e].rearrange("e (p k) f -> p (e k) f", k=KD)).then_inc(w_loaded[r], 16)
                sp.dma_start(wd[:, r, :, :], io["moe_w_down"][layer, e].rearrange("e (k p) n -> p (e k) n", p=P)).then_inc(w_loaded[r], 16)

            for r in range(RING):
                load(slice(r, r + 1), r)
            with sp.Fori(0, E // RING - 1) as i:
                for r in range(RING):
                    done = sp.value_load(R.ends[0:1, bass.ds(i * RING + r, 1)], min_val=1, max_val=NB)
                    sp.wait_ge(M["y_ps"], done)
                    load(bass.ds(i * RING + (RING + r), 1), r)

        @block.gpsimd
        def _(pool):
            def gather(b):
                nc.gpsimd.indirect_dma_start(xg[b][:, :], None, g.h_rows, bass.IndirectOffsetOnAxis(ap=idx[b][:, 0:1], axis=0))\
                    .then_inc(TW["gathered"][b], 16)

            nc.gpsimd.memset(tiny[:, :], 0.0).then_inc(tiny_made, 1)
            pool.wait_ge(tiny_made, 1)
            for b in range(2):
                pool.sem_inc(TW["passed"][b], 1)
                pool.wait_ge(TW["idx_ready"][b], 1)
                gather(b)
            pairs = pool.value_load(R.pairs[0:1, 0:1], min_val=1, max_val=NB // 2)
            with pool.Fori(0, NB // 2) as i:
                with pool.If(i < pairs):
                    for b in range(2):
                        pool.wait_ge(TW["xT_ps"][b], i + 1)
                        pool.wait_ge(TW["idx_ready"][b], i + 2)
                        pool.wait_ge(TW["passed"][b], i + 1)
                        nc.gpsimd.tensor_tensor(tiny[:, 1 + b:2 + b], tiny[:, 0:1], tiny[:, 0:1], ALU.add).then_inc(TW["passed"][b], 1)
                        gather(b)

        @block.tensor
        def _(pe):
            def turn_x(b):
                cols = xg[b][:, :].rearrange("p (q k) -> p k q", k=KD)
                for k in range(KD):
                    last = nc.tensor.transpose(g.ps[:, 2 * b + k // 4, (k % 4) * P:(k % 4 + 1) * P], cols[:, k, :], g.ident[:, :])
                last.then_inc(TW["xT_ps"][b], 1)

            for b in range(2):
                pe.wait_ge(TW["gathered"][b], 16)
                turn_x(b)
            pairs = pe.value_load(R.pairs[0:1, 0:1], min_val=1, max_val=NB // 2)
            with pe.Fori(0, NB // 2) as i:
                with pe.If(i < pairs):
                    slot = []
                    for b in range(2):
                        e = pe.value_load(R.block_expert[0:1, bass.ds(i * 2 + b, 1)], min_val=0, max_val=E - 1)
                        slot.append(pe.snap(e & (RING - 1)))
                        pe.wait_ge(TW["xT_copied"][b], i + 1)
                        for r in range(RING):
                            pe.wait_ge(w_loaded[r], ((e + (RING - r)) >> 2) * 48 + 48)
                        gate_up(b, lambda k: xT[b][:, k, :],
                                lambda k: wgu[:, bass.ds(slot[b], 1), k, :].rearrange("p a n -> p (a n)")).then_inc(M["gu_ps"], 1)
                    for b in range(2):
                        pe.wait_ge(M["h_ready"], i * 2 + (b + 1))
                        turn_h(b).then_inc(M["ht_ps"], 1)
                        pe.wait_ge(TW["gathered"][b], i * 16 + 32)
                        if b == 0:
                            pe.wait_ge(M["y_low"], i * 2 + 1)
                            pe.wait_ge(M["y_high"], i * 2 + 1)
                        turn_x(b)
                    for b in range(2):
                        pe.wait_ge(M["ht_copied"], i * 2 + (b + 1))
                        if b == 1:
                            pe.wait_ge(TW["xT_copied"][0], i + 2)
                        down(b, 6 if b == 0 else 0, lambda f, o: wd[:, bass.ds(slot[b], 1), f, o * 512:(o + 1) * 512].rearrange("p a n -> p (a n)"))\
                            .then_inc(M["y_ps"], 1)

        @block.scalar
        def _(act):
            def silu(b, waited, at, done):
                act.wait_ge(waited, at)
                nc.scalar.activation(sg[b][:, :], g.ps[:, 4 + b, 0:FF], ACT.Silu).then_inc(done, 1)

            def take_ht(b, waited, at, done):
                act.wait_ge(waited, at)
                nc.scalar.activation(hmT[b][:, :, :].rearrange("p f r -> p (f r)"), g.ps[:, 4 + b, 0:FF], ACT.Copy).then_inc(done, 1)

            def take_x(b, at):
                act.wait_ge(TW["xT_ps"][b], at)
                nc.scalar.activation(xT[b][:, :, :].rearrange("p k r -> p (k r)"),
                                     g.ps[:, 2 * b:2 * b + 2, :].rearrange("p a c -> p (a c)"), ACT.Copy)\
                    .then_inc(TW["xT_copied"][b], 1)

            for r in range(RING):
                act.sem_inc(w_loaded[r], 48)
            act.sem_inc(M["y_low"], 1)
            for b in range(2):
                act.sem_inc(TW["y_stored"][b], 16)
                take_x(b, 1)
            pairs = act.value_load(R.pairs[0:1, 0:1], min_val=1, max_val=NB // 2)
            with act.Fori(0, NB // 2) as i:
                with act.If(i < pairs):
                    for b in range(2):
                        silu(b, M["gu_ps"], i * 2 + (b + 1), M["silu_done"])
                    for b in range(2):
                        take_ht(b, M["ht_ps"], i * 2 + (b + 1), M["ht_copied"])
                        take_x(b, i + 2)
                    for b in range(2):
                        act.wait_ge(M["y_ps"], i * 2 + (b + 1))
                        act.wait_ge(TW["y_stored"][b], i * 16 + 16)
                        nc.scalar.activation(y[b][:, 0:512], g.ps[:, 6 if b == 0 else 0, :], ACT.Copy).then_inc(M["y_low"], 1)
                        act.wait_ge(M["y_low"], i * 2 + (b + 2))
                        act.wait_ge(M["y_high"], i * 2 + (b + 2))
                        act.dma_start(g.y_rows[bass.ds(i * (2 * P) + b * P, P), :], y[b][:, :]).then_inc(TW["y_stored"][b], 16)
            for b in range(2):
                act.wait_ge(TW["y_stored"][b], pairs * 16 + 16)
                nc.scalar.activation(y[b][:, 0:1], y[b][:, 0:1], ACT.Copy)

        @block.vector
        def _(dve):
            def multiply(b, waited, at, done):
                dve.wait_ge(waited, at)
                nc.vector.tensor_tensor(hm[b][:, :], sg[b][:, :], g.ps[:, 4 + b, FF:2 * FF], ALU.mult).then_inc(done, 1)

            for b in range(2):
                nc.vector.tensor_copy(idx[b][:, :], R.rows[:, b:b + 1]).then_inc(TW["idx_ready"][b], 1)
            dve.sem_inc(M["y_high"], 1)
            for b in range(2):
                dve.wait_ge(TW["gathered"][b], 16)
                nc.vector.tensor_copy(idx[b][:, :], R.rows[:, 2 + b:3 + b]).then_inc(TW["idx_ready"][b], 1)
            pairs = dve.value_load(R.pairs[0:1, 0:1], min_val=1, max_val=NB // 2)
            with dve.Fori(0, NB // 2) as i:
                with dve.If(i < pairs):
                    for b in range(2):
                        multiply(b, M["silu_done"], i * 2 + (b + 1), M["h_ready"])
                    for b in range(2):
                        dve.wait_ge(TW["gathered"][b], i * 16 + 32)
                        nc.vector.tensor_copy(idx[b][:, :], R.rows[:, bass.ds(i * 2 + (4 + b), 1)]).then_inc(TW["idx_ready"][b], 1)
                    for b in range(2):
                        dve.wait_ge(M["y_ps"], i * 2 + (b + 1))
                        dve.wait_ge(TW["y_stored"][b], i * 16 + 16)
                        nc.vector.tensor_scalar(y[b][:, 512:D], g.ps[:, 7 if b == 0 else 1, :], 1.0, None, ALU.mult)\
                            .then_inc(M["y_high"], 1)


def program(nc, io):
    g = Core()
    g.io = io
    g.names = {}
    outer = ExitStack()
    with outer:
        def sb(stack, name, shape, dt=fp32):
            g.names[name] = g.names.get(name, 0) + 1
            return stack.enter_context(nc.sbuf_tensor(f"{name}_{g.names[name]}", shape, dt))

        def sem(name):
            return nc.alloc_semaphore(name)

        def recycle():
            nc.clear_and_free_semaphores(nc.allocated_since(g.kept))
            nc.all_engine_barrier()

        g.sb, g.sem = sb, sem
        g.sems = lambda stage, names: [sem(f"{stage}_{n}") for n in names.split()]
        g.mod_vecs = nc.dram_tensor("mod_vecs", [2, 2, 6, D], fp32).ap()
        g.h_rows = nc.dram_tensor("h_rows", [T, D], fp32).ap()
        g.x_rows = nc.dram_tensor("x_rows", [T, D], fp32).ap()
        g.ps = outer.enter_context(nc.psum_tensor("ps", [P, 8, 512], fp32))
        g.ident = sb(outer, "ident", [P, P])
        g.ones = sb(outer, "ones", [P, P])
        g.before = sb(outer, "before", [P, P])
        g.token_id = sb(outer, "token_id", [P, TT], i32)
        g.mask = sb(outer, "mask", [P, 2, P], i32)
        g.eps = sb(outer, "eps", [P, 1])
        hT = sb(outer, "hT", [P, KD, T])
        g.y_rows = nc.dram_tensor("y_rows", [n_blocks(TT) * P, D], fp32).ap()
        g.ya_rows = nc.dram_tensor("ya_rows", [P, KD, T], fp32).ap()
        g.yb_rows = nc.dram_tensor("yb_rows", [P, KD, T], fp32).ap()
        settled = sem("settled")

        def hold(eng, n=1):
            eng.wait_ge(settled, n)
        g.hold = hold
        g.settled = settled

        stage_constants(nc, g)
        g.kept = nc.snapshot_sems()
        x0 = lambda t: tile_rows(io["ctx"][0], t) if t < CT else tile_rows(io["x"][0], t - CT)
        x_row = lambda t: tile_rows(g.x_rows, t)
        out_row = lambda t: tile_rows(io["out"][0], t - CT)
        every, latent = list(range(TT)), list(range(CT, TT))

        def moe(layer, X, tiles, **tail):
            name = f"moe{layer}"
            with ExitStack() as s:
                R = Core()
                R.gates = sb(s, "gates", [P, TT, TOPK])
                R.pos = sb(s, "pos", [P, TT * TOPK], u32)
                R.rows = sb(s, "rows", [P, n_blocks(TT) + 4], u32)
                R.ends = sb(s, "ends", [1, E], i32)
                R.block_expert = sb(s, "block_expert", [1, P], i32)
                R.pairs = sb(s, "pairs", [1, 1], i32)
                F = sb(s, "F", [P, TT, D])
                recycle()
                stage_route(nc, g, name + "r", layer, hT, tiles, R, F)
                stage_experts(nc, g, name + "e", layer, tiles, R)
                recycle()
                stage_rows(nc, g, name + "x", tiles, hT, X, experts=(R, F), residual=(layer, 1), **tail)

        stage_modulation(nc, g, hT, x0)
        stage_lru(nc, g, hT)
        stage_attention(nc, g, "gla", hT, True)
        with ExitStack() as s:
            X = sb(s, "X", [P, TT, D])
            stage_rows(nc, g, "r0", every, hT, X, mix=(io["ab_w_out"][0], ((g.ya_rows, KD), (g.yb_rows, KD))),
                       residual=(0, 0), norm=(0, 1), load_x=x0, store_h=True)
            moe(0, X, every, norm=(1, 0), store_x=x_row, column_major=True)
        stage_attention(nc, g, "hgrn", hT, False)
        with ExitStack() as s:
            X = sb(s, "X", [P, TT, D])
            stage_rows(nc, g, "r1", latent, hT, X, mix=(io["c_w_out"][0], ((g.yb_rows, KD),)),
                       residual=(1, 0), norm=(1, 1), load_x=x_row, store_h=True)
            moe(1, X, latent, store_x=out_row)



_INPUTS = ["x", "c", "ctx", "c_ctx", "mod_w", "mod_b", "pre_gain", "post_gain", "ab_w_in", "ab_conv_w", "ab_conv_b",
           "ab_lru_wa", "ab_lru_ba", "ab_lru_wi", "ab_lru_bi", "ab_lru_lambda", "ab_gla_wa2", "ab_gla_ba", "ab_w_out",
           "c_w_in", "hgrn_lb_logits", "c_w_out", "moe_router", "moe_bias", "moe_w_gate", "moe_w_up", "moe_w_down",
           "moe_ws_gate", "moe_ws_up", "moe_ws_down"]


def kernel(**inputs):
    import numpy as np
    import concourse.bacc as bacc
    from concourse.bass_utils import run_bass_kernel_spmd

    nc = bacc.Bacc("TRN2", target_bir_lowering=False, num_devices=1)
    arrays, io = {}, {}
    for name in _INPUTS:
        a = np.ascontiguousarray(inputs[name])
        arrays[f"in_{name}"] = a
        io[name] = nc.dram_tensor(f"in_{name}", a.shape, mybir.dt.from_np(a.dtype), kind="ExternalInput").ap()
    io["out"] = nc.dram_tensor("out_0", (1, LAT, D), fp32, kind="ExternalOutput").ap()
    program(nc, io)
    r = run_bass_kernel_spmd(nc, [arrays], core_ids=[0])
    return r.results[0]["out_0"]
```

```python
import concourse.bass as bass
from concourse import mybir
from contextlib import ExitStack

fp32 = mybir.dt.float32
i32 = mybir.dt.int32
u32 = mybir.dt.uint32
ALU = mybir.AluOpType
ACT = mybir.ActivationFunctionType
AX = mybir.AxisListType

P = 128
D = 1024
KD = D // P
CTX, LAT = 256, 512
T = CTX + LAT
TT = T // P
CT = CTX // P
EPS = 1e-6
GRID_W = 64
GRID_H = LAT // GRID_W
CHUNK = 64
NCH = T // CHUNK
CCH = CTX // CHUNK
E = 64
TOPK = 8
FF = 256
KF = FF // P
ROUTED_SCALE = 2.5
LRU_C = 8.0
GLA_TAU = 16.0
GLA_RANK = 16


class Link:

    def __init__(self, eng, sem):
        self.eng, self.sem, self.n, self.trip, self.per = eng, sem, 0, None, 0

    def value(self):
        return self.n if self.trip is None else self.trip * self.per + self.n

    def mark(self, ins):
        ins.then_inc(self.sem, 1)
        self.n += 1

    def wait(self):
        self.eng.wait_ge(self.sem, self.value())

    def __call__(self, ins):
        self.mark(ins)
        self.wait()

    def enter(self, trip, per):
        self.trip, self.per, self.before = trip, per, self.n

    def leave(self, trips):
        assert self.n - self.before == self.per, (self.n - self.before, self.per)
        self.n = self.before + trips * self.per
        self.trip = None


class Core:
    pass


def stage_constants(nc, g):
    with nc.Block() as block:
        made = g.sem("const_made")

        @block.gpsimd
        def _(pool):
            link = Link(pool, made)
            pool.sem_inc(g.settled, 4)
            link.mark(nc.gpsimd.memset(g.ones[:, :], 1.0))
            link.mark(nc.gpsimd.memset(g.eps[:, :], EPS))
            link.mark(nc.gpsimd.memset(g.ident[:, :], 0.0))
            link.mark(nc.gpsimd.memset(g.before[:, :], 0.0))
            link.mark(nc.gpsimd.iota(g.token_id[:, :], pattern=[[P, TT]], base=0, channel_multiplier=1))
            link(nc.gpsimd.memset(g.mask[:, :, :], 0.0))
            link.mark(nc.gpsimd.affine_select(out=g.ident[:, :], in_=g.ident[:, :], compare_op=ALU.not_equal,
                                              fill=1.0, base=0, pattern=[[-1, P]], channel_multiplier=1))
            link.mark(nc.gpsimd.affine_select(out=g.before[:, :], in_=g.before[:, :], compare_op=ALU.is_ge,
                                              fill=1.0, base=0, pattern=[[-1, P]], channel_multiplier=1))
            for h in range(2):
                rows = slice(h * CHUNK, (h + 1) * CHUNK)
                link.mark(nc.gpsimd.affine_select(out=g.mask[rows, 0, rows], in_=g.mask[rows, 0, rows],
                                                  compare_op=ALU.is_gt, fill=1.0, base=0, pattern=[[-1, CHUNK]],
                                                  channel_multiplier=1))
                link(nc.gpsimd.affine_select(out=g.mask[rows, 1, rows], in_=g.mask[rows, 1, rows],
                                             compare_op=ALU.is_gt, fill=1.0, base=0, pattern=[[1, CHUNK]],
                                             channel_multiplier=-1))


GROUPS = 4


class Modulation:

    def __init__(self, nc, g, s, name, layer, width, banks):
        self.nc, self.g, self.layer, self.width, self.banks = nc, g, layer, width, banks
        self.slices = 6 * D // width
        self.w = [g.sb(s, f"modw{b}", [P, KD, width]) for b in range(2)]
        self.m = g.sb(s, "m", [2, 6, D])
        self.gain = g.sb(s, "gain", [2, 4, D])
        self.loaded, self.used, self.taken = (g.sems(name, f"{v}0 {v}1") for v in ("mod_w_loaded", "mod_w_used", "mod_taken"))
        self.par_loaded, self.chain = g.sems(name, "mod_par_loaded mod_chain")
        self.cols = g.io["mod_w"][layer].rearrange("(k p) n -> p k n", p=P)

    def load_parameters(self, eng):
        io, layer = self.g.io, self.layer
        for dst, src in ((self.m[:, :, :], io["mod_b"][layer]),
                         (self.gain[:, 0:2, :], io["pre_gain"][layer].rearrange("r d -> (r d)")),
                         (self.gain[:, 2:4, :], io["post_gain"][layer].rearrange("r d -> (r d)"))):
            eng.dma_start(dst.rearrange("s r d -> s (r d)"), src.partition_broadcast(2)).then_inc(self.par_loaded, 16)

    def load_first(self, sp):
        for b in range(2):
            sp.dma_start(self.w[b][:, :, :], self.cols[:, :, b * self.width:(b + 1) * self.width]).then_inc(self.loaded[b], 16)

    def load_next(self, sp, i):
        for b in range(2):
            sp.wait_ge(self.used[b], i + 1)
            sp.dma_start(self.w[b][:, :, :], self.cols[:, :, bass.ds(i * (2 * self.width) + (2 + b) * self.width, self.width)])\
                .then_inc(self.loaded[b], 16)

    def multiply(self, pe, i):
        for b in range(2):
            pe.wait_ge(self.taken[b], i + 1)
            pe.wait_ge(self.loaded[b], i * 16 + 16)
            for k in range(KD):
                at = 32 * (k % GROUPS)
                last = self.nc.tensor.matmul(self.g.ps[at:at + 2, self.banks + b, 0:self.width], self.g.cT[:, k:k + 9:8],
                                             self.w[b][:, k, :], start=(k < GROUPS), stop=(k >= KD - GROUPS),
                                             tile_position=(0, at))
            last.then_inc(self.used[b], 1)

    def add(self, dve, link, i):
        m = self.m[:, :, :].rearrange("s r d -> s (r d)")
        for b in range(2):
            at = bass.ds(i * (2 * self.width) + b * self.width, self.width)
            dve.wait_ge(self.used[b], i + 1)
            for j in range(GROUPS):
                last = self.nc.vector.tensor_tensor(m[:, at], self.g.ps[32 * j:32 * j + 2, self.banks + b, 0:self.width],
                                                    m[:, at], ALU.add)
                if j < GROUPS - 1:
                    link(last)
            last.then_inc(self.taken[b], 1)

    LINKS = 2 * (GROUPS - 1)


def stage_modulation(nc, g, hT, load_x):
    with ExitStack() as s:
        cc = g.sb(s, "cc", [16, P])
        cs = g.sb(s, "cs", [16, P])
        M = Modulation(nc, g, s, "mod", 0, 512, 0)
        m, gain = M.m, M.gain
        trips, early = M.slices // 2, 2
        X = g.sb(s, "X", [P, TT, D])
        sq = g.sb(s, "sq", [P, D])
        xn = g.sb(s, "xn", [P, 2, D])
        st = g.sb(s, "st", [P, 3, TT])
        abT = g.sb(s, "abT", [P, 2, KD, 2])
        x_loaded, x_squared, x_root, rstd_ready, xn_ready, x_turned, x_taken, ab_made, ab_ps, ab_ready = g.sems(
            "mod", "x_loaded x_squared x_root rstd_ready xn_ready x_turned x_taken ab_made ab_ps ab_ready")
        c_loaded, silu_done, cT_ps, cT_done = g.sems("mod", "c_loaded silu_done cT_ps cT_done")
        vec_ready, vec_stored, chain = g.sems("mod", "vec_ready vec_stored chain")
        turned = lambda t: g.ps[:, 4 + 2 * (t % 2):6 + 2 * (t % 2), :]
        block = s.enter_context(nc.Block())

        @block.sync
        def _(sp):
            sp.dma_start(cc[0:8, :], g.io["c"].rearrange("a (k p) -> (a k) p", p=P)).then_inc(c_loaded, 16)
            sp.dma_start(cc[8:16, :], g.io["c_ctx"].rearrange("(k p) -> k p", p=P)).then_inc(c_loaded, 16)
            M.load_parameters(sp)
            M.load_first(sp)
            with sp.Fori(0, trips - 1) as i:
                M.load_next(sp, i)
            sp.wait_ge(vec_ready, 1)
            sp.dma_start(g.mod_vecs[0], m[:, :, :]).then_inc(vec_stored, 16)
            sp.wait_ge(vec_stored, 16)

        @block.scalar
        def _(act):
            act.wait_ge(c_loaded, 32)
            nc.scalar.activation(cs[:, :], cc[:, :], ACT.Silu).then_inc(silu_done, 1)
            act.wait_ge(x_loaded, 16 * TT)
            for t in range(TT):
                if t:
                    act.wait_ge(x_squared, t)
                nc.scalar.activation(sq[:, :], X[:, t, :], ACT.Square, accum_out=st[:, 0, t:t + 1]).then_inc(x_squared, 1)
            act.wait_ge(x_squared, TT)
            nc.scalar.activation(st[:, 1, :], st[:, 0, :], ACT.Sqrt, scale=1.0 / D, bias=g.eps[:, 0:1]).then_inc(x_root, 1)
            act.wait_ge(rstd_ready, 1)

            def take(t):
                act.wait_ge(x_turned, t + 1)
                nc.scalar.activation(hT[:, :, t * P:(t + 1) * P], turned(t).rearrange("p a (k q) -> p (a k) q", q=P), ACT.Copy)\
                    .then_inc(x_taken, 1)

            for t in range(TT):
                nc.scalar.activation(xn[:, t % 2, :], X[:, t, :], ACT.Copy, scale=st[:, 2, t:t + 1]).then_inc(xn_ready, 1)
                if t:
                    take(t - 1)
            take(TT - 1)
            act.wait_ge(x_taken, TT)
            act.wait_ge(ab_ready, 1)
            for k in range(KD // 2, KD):
                for o, n, stream in ((0, CTX, 1), (CTX, LAT, 0)):
                    nc.scalar.activation(hT[:, k, o:o + n], hT[:, k, o:o + n], ACT.Identity,
                                         scale=abT[:, 0, k, stream:stream + 1], bias=abT[:, 1, k, stream:stream + 1])

        @block.gpsimd
        def _(pool):
            for t in range(TT):
                pool.dma_start(X[:, t, :], load_x(t)).then_inc(x_loaded, 16)

        @block.tensor
        def _(pe):
            pe.wait_ge(silu_done, 1)
            nc.tensor.transpose(g.ps[:, 2, 0:16], cs[:, :], g.ident[0:16, 0:16]).then_inc(cT_ps, 1)
            pe.wait_ge(cT_done, 1)
            with pe.Fori(0, early) as i:
                M.multiply(pe, i)
            for t in range(TT):
                pe.wait_ge(xn_ready, t + 1)
                if t >= 2:
                    pe.wait_ge(x_taken, t - 1)
                for k in range(KD):
                    last = nc.tensor.transpose(turned(t)[:, k // 4, (k % 4) * P:(k % 4 + 1) * P],
                                               xn[:, t % 2, k * P:(k + 1) * P], g.ident[:, :])
                last.then_inc(x_turned, 1)
            with pe.Fori(early, trips) as i:
                M.multiply(pe, i)
            pe.wait_ge(ab_made, 1)
            for r in range(2):
                for k in range(KD):
                    c = 2 * (r * KD + k)
                    last = nc.tensor.transpose(g.ps[:, 2, c:c + 2], m[:, 1 - r, k * P:(k + 1) * P], g.ident[0:2, 0:2])
            last.then_inc(ab_ps, 1)

        @block.vector
        def _(dve):
            link = Link(dve, chain)
            for b in range(2):
                dve.sem_inc(M.taken[b], 1)
            dve.wait_ge(cT_ps, 1)
            nc.vector.tensor_copy(g.cT[:, :], g.ps[:, 2, 0:16]).then_inc(cT_done, 1)
            dve.wait_ge(M.par_loaded, 48)
            for first, end in ((0, early), (early, trips)):
                with dve.Fori(first, end) as i:
                    link.enter(i, M.LINKS)
                    if first:
                        link.n -= first * M.LINKS
                        link.before = link.n
                    M.add(dve, link, i)
                    link.leave(end if first else end - first)
                if not first:
                    dve.wait_ge(x_root, 1)
                    nc.vector.reciprocal(st[:, 2, :], st[:, 1, :]).then_inc(rstd_ready, 1)
            for b in range(2):
                dve.wait_ge(M.taken[b], trips + 1)
            nc.vector.scalar_tensor_tensor(m[:, 1, :], m[:, 1, :], 1.0, gain[:, 0, :], ALU.add, ALU.mult).then_inc(ab_made, 1)
            nc.vector.tensor_tensor(m[:, 2, :], m[:, 2, :], gain[:, 2, :], ALU.mult)
            dve.wait_ge(ab_ps, 1)
            nc.vector.tensor_copy(abT[:, :, :, :].rearrange("p r k s -> p (r k s)"), g.ps[:, 2, 0:4 * KD]).then_inc(ab_ready, 1)
            dve.wait_ge(ab_ready, 1)
            dve.wait_ge(x_taken, TT)
            for k in range(KD // 2):
                for o, n, stream in ((0, CTX, 1), (CTX, LAT, 0)):
                    nc.vector.tensor_scalar(hT[:, k, o:o + n], hT[:, k, o:o + n], abT[:, 0, k, stream:stream + 1],
                                            abT[:, 1, k, stream:stream + 1], ALU.mult, ALU.add)
            nc.vector.scalar_tensor_tensor(m[:, 4, :], m[:, 4, :], 1.0, gain[:, 1, :], ALU.add, ALU.mult)
            nc.vector.tensor_tensor(m[:, 5, :], m[:, 5, :], gain[:, 3, :], ALU.mult).then_inc(vec_ready, 1)


def load_vectors(nc, g, sp, layer, row, dst, loaded, streams=(0, 1)):
    for st in streams:
        sp.dma_start(dst[:, st, :], g.mod_vecs[layer, st, row].partition_broadcast(P)).then_inc(loaded, 16)


def tile_rows(ap, t):
    return ap[t * P:(t + 1) * P, :]


SEGS = ((0, CTX), (CTX, LAT))


def token_row(g, bank):
    return g.ps[:, bank:bank + 2, :].rearrange("p b c -> p (b c)")[:, 512 - CTX:512 + LAT]


def project(nc, out, lhsT, hT, segs=SEGS):
    for o, n in segs:
        for k in range(KD):
            last = nc.tensor.matmul(out[:, o - segs[0][0]:o - segs[0][0] + n], lhsT(k), hT[:, k, o:o + n],
                                    start=(k == 0), stop=(k == KD - 1))
    return last


AB_LRU_IN = D
AB_Q, AB_K, AB_V, AB_OG, AB_ALR = 2048, 2560, 3072, 4096, 5120


def stage_lru(nc, g, hT):
    io = g.io
    NP = 11
    LEFT, GAP = 2, 3
    XP = CTX + LAT + 2 * GAP
    XC = CTX + GAP + LAT
    with ExitStack() as s:
        wx = g.sb(s, "wx", [P, KD, P])
        wg = g.sb(s, "wg", [P, KD, P])
        w4 = g.sb(s, "w4", [P, 4, P])
        par = g.sb(s, "par", [P, P])
        table = g.sb(s, "table", [P, 13, 8])
        tmp = g.sb(s, "tmp", [P, 8, 16])
        cur = g.sb(s, "cur", [P, 13])
        xp = g.sb(s, "xp", [P, XP])
        xc = g.sb(s, "xc", [P, XC])
        gel = g.sb(s, "gel", [P, T])
        Rg = g.sb(s, "Rg", [P, 2, T])
        Ig = g.sb(s, "Ig", [P, 2, T])
        Ag = g.sb(s, "Ag", [P, 2, T])
        Th = g.sb(s, "Th", [P, 2, T])
        V = g.sb(s, "V", [P, 2, T])
        S2 = g.sb(s, "S2", [P, 2, T])
        ya = g.sb(s, "ya", [P, KD, T])
        par_loaded, par_ps, lam_ready, lam_exp, lam_w, lam_ln, chain, achain = g.sems(
            "lru", "par_loaded par_ps lam_ready lam_exp lam_w lam_ln chain achain")
        wx_loaded, wg_loaded, w4_loaded = g.sems("lru", "wx_loaded wg_loaded w4_loaded")
        x_ready, xp_ready, xc_ready, g_ready, gel_ready, ri_ready, ri_copied = g.sems(
            "lru", "x_ready xp_ready xc_ready g_ready gel_ready ri_ready ri_copied")
        decay_ready, v_ready, s_ready, y_ready, stored = g.sems("lru", "decay_ready v_ready s_ready y_ready stored")
        wx_d = io["ab_w_in"][0].rearrange("(k p) n -> p k n", p=P)
        M = Modulation(nc, g, s, "lru", 1, 6 * D // (2 * KD), 6)
        m, gain = M.m, M.gain
        vec_ready, plus_one, vec_stored = g.sems("lru", "vec_ready plus_one vec_stored")
        block = s.enter_context(nc.Block())

        @block.gpsimd
        def _(pool):
            one = g.ones[0:2, 0:1].broadcast_to([2, D])
            for b in range(2):
                pool.wait_ge(M.taken[b], KD + 1)
            for sub in range(2):
                nc.gpsimd.tensor_tensor(m[:, 3 * sub + 2, :], m[:, 3 * sub + 2, :], gain[:, 2 + sub, :], ALU.mult).then_inc(vec_ready, 1)
                nc.gpsimd.tensor_tensor(m[:, 3 * sub + 1, :], m[:, 3 * sub + 1, :], one, ALU.add).then_inc(plus_one, 1)
                pool.wait_ge(plus_one, sub + 1)
                nc.gpsimd.tensor_tensor(m[:, 3 * sub + 1, :], m[:, 3 * sub + 1, :], gain[:, sub, :], ALU.mult).then_inc(vec_ready, 1)

        @block.sync
        def _(sp):
            rows = lambda ap: ap.rearrange("r (j p) -> (r j) p", p=P)
            for r, name in ((0, "ab_conv_w"), (5, "ab_lru_ba"), (7, "ab_lru_bi"), (9, "ab_lru_lambda")):
                src = rows(io[name][0])
                sp.dma_start(par[8 * r:8 * r + src.shape[0], :], src).then_inc(par_loaded, 16)
            sp.dma_start(par[32:40, :], rows(io["ab_conv_b"])).then_inc(par_loaded, 16)

            def load_x(col):
                sp.dma_start(wx[:, :, :], wx_d[:, :, col(AB_LRU_IN)]).then_inc(wx_loaded, 16)

            def load_g(col):
                sp.dma_start(wg[:, :, :], wx_d[:, :, col(0)]).then_inc(wg_loaded, 16)

            def load_4(head):
                for n, name in enumerate(("ab_lru_wa", "ab_lru_wi")):
                    sp.dma_start(w4[:, n:n + 3:2, :].rearrange("p d e -> p d e"),
                                 io[name][0][:, head, :, :].rearrange("d h p e -> p (d h) e")).then_inc(w4_loaded, 16)

            load_x(lambda o: slice(o, o + P))
            load_g(lambda o: slice(o, o + P))
            load_4(slice(0, 1))
            M.load_parameters(sp)
            M.load_first(sp)
            with sp.Fori(0, KD - 1) as i:
                sp.wait_ge(x_ready, i + 1)
                load_x(lambda o: bass.ds(i * P + (o + P), P))
                sp.wait_ge(g_ready, i + 1)
                load_g(lambda o: bass.ds(i * P + (o + P), P))
                sp.wait_ge(ri_ready, i * 2 + 2)
                load_4(bass.ds(i + 1, 1))
                M.load_next(sp, i)
                sp.wait_ge(y_ready, i + 2)
                sp.dma_start(g.ya_rows[:, bass.ds(i, 1), :], ya[:, bass.ds(i, 1), :]).then_inc(stored, 16)
            sp.wait_ge(y_ready, KD + 1)
            sp.dma_start(g.ya_rows[:, KD - 1:KD, :], ya[:, KD - 1:KD, :]).then_inc(stored, 16)
            sp.wait_ge(vec_ready, 4)
            sp.dma_start(g.mod_vecs[1], m[:, :, :]).then_inc(vec_stored, 16)
            sp.wait_ge(stored, 16 * KD)
            sp.wait_ge(vec_stored, 16)

        @block.tensor
        def _(pe):
            pe.wait_ge(par_loaded, 80)
            nc.tensor.transpose(g.ps[:, 7, 0:8 * NP], par[0:8 * NP, :], g.ident[0:8 * NP, 0:8 * NP]).then_inc(par_ps, 1)
            with pe.Fori(0, KD) as i:
                pe.wait_ge(wx_loaded, i * 16 + 16)
                pe.wait_ge(xp_ready, i + 1)
                project(nc, token_row(g, 0), lambda k: wx[:, k, :], hT).then_inc(x_ready, 1)
                pe.wait_ge(wg_loaded, i * 16 + 16)
                pe.wait_ge(ri_copied, i * 2 + 1)
                project(nc, token_row(g, 2), lambda k: wg[:, k, :], hT).then_inc(g_ready, 1)
                M.multiply(pe, i)
                pe.wait_ge(w4_loaded, i * 32 + 32)
                pe.wait_ge(xc_ready, i + 2)
                pe.wait_ge(gel_ready, i + 1)
                for d in range(2):
                    pe.wait_ge(ri_copied, i * 2 + (d + 1))
                    for n in range(2):
                        out = token_row(g, 4 if n == 0 else 2)
                        nc.tensor.matmul(out[:, 0:CTX], w4[:, 2 * d + n, :], xc[:, 0:CTX], start=True, stop=True)
                        last = nc.tensor.matmul(out[:, CTX:T], w4[:, 2 * d + n, :], xc[:, CTX + GAP:XC], start=True, stop=True)
                    last.then_inc(ri_ready, 1)

        @block.scalar
        def _(act):
            link = Link(act, achain)
            act.wait_ge(lam_ready, 1)
            nc.scalar.activation(tmp[:, 1, :], tmp[:, 0, :], ACT.Exp, scale=-1.0).then_inc(lam_exp, 1)
            act.wait_ge(lam_w, 1)
            nc.scalar.activation(tmp[:, 3, :], tmp[:, 2, :], ACT.Ln).then_inc(lam_ln, 1)
            for credit in (xp_ready, ri_copied):
                act.sem_inc(credit, 1)
            with act.Fori(0, KD) as i:
                link.enter(i, 2)
                act.wait_ge(x_ready, i + 1)
                act.wait_ge(xc_ready, i + 1)
                src = token_row(g, 0)
                nc.scalar.activation(xp[:, LEFT:LEFT + CTX], src[:, 0:CTX], ACT.Copy)
                nc.scalar.activation(xp[:, LEFT + CTX + GAP:LEFT + CTX + GAP + LAT], src[:, CTX:T], ACT.Copy).then_inc(xp_ready, 1)
                act.wait_ge(g_ready, i + 1)
                act.wait_ge(y_ready, i + 1)
                nc.scalar.activation(gel[:, :], token_row(g, 2), ACT.Gelu_apprx_tanh).then_inc(gel_ready, 1)
                for d in range(2):
                    act.wait_ge(ri_ready, i * 2 + (d + 1))
                    link.mark(nc.scalar.activation(Rg[:, d, :], token_row(g, 4), ACT.Sigmoid, bias=cur[:, 5 + d:6 + d]))
                    nc.scalar.activation(Ig[:, d, :], token_row(g, 2), ACT.Sigmoid, bias=cur[:, 7 + d:8 + d]).then_inc(ri_copied, 1)
                link.wait()
                for d in range(2):
                    nc.scalar.activation(Th[:, d, :], Rg[:, d, :], ACT.Tanh, scale=cur[:, 11 + d:12 + d])
                    nc.scalar.activation(Ag[:, d, :], Rg[:, d, :], ACT.Exp, scale=cur[:, 9 + d:10 + d]).then_inc(decay_ready, 1)
                for d in range(2):
                    act.wait_ge(v_ready, i * 2 + (d + 1))
                    nc.scalar.activation(S2[:, d, :], V[:, d, :], ACT.Sqrt).then_inc(s_ready, 1)
                link.leave(KD)

        @block.vector
        def _(dve):
            link = Link(dve, chain)
            dve.wait_ge(par_ps, 1)
            link.mark(nc.vector.memset(xp[:, :], 0.0))
            tf = table[:, :, :].rearrange("p r j -> p (r j)")
            link(nc.vector.tensor_copy(tf[:, 0:88], g.ps[:, 7, 0:88]))
            lam = tf[:, 72:88]
            nc.vector.scalar_tensor_tensor(tmp[:, 0, :], lam, -1.0, lam, ALU.mult, ALU.max).then_inc(lam_ready, 1)
            dve.wait_ge(lam_exp, 1)
            nc.vector.tensor_scalar(tmp[:, 2, :], tmp[:, 1, :], 1.0, None, ALU.add).then_inc(lam_w, 1)
            dve.wait_ge(lam_w, 1)
            link.mark(nc.vector.tensor_scalar(tmp[:, 4, :], tmp[:, 2, :], 1.0, None, ALU.is_equal))
            link(nc.vector.tensor_scalar(tmp[:, 5, :], tmp[:, 2, :], -1.0, None, ALU.add))
            link(nc.vector.tensor_tensor(tmp[:, 5, :], tmp[:, 5, :], tmp[:, 4, :], ALU.add))
            link(nc.vector.reciprocal(tmp[:, 6, :], tmp[:, 5, :]))
            dve.wait_ge(lam_ln, 1)
            link(nc.vector.tensor_tensor(tmp[:, 6, :], tmp[:, 6, :], tmp[:, 3, :], ALU.mult))
            link(nc.vector.tensor_tensor(tmp[:, 6, :], tmp[:, 6, :], tmp[:, 4, :], ALU.add))
            link(nc.vector.tensor_tensor(tmp[:, 6, :], tmp[:, 6, :], tmp[:, 1, :], ALU.mult))
            link(nc.vector.tensor_scalar(tmp[:, 7, :], lam, -1.0, 0.0, ALU.mult, ALU.max))
            link(nc.vector.tensor_tensor(tmp[:, 7, :], tmp[:, 7, :], tmp[:, 6, :], ALU.add))
            link.mark(nc.vector.tensor_scalar(tf[:, 72:88], tmp[:, 7, :], -LRU_C, None, ALU.mult))
            link(nc.vector.tensor_scalar(tf[:, 88:104], tmp[:, 7, :], LRU_C, None, ALU.mult))
            for credit in (xc_ready, y_ready, *M.taken):
                dve.sem_inc(credit, 1)
            dve.wait_ge(M.par_loaded, 48)
            g.hold(dve)
            with dve.Fori(0, KD) as i:
                link.enter(i, 14 + M.LINKS)
                dve.wait_ge(xp_ready, i + 2)
                g.hold(dve)
                link(nc.vector.tensor_copy(cur[:, :], table[:, :, bass.ds(i, 1)].rearrange("p r j -> p (r j)")))
                link(nc.vector.tensor_scalar(xc[:, :], xp[:, 0:XC], cur[:, 0:1], cur[:, 4:5], ALU.mult, ALU.add))
                for j in (1, 2):
                    link(nc.vector.scalar_tensor_tensor(xc[:, :], xp[:, j:j + XC], cur[:, j:j + 1], xc[:, :], ALU.mult, ALU.add))
                nc.vector.scalar_tensor_tensor(xc[:, :], xp[:, 3:3 + XC], cur[:, 3:4], xc[:, :], ALU.mult, ALU.add).then_inc(xc_ready, 1)
                dve.wait_ge(xc_ready, i + 2)
                M.add(dve, link, i)
                for d in range(2):
                    dve.wait_ge(decay_ready, i * 2 + (d + 1))
                    link(nc.vector.tensor_tensor(V[:, d, :], Ag[:, d, :], Ag[:, d, :], ALU.mult))
                    nc.vector.scalar_tensor_tensor(V[:, d, :], V[:, d, :], 1.0, Th[:, d, :], ALU.add, ALU.mult).then_inc(v_ready, 1)
                    nc.vector.tensor_tensor(Ig[:, d, 0:CTX], Ig[:, d, 0:CTX], xc[:, 0:CTX], ALU.mult)
                    link.mark(nc.vector.tensor_tensor(Ig[:, d, CTX:T], Ig[:, d, CTX:T], xc[:, CTX + GAP:XC], ALU.mult))
                for d in range(2):
                    dve.wait_ge(s_ready, i * 2 + (d + 1))
                    if d == 0:
                        link.wait()
                    link(nc.vector.tensor_tensor(Ig[:, d, :], Ig[:, d, :], S2[:, d, :], ALU.mult))
                    if d == 0:
                        link(nc.vector.tensor_tensor_scan(V[:, 0, :], Ag[:, 0, :], Ig[:, 0, :], 0.0, ALU.mult, ALU.add))
                    else:
                        link(nc.vector.tensor_tensor_scan(V[:, 1, 0:CTX][:, ::-1], Ag[:, 1, 0:CTX][:, ::-1],
                                                          Ig[:, 1, 0:CTX][:, ::-1], 0.0, ALU.mult, ALU.add))
                        link(nc.vector.tensor_tensor_scan(V[:, 1, CTX:T][:, ::-1], Ag[:, 1, CTX:T][:, ::-1],
                                                          Ig[:, 1, CTX:T][:, ::-1], V[:, 1, 0:1], ALU.mult, ALU.add))
                link(nc.vector.tensor_tensor(V[:, 0, :], V[:, 0, :], V[:, 1, :], ALU.add))
                nc.vector.tensor_tensor(ya[:, bass.ds(i, 1), :].rearrange("p a t -> p (a t)"), V[:, 0, :], gel[:, :],
                                        ALU.mult).then_inc(y_ready, 1)
                link.leave(KD)


def scan_chunks(d):
    if d == 0:
        return list(range(NCH))
    return list(range(CCH - 1, -1, -1)) + list(range(NCH - 1, CCH - 1, -1))


def stage_attention(nc, g, name, hT, gla):
    io = g.io
    heads, NV = (4, 2) if gla else (8, 1)
    DV = NV * P
    first_tile = 0 if gla else CT
    gate_scale = 1.0 / GLA_TAU if gla else 1.0
    w_in = io["ab_w_in" if gla else "c_w_in"][0].rearrange("(k p) n -> p k n", p=P)
    if gla:
        parts = [("v", AB_V, DV), ("k", AB_K, P), ("q", AB_Q, P), ("o", AB_OG, DV)]
        n_dma, n_par = 6, 8
    else:
        parts = [("v", 3 * D, DV), ("f0", D, P), ("f1", 2 * D, P), ("q", 0, P), ("o", 4 * D, DV)]
        n_dma, n_par = 5, 16
    at, width = {}, 0
    for what, _, n in parts:
        at[what] = width
        width += n
    out_segs = SEGS if gla else SEGS[1:]
    out_at = first_tile * P
    with ExitStack() as s:
        W = g.sb(s, "W", [P, KD, width])
        par = g.sb(s, "par", [16, P])
        table = g.sb(s, "table", [P, 3, 8])
        cur = g.sb(s, "cur", [P, 5])
        q = g.sb(s, "q", [P, T])
        K = g.sb(s, "K", [P, 1 if gla else 2, T])
        vt = g.sb(s, "vt", [P, TT, DV])
        OG = g.sb(s, "OG", [P, NV, T])
        Z = g.sb(s, "Z", [P, 2, T])
        B = g.sb(s, "B", [P, 2, T])
        D1 = g.sb(s, "D1", [P, 2, T])
        D2 = g.sb(s, "D2", [P, 2, T])
        Es = g.sb(s, "Es", [P, 2, 4, T])
        decay = g.sb(s, "decay", [P, 2, NCH])
        kdT = g.sb(s, "kdT", [P, 2, TT, P])
        sc = g.sb(s, "sc", [P, 2, TT, P])
        term = g.sb(s, "term", [P, P, NCH - 1])
        factor = g.sb(s, "factor", [P, 2, P, NCH - 1])
        ST = g.sb(s, "ST", [P, 2, NV, P, NCH - 1])
        start = g.sb(s, "start", [P, 2, T])
        if gla:
            walr = g.sb(s, "walr", [P, KD, 2 * GLA_RANK])
            wa2 = g.sb(s, "wa2", [2 * GLA_RANK, 2, P])
            alr = g.sb(s, "alr", [2 * GLA_RANK, T])
            Y = g.sb(s, "Y", [P, KD, T])
            zero = g.sb(s, "zero", [P, D // 2])
        else:
            Y = g.sb(s, "Y", [P, KD, LAT])
        names = ("par_loaded par_ps par_ready par_act w_loaded alr_loaded alr_ps alr_copied proj_ready proj_copied "
                 "abs_ready soft_ready d_ready e_ready qk_ready kd_ready kdT_ps kdT_copied s_ps sc_ready kv_ps "
                 "kv_taken decay_ready factor_ready state_ready o_ready o_taken sq_ready n_ready root_ready "
                 "head_done stored chain achain masks zero_made zero_stored wa2_zero")
        S = dict(zip(names.split(), g.sems(name, names)))
        block = s.enter_context(nc.Block())
        items = (["v", "z0", "z1", "k", "q", "o0", "o1"] if gla else ["v", "f0", "f1", "q", "o0"])
        NI = len(items)
        row = lambda bank: token_row(g, bank)
        flat = lambda bank: g.ps[:, bank:bank + 3, :].rearrange("p b c -> p (b c)")
        seg_of = {what: SEGS for what in items}
        if gla:
            bank_row = dict(z0=row(4), z1=row(6), k=row(4), q=row(6), o0=row(0), o1=row(2))
            turned, kv_bank = row(4), 0
            score_row = (row(6), row(6))
            out_row = (row(4), row(6))
        else:
            seg_of["q"] = seg_of["o0"] = SEGS[1:]
            bank_row = dict(f0=row(4), f1=row(6), q=g.ps[:, 3, :], o0=g.ps[:, 4, :])
            turned, kv_bank = row(0), 4
            score_row = (g.ps[:, 3, :], g.ps[:, 2, :])
            out_row = (g.ps[:, 3, :],)
        norm_row = row(2) if gla else g.ps[:, 2, :]
        kv_row = [g.ps[:, kv_bank + 2 * m:kv_bank + 2 * m + 2, :].rearrange("p b c -> p (b c)") for m in range(2)]
        rows = lambda ap: ap.rearrange("r (j p) -> (r j) p", p=P)
        copied_at = lambda i, item: i * NI + (items.index(item) + 1)
        updates = [(d, v) for d in range(2) for v in range(NV)]
        NU = len(updates)

        @block.sync
        def _(sp):
            if gla:
                sp.dma_start(par[0:8, :], rows(io["ab_gla_ba"][0])).then_inc(S["par_loaded"], 16)
                sp.dma_start(walr[:, :, :], w_in[:, :, AB_ALR:AB_ALR + 2 * GLA_RANK]).then_inc(S["alr_loaded"], 16)
            else:
                sp.dma_start(par[0:16, :], rows(io["hgrn_lb_logits"])).then_inc(S["par_loaded"], 16)

            def load(col):
                for what, first, n in parts:
                    sp.dma_start(W[:, :, at[what]:at[what] + n], w_in[:, :, col(first, n)]).then_inc(S["w_loaded"], 16)
                if gla:
                    for d in range(2):
                        sp.dma_start(wa2[d * GLA_RANK:(d + 1) * GLA_RANK, d, :], io["ab_gla_wa2"][0, d][:, col(0, P)]).then_inc(S["w_loaded"], 16)

            def store(at):
                sp.dma_start(g.yb_rows[:, at, out_at:T], Y[:, at, :]).then_inc(S["stored"], 16)

            if gla:
                sp.wait_ge(S["wa2_zero"], 1)
            load(lambda first, n: slice(first, first + n))
            with sp.Fori(0, heads - 1) as i:
                sp.wait_ge(S["proj_ready"], i * NI + NI)
                load(lambda first, n: bass.ds(i * n + (first + n), n))
                sp.wait_ge(S["head_done"], i + 2)
                store(bass.ds(i * NV, NV))
            sp.wait_ge(S["head_done"], heads + 1)
            store(slice((heads - 1) * NV, heads * NV))
            sp.wait_ge(S["stored"], 16 * heads)

        @block.tensor
        def _(pe):
            def sums(ready):
                pe.wait_ge(S["sq_ready"], ready)
                for o, n in out_segs:
                    for v in range(NV):
                        last = nc.tensor.matmul(norm_row[:, o - out_at:o - out_at + n], g.ones[:, :], D1[:, v, o:o + n],
                                                start=(v == 0), stop=(v == NV - 1))
                last.then_inc(S["n_ready"], 1)

            pe.wait_ge(S["par_loaded"], 16)
            nc.tensor.transpose(g.ps[:, 7, 0:n_par], par[0:n_par, :], g.ident[0:n_par, 0:n_par]).then_inc(S["par_ps"], 1)
            if gla:
                pe.wait_ge(S["alr_loaded"], 16)
                project(nc, row(0)[0:2 * GLA_RANK], lambda k: walr[:, k, :], hT).then_inc(S["alr_ps"], 1)
                pe.wait_ge(S["alr_copied"], 1)
            with pe.Fori(0, heads) as i:
                def await_copy(item):
                    pe.wait_ge(S["proj_copied"], copied_at(i, item))

                pe.wait_ge(S["w_loaded"], i * (16 * n_dma) + 16 * n_dma)
                for item in items:
                    if item in ("z0", "f0"):
                        pe.wait_ge(S["o_taken"], i + 1)
                    if item in ("k", "q") and gla:
                        await_copy("z0" if item == "k" else "z1")
                    if item == "o0":
                        await_copy("v" if gla else "f0")
                    if item == ("o1" if gla else "q"):
                        pe.wait_ge(S["root_ready"], i + 1)
                    if item == "v":
                        for t in range(TT):
                            for k in range(KD):
                                last = nc.tensor.matmul(flat(0)[:, t * DV:(t + 1) * DV], hT[:, k, t * P:(t + 1) * P],
                                                        W[:, k, at["v"]:at["v"] + DV],
                                                        start=(k == 0), stop=(k == KD - 1))
                    elif item in ("z0", "z1"):
                        for o, n in SEGS:
                            last = nc.tensor.matmul(bank_row[item][:, o:o + n], wa2[:, int(item[1]), :],
                                                    alr[:, o:o + n], start=True, stop=True)
                    else:
                        c = at[item[0]] + P * int(item[1]) if item[0] == "o" else at[item]
                        last = project(nc, bank_row[item], lambda k: W[:, k, c:c + P], hT, seg_of[item])
                    last.then_inc(S["proj_ready"], 1)
                    if item == ("z1" if gla else "v"):
                        if gla:
                            await_copy("v")
                        sums(i + 1)

                def turn_keys(d):
                    pe.wait_ge(S["kd_ready"], i * 2 + (d + 1))
                    if d:
                        pe.wait_ge(S["kdT_copied"], i * 2 + 1)
                    for t in range(TT):
                        last = nc.tensor.transpose(turned[:, t * P:(t + 1) * P], Es[:, d, 3, t * P:(t + 1) * P], g.ident[:, :])
                    last.then_inc(S["kdT_ps"], 1)

                def scores(d):
                    pe.wait_ge(S["qk_ready"], i * 2 + (d + 1))
                    if d and gla:
                        pe.wait_ge(S["sc_ready"], i * 2 + 1)
                    for t in range(first_tile, TT):
                        last = nc.tensor.matmul(score_row[d][:, t * P - out_at:(t + 1) * P - out_at], Es[:, d, 1, t * P:(t + 1) * P],
                                                Es[:, d, 0, t * P:(t + 1) * P], start=True, stop=True)
                    last.then_inc(S["s_ps"], 1)

                def update(n):
                    d, v = updates[n]
                    if v == 0:
                        pe.wait_ge(S["kdT_copied"], i * 2 + (d + 1))
                    if n:
                        pe.wait_ge(S["kv_taken"], i * NU + n)
                    for m, c in enumerate(scan_chunks(d)[:-1]):
                        half = slice(CHUNK * (c % 2), CHUNK * (c % 2) + CHUNK)
                        last = nc.tensor.matmul(kv_row[m % 2][:, m // 2 * P:(m // 2 + 1) * P], kdT[half, d, c // 2, :],
                                                vt[half, c // 2, v * P:(v + 1) * P], start=True, stop=True)
                    last.then_inc(S["kv_ps"], 1)

                def inside(d):
                    pe.wait_ge(S["sc_ready"], i * 2 + (2 if gla else d + 1))
                    for v in range(NV):
                        for t in range(first_tile, TT):
                            nc.tensor.matmul(out_row[v][:, t * P - out_at:(t + 1) * P - out_at], vt[:, t, v * P:(v + 1) * P],
                                             sc[:, d, t, :], start=(d == 0 and t in (0, CT)), stop=False,
                                             skip_group_check=True)

                def from_state(d, v):
                    pe.wait_ge(S["state_ready"], i * NU + (d * NV + v + 1))
                    order = scan_chunks(d)
                    for c in range(2 * first_tile, NCH):
                        if order[0] != c:
                            last = nc.tensor.matmul(out_row[v][:, c * CHUNK - out_at:(c + 1) * CHUNK - out_at],
                                                    ST[:, d, v, :, order.index(c) - 1],
                                                    Es[:, d, 2, c * CHUNK:(c + 1) * CHUNK], start=False,
                                                    stop=(d == 1 and c in (CCH - 2, NCH - 1)), skip_group_check=True)
                    return last

                await_copy("q")
                turn_keys(0)
                scores(0)
                turn_keys(1)
                if gla:
                    scores(1)
                await_copy(items[-1])
                update(0)
                if not gla:
                    scores(1)
                else:
                    pe.wait_ge(S["kdT_copied"], i * 2 + 2)
                inside(0)
                for n, (d, v) in enumerate(updates):
                    if n + 1 < NU:
                        update(n + 1)
                    if d and v == 0:
                        inside(1)
                    last = from_state(d, v)
                last.then_inc(S["o_ready"], 1)
            sums(heads + 1)

        @block.scalar
        def _(act):
            link = Link(act, S["achain"])

            def root(ready):
                act.wait_ge(S["n_ready"], ready)
                nc.scalar.activation(D2[:, 0, out_at:T], norm_row, ACT.Sqrt, scale=1.0 / DV,
                                     bias=g.eps[:, 0:1]).then_inc(S["root_ready"], 1)

            if gla:
                act.wait_ge(S["alr_ps"], 1)
                nc.scalar.activation(alr[:, :], row(0)[0:2 * GLA_RANK], ACT.Copy).then_inc(S["alr_copied"], 1)
            else:
                act.wait_ge(S["par_ready"], 1)
                nc.scalar.activation(table[:, 0, :], table[:, 2, :], ACT.Sigmoid)
                nc.scalar.activation(table[:, 1, :], table[:, 2, :], ACT.Sigmoid, scale=-1.0).then_inc(S["par_act"], 1)
            with act.Fori(0, heads) as i:
                link.enter(i, 1 if gla else 2)

                def copied(ins):
                    ins.then_inc(S["proj_copied"], 1)

                def await_item(item):
                    act.wait_ge(S["proj_ready"], copied_at(i, item))

                await_item("v")
                copied(nc.scalar.activation(vt[:, :, :].rearrange("p t v -> p (t v)"), flat(0)[:, 0:TT * DV], ACT.Copy))
                act.wait_ge(S["par_ready"], i + 2)
                if gla:
                    for d in range(2):
                        await_item(f"z{d}")
                        copied(nc.scalar.activation(Z[:, d, :], bank_row[f"z{d}"], ACT.Identity, bias=cur[:, d:d + 1]))
                root(i + 1)
                if gla:
                    act.wait_ge(S["abs_ready"], i + 1)
                    link(nc.scalar.activation(D1[:, :, :], D1[:, :, :], ACT.Exp, scale=-1.0))
                    nc.scalar.activation(D1[:, :, :], D1[:, :, :], ACT.Ln, bias=1.0).then_inc(S["soft_ready"], 1)
                    await_item("k")
                    copied(nc.scalar.activation(K[:, 0, :], bank_row["k"], ACT.Copy))
                else:
                    for d in range(2):
                        await_item(f"f{d}")
                        link(nc.scalar.activation(D1[:, d, :], bank_row[f"f{d}"], ACT.Sigmoid))
                        copied(nc.scalar.activation(K[:, d, :], bank_row[f"f{d}"], ACT.Sigmoid, scale=-1.0))
                    for d in range(2):
                        nc.scalar.activation(Z[:, d, :], D1[:, d, :], ACT.Ln, scale=cur[:, 1:2],
                                             bias=cur[:, 0:1]).then_inc(S["soft_ready"], 1)
                await_item("q")
                copied(nc.scalar.activation(q[:, out_at:T], bank_row["q"], ACT.Copy, scale=float(P) ** -0.5 if gla else 1.0))
                for d in range(2):
                    act.wait_ge(S["d_ready"], i * 2 + (d + 1))
                    nc.scalar.activation(Es[:, d, 0, out_at:T], D1[:, d, out_at:T], ACT.Exp, scale=gate_scale)
                    nc.scalar.activation(Es[:, d, 1, out_at:T], D1[:, d, out_at:T], ACT.Exp, scale=-gate_scale)
                    nc.scalar.activation(Es[:, d, 2, :], B[:, d, :], ACT.Exp, scale=gate_scale)
                    nc.scalar.activation(Es[:, d, 3, :], D2[:, d, :], ACT.Exp, scale=-gate_scale).then_inc(S["e_ready"], 1)
                act.wait_ge(S["head_done"], i + 1)
                for v in range(NV):
                    await_item(f"o{v}")
                    copied(nc.scalar.activation(OG[:, v, out_at:T], bank_row[f"o{v}"], ACT.Silu))
                for d in range(2):
                    act.wait_ge(S["kdT_ps"], i * 2 + (d + 1))
                    nc.scalar.activation(kdT[:, d, :, :].rearrange("p t k -> p (t k)"), turned, ACT.Copy)\
                        .then_inc(S["kdT_copied"], 1)
                for n in range(NU):
                    act.wait_ge(S["kv_ps"], i * NU + (n + 1))
                    if n:
                        act.wait_ge(S["state_ready"], i * NU + n)
                    for m in range(2):
                        last = nc.scalar.activation(term[:, :, m::2].rearrange("p v n -> p n v"),
                                                    kv_row[m].rearrange("p (n v) -> p n v", v=P)[:, 0:(NCH - m) // 2, :], ACT.Copy)
                    last.then_inc(S["kv_taken"], 1)
                act.wait_ge(S["o_ready"], i + 1)
                for v in range(NV):
                    last = nc.scalar.activation(D1[:, v, out_at:T], out_row[v], ACT.Square)
                last.then_inc(S["sq_ready"], 1)
                link.leave(heads)
            root(heads + 1)

        @block.gpsimd
        def _(pool):
            if gla:
                nc.gpsimd.memset(wa2[:, :, :], 0.0).then_inc(S["wa2_zero"], 1)
            nc.gpsimd.memset(D1[:, :, :], 0.0).then_inc(S["sq_ready"], 1)
            nc.gpsimd.memset(OG[:, :, :], 0.0)
            nc.gpsimd.memset(decay[:, :, :], 0.0)
            nc.gpsimd.memset(start[:, :, :], 1.0).then_inc(S["masks"], 1)
            pool.wait_ge(S["masks"], 1)
            chunks = start[:, :, :].rearrange("p d (c s) -> p d c s", s=CHUNK)
            nc.gpsimd.memset(chunks[:, 0, :, 0:1], 0.0)
            nc.gpsimd.memset(chunks[:, 1, :, CHUNK - 1:CHUNK], 0.0)
            nc.gpsimd.memset(sc[:, :, :, :], 0.0).then_inc(S["masks"], 1)
            if gla:
                sure, most, step = E, n_blocks(TT), 8
                nc.gpsimd.memset(zero[:, :], 0.0).then_inc(S["zero_made"], 1)
                pool.wait_ge(S["w_loaded"], 16 * n_dma)
                pool.wait_ge(S["zero_made"], 1)
                for b in range(sure, most, step):
                    pool.dma_start(g.y_rows[b * P:(b + step) * P, :].rearrange("(p b) (q d) -> p (b q) d", p=P, q=2),
                                   zero[:, :].unsqueeze(1).broadcast_to([P, step * 2, D // 2]))\
                        .then_inc(S["zero_stored"], 16)
            with pool.Fori(0, heads) as i:
                for d in range(2):
                    key = K[:, 0 if gla else d, :]
                    pool.wait_ge(S["e_ready"], i * 2 + (d + 1))
                    nc.gpsimd.tensor_tensor(Es[:, d, 3, :], Es[:, d, 3, :], key, ALU.mult).then_inc(S["kd_ready"], 1)
                for d in range(2):
                    ones = g.ones[:, 0:1].unsqueeze(1).broadcast_to([P, P, NCH - 1])
                    pool.wait_ge(S["decay_ready"], i * 2 + (d + 1))
                    every = decay[:, d, 0:NCH - 1].unsqueeze(1).broadcast_to([P, P, NCH - 1])
                    nc.gpsimd.tensor_tensor(factor[:, d, :, :], every, ones, ALU.mult).then_inc(S["factor_ready"], 1)
            if gla:
                pool.wait_ge(S["zero_stored"], 16 * ((n_blocks(TT) - E) // 8))

        @block.vector
        def _(dve):
            link = Link(dve, S["chain"])

            def tail(ready, head):
                dve.wait_ge(S["root_ready"], ready)
                link(nc.vector.reciprocal(D2[:, 1, out_at:T], D2[:, 0, out_at:T]))
                for v in range(NV):
                    y = Y[:, bass.ds(head * NV + v, 1), :].rearrange("p a t -> p (a t)")
                    if gla:
                        last = nc.vector.tensor_tensor(y, OG[:, v, :], D2[:, 1, :], ALU.mult)
                    else:
                        back = lambda a: a.rearrange("p (w r) -> p w r", r=GRID_H)
                        last = nc.vector.tensor_tensor(y.rearrange("p (r w) -> p w r", w=GRID_W), back(OG[:, v, CTX:T]),
                                                       back(D2[:, 1, CTX:T]), ALU.mult)
                last.then_inc(S["head_done"], 1)

            dve.wait_ge(S["par_ps"], 1)
            tf = table[:, :, :].rearrange("p r j -> p (r j)")
            if gla:
                link(nc.vector.memset(table[:, :, :], 0.0))
                nc.vector.tensor_copy(table[:, 0:2, 0:4], g.ps[:, 7, 0:8].rearrange("p (r j) -> p r j", r=2)).then_inc(S["par_ready"], 1)
                dve.wait_ge(S["par_ready"], 1)
            else:
                link(nc.vector.tensor_copy(tf[:, 0:16], g.ps[:, 7, 0:16]))
                nc.vector.tensor_tensor(table[:, 2, :], table[:, 1, :], table[:, 0, :], ALU.subtract).then_inc(S["par_ready"], 1)
                dve.wait_ge(S["par_act"], 1)
            dve.sem_inc(S["o_taken"], 1)
            dve.wait_ge(S["masks"], 2)
            g.hold(dve)
            with dve.Fori(0, heads) as i:
                link.enter(i, PER_HEAD)
                nc.vector.tensor_copy(cur[:, 0:3], table[:, :, bass.ds(i, 1)].rearrange("p r j -> p (r j)"))\
                    .then_inc(S["par_ready"], 1)
                tail(i + 1, (i + (heads - 1)) & (heads - 1))
                if gla:
                    dve.wait_ge(S["proj_copied"], copied_at(i, "z1"))
                    nc.vector.scalar_tensor_tensor(D1[:, :, :], Z[:, :, :], -1.0, Z[:, :, :], ALU.mult, ALU.max)\
                        .then_inc(S["abs_ready"], 1)
                    dve.wait_ge(S["soft_ready"], i + 1)
                    link(nc.vector.scalar_tensor_tensor(Z[:, :, :], Z[:, :, :], 0.0, D1[:, :, :], ALU.min, ALU.subtract))
                else:
                    dve.wait_ge(S["proj_copied"], copied_at(i, "f1"))
                    dve.wait_ge(S["par_ready"], i + 2)
                    link(nc.vector.tensor_scalar(K[:, :, :], K[:, :, :], cur[:, 1:2], None, ALU.mult))
                    dve.wait_ge(S["soft_ready"], i * 2 + 2)
                for d in range(2):
                    turn = (lambda a: a) if d == 0 else (lambda a: a[:, ::-1])
                    ref, end = (CHUNK // 2 - 1, CHUNK - 1) if d == 0 else (CHUNK // 2, 0)
                    link(nc.vector.tensor_tensor_scan(turn(B[:, d, :]), turn(start[:, d, :]), turn(Z[:, d, :]), 0.0, ALU.mult, ALU.add))

                    def sub(out, col, c0):
                        chunks = lambda a: a[:, c0 * CHUNK:T].rearrange("p (c s) -> p c s", s=CHUNK)
                        b3 = chunks(B[:, d, :])
                        return nc.vector.tensor_tensor(chunks(out), b3,
                                                       b3[:, :, col:col + 1].broadcast_to([P, NCH - c0, CHUNK]), ALU.subtract)
                    sub(D1[:, d, :], ref, 2 * first_tile)
                    sub(D2[:, d, :], end, 0).then_inc(S["d_ready"], 1)
                dve.wait_ge(S["proj_copied"], copied_at(i, "q"))
                for d in range(2):
                    key = K[:, 0 if gla else d, out_at:T]
                    dve.wait_ge(S["e_ready"], i * 2 + (d + 1))
                    at_end = Es[:, d, 2, :].rearrange("p (c s) -> p c s", s=CHUNK)[:, :, CHUNK - 1 if d == 0 else 0]
                    if d == 0:
                        nc.vector.tensor_scalar(decay[:, 0, 1:NCH], at_end[:, 1:NCH], 1.0, None, ALU.mult).then_inc(S["decay_ready"], 1)
                    else:
                        nc.vector.tensor_scalar(decay[:, 1, 1:CCH], at_end[:, 0:CCH - 1][:, ::-1], 1.0, None, ALU.mult)
                        nc.vector.tensor_scalar(decay[:, 1, CCH:NCH], at_end[:, CCH:NCH][:, ::-1], 1.0, None, ALU.mult)\
                            .then_inc(S["decay_ready"], 1)
                    dve.wait_ge(S["decay_ready"], i * 2 + (d + 1))
                    nc.vector.tensor_tensor(Es[:, d, 0, out_at:T], Es[:, d, 0, out_at:T], q[:, out_at:T], ALU.mult)
                    nc.vector.tensor_tensor(Es[:, d, 2, out_at:T], Es[:, d, 2, out_at:T], q[:, out_at:T], ALU.mult)
                    nc.vector.tensor_tensor(Es[:, d, 1, out_at:T], Es[:, d, 1, out_at:T], key, ALU.mult).then_inc(S["qk_ready"], 1)

                def mask_scores(d):
                    dve.wait_ge(S["s_ps"], i * 2 + (d + 1))
                    nc.vector.memset(cur[:, 3 + d:4 + d], 0.0)
                    NS = TT - first_tile
                    nc.vector.copy_predicated(sc[:, d, first_tile:TT, :], g.mask[:, d:d + 1, :].broadcast_to([P, NS, P]),
                                              score_row[d].rearrange("p (t c) -> p t c", c=P)).then_inc(S["sc_ready"], 1)

                def scan_states(n):
                    d, v = updates[n]
                    if v == 0:
                        dve.wait_ge(S["factor_ready"], i * 2 + (d + 1))
                    dve.wait_ge(S["kv_taken"], i * NU + (n + 1))
                    one_row = lambda a: a.rearrange("p v n -> p (v n)")
                    nc.vector.tensor_tensor_scan(one_row(ST[:, d, v, :, :]), one_row(factor[:, d, :, :]), one_row(term[:, :, :]),
                                                 0.0, ALU.mult, ALU.add).then_inc(S["state_ready"], 1)

                mask_scores(0)
                if gla:
                    mask_scores(1)
                scan_states(0)
                if not gla:
                    mask_scores(1)
                for n in range(1, NU):
                    scan_states(n)
                dve.wait_ge(S["proj_copied"], i * NI + NI)
                dve.wait_ge(S["sq_ready"], i + 2)
                for v in range(NV):
                    last = nc.vector.tensor_tensor(OG[:, v, out_at:T], out_row[v], OG[:, v, out_at:T], ALU.mult)
                last.then_inc(S["o_taken"], 1)
                dve.wait_ge(S["o_taken"], i + 2)
                link.leave(heads)
            tail(heads + 1, heads - 1)


PER_HEAD = 1 + 1 + 2


def stage_rows(nc, g, name, tiles, hT, X, mix=None, experts=None, residual=None, norm=None, load_x=None,
               store_x=None, store_h=False, column_major=False):
    lat_only = tiles[0] == CT
    streams = (0,) if lat_only else (0, 1)
    N = len(tiles)
    ON_VECTOR = TOPK // 2
    with ExitStack() as s:
        if mix:
            w_out, sources = mix
            KY = sum(n for _, n in sources)
            first = tiles[0] * P
            Y = g.sb(s, "Yin", [P, KY, T])
            W = g.sb(s, "Wout", [P, KY, D])
        if experts:
            R, F = experts
            buf = g.sb(s, "buf", [P, TOPK, D])
            diag = g.sb(s, "diag", [P, 2, TOPK, P])
            gathered = g.sems(name, " ".join(f"gathered{k}" for k in range(TOPK)))
            diag_ready, summed_pe = g.sems(name, "diag_ready summed_pe")
        G, A, B = (g.sb(s, v, [P, 2, D]) if use else None for v, use in (("G", residual), ("A", norm), ("B", norm)))
        H = g.sb(s, "H", [P, 2, D]) if norm else None
        U = g.sb(s, "U", [P, D])
        sq = g.sb(s, "sq", [P, D])
        st = g.sb(s, "st", [P, 2, 4, TT])
        names = ("x_loaded vec_loaded f_ready f_squared f_var f_root x_ready x_squared x_var x_root "
                 "h_ready transposed copied chain summed")
        S = dict(zip(names.split(), g.sems(name, names)))
        if mix:
            w_loaded = g.sems(name, " ".join(f"w_loaded{c}" for c in range(KY // 2)))
            y_loaded = g.sems(name, " ".join(f"y_loaded{n}" for n in range(N)))
        h_stored = g.sems(name, "h_stored0 h_stored1")
        x_stored, = g.sems(name, "x_stored")
        block = s.enter_context(nc.Block())

        def f_tile(n, t):
            if experts:
                return F[:, t, :]
            return g.ps[:, 2 * (n % 2):2 * (n % 2) + 2, :].rearrange("p a c -> p (a c)")

        @block.sync
        def _(sp):
            if mix:
                wv = w_out.rearrange("(k p) n -> p k n", p=P)

                def load_y(n):
                    k, at = 0, slice(tiles[n] * P, (tiles[n] + 1) * P)
                    for rows, count in sources:
                        sp.dma_start(Y[:, k:k + count, at], rows[:, :, at]).then_inc(y_loaded[n], 16)
                        k += count

                load_y(0)
                for c in range(KY // 2):
                    sp.dma_start(W[:, 2 * c:2 * c + 2, :], wv[:, 2 * c:2 * c + 2, :]).then_inc(w_loaded[c], 16)
                load_y(1)
            if load_x:
                for t in tiles:
                    sp.dma_start(X[:, t, :], load_x(t)).then_inc(S["x_loaded"], 16)
            if residual:
                load_vectors(nc, g, sp, residual[0], 3 * residual[1] + 2, G, S["vec_loaded"], streams)
            if norm:
                load_vectors(nc, g, sp, norm[0], 3 * norm[1] + 1, A, S["vec_loaded"], streams)
                load_vectors(nc, g, sp, norm[0], 3 * norm[1], B, S["vec_loaded"], streams)
            if mix:
                for n in range(2, N):
                    load_y(n)
            for n, t in enumerate(tiles):
                if store_x:
                    sp.wait_ge(S["x_ready"], n + 1)
                    sp.dma_start(store_x(t), X[:, t, :]).then_inc(x_stored, 16)
                if store_h:
                    sp.wait_ge(S["h_ready"], n + 1)
                    sp.dma_start(tile_rows(g.h_rows, t), H[:, n % 2, :]).then_inc(h_stored[n % 2], 16)
            if store_x:
                sp.wait_ge(x_stored, 16 * N)
            if store_h:
                for b in range(2):
                    sp.wait_ge(h_stored[b], 16 * (N // 2))

        @block.gpsimd
        def _(pool):
            if experts:
                for n in range(N):
                    for k in [k + j for k in range(ON_VECTOR) for j in (0, ON_VECTOR)]:
                        if n and k < ON_VECTOR:
                            pool.wait_ge(S["summed"], (n - 1) * ON_VECTOR + k + 1)
                        elif n:
                            pool.wait_ge(summed_pe, (n - 1) * (TOPK - ON_VECTOR) + k - ON_VECTOR + 1)
                        c = n * TOPK + k
                        nc.gpsimd.indirect_dma_start(buf[:, k, :], None, g.y_rows,
                                                     bass.IndirectOffsetOnAxis(ap=R.pos[:, c:c + 1], axis=0))\
                            .then_inc(gathered[k], 16)

        @block.tensor
        def _(pe):
            def turn(n):
                pe.wait_ge(S["h_ready"], n + 1)
                if n >= 2:
                    pe.wait_ge(S["copied"], n - 1)
                for k in range(KD):
                    last = nc.tensor.transpose(g.ps[:, 4 + 2 * (n % 2) + k // 4, (k % 4) * P:(k % 4 + 1) * P],
                                               H[:, n % 2, k * P:(k + 1) * P], g.ident[:, :])
                last.then_inc(S["transposed"], 1)

            for n, t in enumerate(tiles):
                if mix:
                    if n >= 2:
                        pe.wait_ge(S["x_ready"], n - 1)
                    pe.wait_ge(y_loaded[n], 16 * len(sources))
                    for k in range(KY):
                        if n == 0 and k % 2 == 0:
                            pe.wait_ge(w_loaded[k // 2], 16)
                        for o in range(2):
                            last = nc.tensor.matmul(g.ps[:, 2 * (n % 2) + o, :], Y[:, k, t * P:(t + 1) * P],
                                                    W[:, k, o * 512:(o + 1) * 512], start=(k == 0), stop=(k == KY - 1))
                    last.then_inc(S["f_ready"], 1)
                if experts:
                    if n >= 2:
                        pe.wait_ge(S["f_ready"], n - 1)
                    pe.wait_ge(diag_ready, n + 1)
                    for k in range(ON_VECTOR, TOPK):
                        pe.wait_ge(gathered[k], 16 * (n + 1))
                        for o in range(2):
                            last = nc.tensor.matmul(g.ps[:, 2 * (n % 2) + o, :], diag[:, n % 2, k, :],
                                                    buf[:, k, o * 512:(o + 1) * 512], start=(k == ON_VECTOR), stop=(k == TOPK - 1))
                        last.then_inc(summed_pe, 1)
                if norm and n:
                    turn(n - 1)
            if norm:
                turn(N - 1)

        @block.scalar
        def _(act):
            def norms(n, t):
                if residual:
                    act.wait_ge(S["f_var"], n + 1)
                    nc.scalar.activation(st[:, 0, 2, t:t + 1], st[:, 0, 1, t:t + 1], ACT.Sqrt).then_inc(S["f_root"], 1)
                    act.wait_ge(S["x_ready"], n + 1)
                if not norm:
                    return
                if n:
                    act.wait_ge(S["x_squared"], n)
                if residual:
                    act.wait_ge(S["f_squared"], n + 1)
                elif load_x:
                    act.wait_ge(S["x_loaded"], 16 * N)
                nc.scalar.activation(sq[:, :], X[:, t, :], ACT.Square, accum_out=st[:, 1, 0, t:t + 1]).then_inc(S["x_squared"], 1)
                act.wait_ge(S["x_var"], n + 1)
                nc.scalar.activation(st[:, 1, 2, t:t + 1], st[:, 1, 1, t:t + 1], ACT.Sqrt).then_inc(S["x_root"], 1)

            def take(n, t):
                act.wait_ge(S["transposed"], n + 1)
                src = g.ps[:, 4 + 2 * (n % 2):6 + 2 * (n % 2), :].rearrange("p a (k q) -> p (a k) q", q=P)
                if column_major and t >= CT:
                    r0 = (t - CT) * (P // GRID_W)
                    lat = hT[:, :, CTX:T].rearrange("p k (w r) -> p k r w", r=GRID_H)
                    for r in range(P // GRID_W):
                        last = nc.scalar.activation(lat[:, :, r0 + r, :], src[:, :, r * GRID_W:(r + 1) * GRID_W], ACT.Copy)
                else:
                    last = nc.scalar.activation(hT[:, :, t * P:(t + 1) * P], src, ACT.Copy)
                last.then_inc(S["copied"], 1)

            def diagonals(n):
                for k in range(ON_VECTOR, TOPK):
                    last = nc.scalar.activation(diag[:, n % 2, k, :], g.ident[:, :], ACT.Copy, scale=R.gates[:, n, k:k + 1])
                last.then_inc(diag_ready, 1)

            if experts:
                diagonals(0)
                diagonals(1)
            for n, t in enumerate(tiles):
                if residual:
                    if n:
                        norms(n - 1, tiles[n - 1])
                    act.wait_ge(S["f_ready"], n + 1)
                    if n:
                        act.wait_ge(S["f_squared"], n)
                        if norm:
                            act.wait_ge(S["x_squared"], n)
                    nc.scalar.activation(sq[:, :], f_tile(n, t), ACT.Square, accum_out=st[:, 0, 0, t:t + 1]).then_inc(S["f_squared"], 1)
                    if experts and n + 2 < N:
                        diagonals(n + 2)
                    if n and norm:
                        take(n - 1, tiles[n - 1])
                else:
                    norms(n, t)
                    if n:
                        take(n - 1, tiles[n - 1])
            if residual:
                norms(N - 1, tiles[N - 1])
            if norm:
                take(N - 1, tiles[N - 1])

        @block.vector
        def _(dve):
            link = Link(dve, S["chain"])
            done = [0]

            def combine(n, k):
                if not experts:
                    return
                j = n * ON_VECTOR + k
                if k:
                    dve.wait_ge(S["summed"], j)
                dve.wait_ge(gathered[k], 16 * (n + 1))
                F_t = F[:, tiles[n], :]
                nc.vector.scalar_tensor_tensor(F_t, buf[:, k, :], R.gates[:, n, k:k + 1], F_t, ALU.mult, ALU.add)\
                    .then_inc(S["summed"], 1)
                if k == ON_VECTOR - 1:
                    dve.wait_ge(S["summed"], j + 1)
                    dve.wait_ge(summed_pe, (n + 1) * (TOPK - ON_VECTOR))
                    nc.vector.tensor_tensor(F_t, g.ps[:, 2 * (n % 2):2 * (n % 2) + 2, :].rearrange("p a c -> p (a c)"), F_t, ALU.add)\
                        .then_inc(S["f_ready"], 1)

            def variance(n, which, waited, ready):
                t = tiles[n]
                dve.wait_ge(S[waited], n + 1)
                nc.vector.tensor_scalar(st[:, which, 1, t:t + 1], st[:, which, 0, t:t + 1], 1.0 / D, EPS, ALU.mult, ALU.add)\
                    .then_inc(S[ready], 1)

            def new_x(n):
                t = tiles[n]
                k = 1 if t < CT else 0
                dve.wait_ge(S["f_root"], n + 1)
                link(nc.vector.reciprocal(st[:, 0, 3, t:t + 1], st[:, 0, 2, t:t + 1]))
                if n == 0:
                    dve.wait_ge(S["vec_loaded"], 16 * len(streams) * (1 + 2 * bool(norm)))
                    if load_x:
                        dve.wait_ge(S["x_loaded"], 16 * N)
                link(nc.vector.scalar_tensor_tensor(U[:, :], f_tile(n, t), st[:, 0, 3, t:t + 1], G[:, k, :], ALU.mult, ALU.mult))
                nc.vector.tensor_tensor(X[:, t, :], X[:, t, :], U[:, :], ALU.add).then_inc(S["x_ready"], 1)
                dve.wait_ge(S["x_ready"], n + 1)

            def new_h(n):
                t = tiles[n]
                k = 1 if t < CT else 0
                dve.wait_ge(S["x_root"], n + 1)
                link(nc.vector.reciprocal(st[:, 1, 3, t:t + 1], st[:, 1, 2, t:t + 1]))
                if n == 0 and not residual:
                    dve.wait_ge(S["vec_loaded"], 32 * len(streams))
                if n >= 2:
                    dve.wait_ge(S["transposed"], n - 1)
                    if store_h:
                        dve.wait_ge(h_stored[n % 2], 16 * (n // 2))
                link(nc.vector.scalar_tensor_tensor(H[:, n % 2, :], X[:, t, :], st[:, 1, 3, t:t + 1], A[:, k, :], ALU.mult, ALU.mult))
                nc.vector.tensor_tensor(H[:, n % 2, :], H[:, n % 2, :], B[:, k, :], ALU.add).then_inc(S["h_ready"], 1)

            for n in range(N + 1):
                if not residual:
                    if n < N:
                        variance(n, 1, "x_squared", "x_var")
                        new_h(n)
                    continue
                if n < N:
                    combine(n, 0)
                if n:
                    variance(n - 1, 0, "f_squared", "f_var")
                if n < N:
                    combine(n, 1)
                if n:
                    new_x(n - 1)
                if n < N:
                    combine(n, 2)
                if n and norm:
                    variance(n - 1, 1, "x_squared", "x_var")
                if n < N:
                    combine(n, 3)
                if n and norm:
                    new_h(n - 1)


def n_blocks(n_tiles):
    return n_tiles * TOPK + E


RING = 4


def load_expert(g, sp, layer, R, e, r):
    io = g.io
    for dst, src in ((R.wgu[:, r, :, 0:FF], io["moe_w_gate"][layer, e].rearrange("e (p k) f -> p (e k) f", k=KD)),
                     (R.wgu[:, r, :, FF:2 * FF], io["moe_w_up"][layer, e].rearrange("e (p k) f -> p (e k) f", k=KD)),
                     (R.wd[:, r, :, :], io["moe_w_down"][layer, e].rearrange("e (k p) n -> p (e k) n", p=P))):
        sp.dma_start(dst, src).then_inc(R.w_loaded[r], 16)


def stage_route(nc, g, name, layer, hT, tiles, R, F):
    t0, N = tiles[0], len(tiles)
    NB = n_blocks(N)
    BIG = 1e30
    with ExitStack() as s:
        wr = g.sb(s, "wr", [P, KD, E])
        bias = g.sb(s, "bias", [P, E])
        iota_i = g.sb(s, "iota_i", [P, P], i32)
        iota = g.sb(s, "iota", [P, P])
        tok = g.sb(s, "tok", [P, TT])
        aff = g.sb(s, "aff", [P, N, E])
        biased = g.sb(s, "biased", [P, N, E])
        m8 = g.sb(s, "m8", [P, N * 8, 8])
        gs = g.sb(s, "gs", [P, N, 8])
        g8 = g.sb(s, "g8", [P, N, 8])
        gi = g.sb(s, "gi", [P, N, 8], u32)
        gif = g.sb(s, "gif", [P, N, 8])
        eq = g.sb(s, "eq", [P, N, 8, 4])
        keep = g.sb(s, "keep", [P, N, 8])
        pen = g.sb(s, "pen", [P, N, 8])
        masked = g.sb(s, "masked", [P, N, E])
        e8 = g.sb(s, "e8", [P, N, 8])
        ei = g.sb(s, "ei", [P, N, 8], u32)
        eif = g.sb(s, "eif", [P, N, 8])
        spare = R.wgu[:, 2, :, :].rearrange("p k n -> p (k n)")
        OH = spare[:, 0:N * 8 * E].rearrange("p (c e) -> p c e", e=E)
        OX = spare[:, TT * 8 * E:(TT + 2) * 8 * E].rearrange("p (b c e) -> p b c e", b=2, e=E)
        Sel = g.sb(s, "Sel", [P, N, E])
        gk = g.sb(s, "gk", [P, N, 8])
        gsum = g.sb(s, "gsum", [P, N])
        cnt = g.sb(s, "cnt", [P, E])
        nb = g.sb(s, "nb", [P, E])
        ends = g.sb(s, "ends", [P, E])
        off = g.sb(s, "off", [P, E])
        cmp_ = g.sb(s, "cmp", [P, E])
        posm = g.sb(s, "posm", [P, N, E])
        posf = g.sb(s, "posf", [P, N * 8])
        posi = g.sb(s, "posi", [P, N * 8], i32)
        slot_i = g.sb(s, "slot_i", [P, N * 8], i32)
        blk_i = g.sb(s, "blk_i", [P, N * 8], i32)
        slot = g.sb(s, "slot", [P, N * 8])
        blk = g.sb(s, "blk", [P, N * 8])
        OS = g.sb(s, "OS", [P, 8, P])
        OB = g.sb(s, "OB", [P, 8, NB])
        eb = g.sb(s, "eb", [P, 1])
        npf = g.sb(s, "npf", [1, 1])
        w_loaded, logits_ps, aff_ready, sel_ready, rank_ps, eb_ready, eb_ps, oh_ready, rows_used, chain, iotas = g.sems(
            name, "w_loaded logits_ps aff_ready sel_ready rank_ps eb_ready eb_ps oh_ready rows_used chain iotas")
        wgu, wd = R.wgu[:, 3, :, :], R.wd[:, 3, :, :]
        sg, up, hm = (g.sb(s, what, [P, 2, FF]) for what in ("s_gate", "s_up", "s_hm"))
        hmT = g.sb(s, "s_hmT", [P, 2, KF, P])
        A = dict(zip("loaded gu taken h ht htc y yc".split(),
                     g.sems(name, "s_loaded s_gu s_taken s_h s_ht s_htc s_y s_yc")))
        gu_bank = lambda n: 5 if n % 2 == 0 else 0
        block = s.enter_context(nc.Block())

        @block.sync
        def _(sp):
            sp.dma_start(wr[:, :, :], g.io["moe_router"][layer].rearrange("(k p) e -> p k e", p=P)).then_inc(w_loaded, 16)
            sp.dma_start(bias[:, :], g.io["moe_bias"][layer].partition_broadcast(P)).then_inc(w_loaded, 16)
            sp.dma_start(wgu[:, :, 0:FF], g.io["moe_ws_gate"][layer].rearrange("(k p) f -> p k f", p=P)).then_inc(A["loaded"], 16)
            sp.dma_start(wgu[:, :, FF:2 * FF], g.io["moe_ws_up"][layer].rearrange("(k p) f -> p k f", p=P)).then_inc(A["loaded"], 16)
            sp.dma_start(wd[:, :, :], g.io["moe_ws_down"][layer].rearrange("(k p) n -> p k n", p=P)).then_inc(A["loaded"], 16)
            for r in range(2):
                load_expert(g, sp, layer, R, slice(r, r + 1), r)

        @block.gpsimd
        def _(pool):
            nc.gpsimd.iota(iota_i[:, :], pattern=[[1, P]], base=0, channel_multiplier=0).then_inc(iotas, 1)
            for n in range(N):
                pool.wait_ge(A["taken"], n + 1)
                nc.gpsimd.tensor_tensor(hm[:, n % 2, :], sg[:, n % 2, :], up[:, n % 2, :], ALU.mult).then_inc(A["h"], 1)

        @block.tensor
        def _(pe):
            def gate_up(n):
                if n == 1:
                    pe.wait_ge(aff_ready, 1)
                if n >= 2:
                    pe.wait_ge(A["htc"], n - 1)
                t = tiles[n]
                for k in range(KD):
                    last = nc.tensor.matmul(g.ps[:, gu_bank(n), :], hT[:, k, t * P:(t + 1) * P], wgu[:, k, :],
                                            start=(k == 0), stop=(k == KD - 1))
                last.then_inc(A["gu"], 1)

            def shared(n):
                pe.wait_ge(A["h"], n + 1)
                for f in range(KF):
                    last = nc.tensor.transpose(g.ps[:, gu_bank(n), f * P:(f + 1) * P], hm[:, n % 2, f * P:(f + 1) * P], g.ident[:, :])
                last.then_inc(A["ht"], 1)
                if n + 1 < N:
                    gate_up(n + 1)
                if n:
                    pe.wait_ge(A["yc"], n)
                pe.wait_ge(A["htc"], n + 1)
                for o in range(2):
                    for f in range(KF):
                        last = nc.tensor.matmul(g.ps[:, 6 + o, :], hmT[:, n % 2, f, :], wd[:, f, o * 512:(o + 1) * 512],
                                                start=(f == 0), stop=(f == KF - 1))
                last.then_inc(A["y"], 1)

            pe.wait_ge(w_loaded, 32)
            for n, t in enumerate(tiles):
                for k in range(KD):
                    last = nc.tensor.matmul(g.ps[:, 0, n * E:(n + 1) * E], hT[:, k, t * P:(t + 1) * P], wr[:, k, :],
                                            start=(k == 0), stop=(k == KD - 1))
            last.then_inc(logits_ps, 1)
            pe.wait_ge(A["loaded"], 48)
            gate_up(0)
            shared(0)
            pe.wait_ge(sel_ready, 1)
            for n in range(N):
                for m in range(n + 1):
                    nc.tensor.matmul(g.ps[:, 1, n * E:(n + 1) * E], (g.before if m == n else g.ones)[:, :], Sel[:, m, :],
                                     start=(m == 0), stop=(m == n))
            for m in range(N):
                last = nc.tensor.matmul(g.ps[:, 2, 0:E], g.ones[:, :], Sel[:, m, :], start=(m == 0), stop=(m == N - 1))
            last.then_inc(rank_ps, 1)
            shared(1)
            pe.wait_ge(eb_ready, 1)
            nc.tensor.matmul(g.ps[0:1, 3, 0:P], eb[:, :], g.ident[:, :], start=True, stop=True).then_inc(eb_ps, 1)
            for n in range(N):
                pe.wait_ge(oh_ready, n + 1)
                for k in range(TOPK):
                    last = nc.tensor.matmul(g.ps[:, 4, 0:NB], OS[:, k, :], OB[:, k, :],
                                            start=(n == 0 and k == 0), stop=(n == N - 1 and k == TOPK - 1))
                last.then_inc(rows_used, 1)
                if n >= 2:
                    shared(n)

        @block.scalar
        def _(act):
            def take(n):
                act.wait_ge(A["gu"], n + 1)
                nc.scalar.activation(sg[:, n % 2, :], g.ps[:, gu_bank(n), 0:FF], ACT.Silu)
                nc.scalar.activation(up[:, n % 2, :], g.ps[:, gu_bank(n), FF:2 * FF], ACT.Copy).then_inc(A["taken"], 1)

            act.wait_ge(logits_ps, 1)
            nc.scalar.activation(aff[:, :, :].rearrange("p n e -> p (n e)"), g.ps[:, 0, 0:N * E], ACT.Sigmoid).then_inc(aff_ready, 1)
            take(0)
            for n, t in enumerate(tiles):
                act.wait_ge(A["ht"], n + 1)
                nc.scalar.activation(hmT[:, n % 2, :, :].rearrange("p f r -> p (f r)"), g.ps[:, gu_bank(n), 0:FF], ACT.Copy)\
                    .then_inc(A["htc"], 1)
                if n + 1 < N:
                    take(n + 1)
                act.wait_ge(A["y"], n + 1)
                nc.scalar.activation(F[:, t, :], g.ps[:, 6:8, :].rearrange("p a c -> p (a c)"), ACT.Copy).then_inc(A["yc"], 1)

        @block.vector
        def _(dve):
            v = nc.vector
            link = Link(dve, chain)
            dve.wait_ge(iotas, 1)
            link.mark(v.tensor_copy(iota[:, :], iota_i[:, :]))
            link.mark(v.tensor_copy(tok[:, :], g.token_id[:, :]))
            dve.wait_ge(w_loaded, 32)
            dve.wait_ge(aff_ready, 1)
            link(v.tensor_tensor(biased[:, :, :], aff[:, :, :], bias[:, None, :].broadcast_to([P, N, E]), ALU.add))
            groups = biased[:, :, :].rearrange("p n (g e) -> p (n g) e", e=8)
            for j in range(N * 8):
                last = v.max(m8[:, j, :], groups[:, j, :])
            link(last)
            m8g = m8[:, :, :].rearrange("p (n g) e -> p n g e", g=8)
            link(v.tensor_tensor(gs[:, :, :], m8g[:, :, :, 0], m8g[:, :, :, 1], ALU.add))
            for n in range(N):
                last = v.max(g8[:, n, :], gs[:, n, :])
            link(last)
            for n in range(N):
                last = v.max_index(gi[:, n, :], g8[:, n, :], gs[:, n, :])
            link(last)
            link(v.tensor_copy(gif[:, :, :], gi[:, :, :]))
            for n in range(N):
                last = v.tensor_tensor(eq[:, n, :, :], iota[:, 0:8].unsqueeze(2).broadcast_to([P, 8, 4]),
                                       gif[:, n, 0:4].unsqueeze(1).broadcast_to([P, 8, 4]), ALU.is_equal)
            link(last)
            link(v.tensor_reduce(keep[:, :, :], eq[:, :, :, :], AX.X, ALU.add))
            link(v.tensor_scalar(pen[:, :, :], keep[:, :, :], -1.0, BIG, ALU.add, ALU.mult))
            over = lambda a: a[:, :, :].rearrange("p n g -> p (n g)").unsqueeze(2).broadcast_to([P, N * 8, 8])
            mg = masked[:, :, :].rearrange("p n (g e) -> p (n g) e", e=8)
            link(v.tensor_tensor(mg, groups, over(keep), ALU.mult))
            link(v.tensor_tensor(mg, mg, over(pen), ALU.add))
            for n in range(N):
                last = v.max(e8[:, n, :], masked[:, n, :])
            link(last)
            for n in range(N):
                last = v.max_index(ei[:, n, :], e8[:, n, :], masked[:, n, :])
            link(last)
            link(v.tensor_copy(eif[:, :, :], ei[:, :, :]))
            link(v.tensor_tensor(OH[:, :, :], iota[:, 0:E].unsqueeze(1).broadcast_to([P, N * 8, E]),
                                 eif[:, :, :].rearrange("p n k -> p (n k)").unsqueeze(2).broadcast_to([P, N * 8, E]), ALU.is_equal))
            v.tensor_reduce(Sel[:, :, :], OH[:, :, :].rearrange("p (n k) e -> p n e k", k=8), AX.X, ALU.add).then_inc(sel_ready, 1)

            def select(out, what, n):
                link(v.tensor_tensor(OX[:, n % 2, :, :], OH[:, n * 8:(n + 1) * 8, :],
                                     what[:, n, :].unsqueeze(1).broadcast_to([P, 8, E]), ALU.mult))
                link.mark(v.tensor_reduce(out, OX[:, n % 2, :, :], AX.X, ALU.add))

            for n in range(N):
                select(gk[:, n, :], aff, n)
            link.wait()
            link(v.tensor_reduce(gsum[:, :], gk[:, :, :], AX.X, ALU.add))
            link(v.reciprocal(gsum[:, :], gsum[:, :]))
            for n in range(N):
                last = v.tensor_scalar(R.gates[:, n, :], gk[:, n, :], gsum[:, n:n + 1], ROUTED_SCALE, ALU.mult, ALU.mult)
            link(last)
            dve.wait_ge(rank_ps, 1)
            link.mark(v.memset(nb[:, :], 1.0))
            link.mark(v.memset(OS[:, 0, 0:E], 1.0))
            link(v.tensor_copy(cnt[:, :], g.ps[:, 2, 0:E]))
            for j in range(1, TT):
                link(v.scalar_tensor_tensor(nb[:, :], cnt[:, :], float(P * j), nb[:, :], ALU.is_gt, ALU.add))
            link(v.tensor_tensor_scan(ends[:, :], OS[:, 0, 0:E], nb[:, :], 0.0, ALU.mult, ALU.add))
            link(v.tensor_tensor(off[:, :], ends[:, :], nb[:, :], ALU.subtract))
            link(v.tensor_scalar(cmp_[:, :], ends[:, :], tok[:, 0:1], None, ALU.is_le))
            link(v.tensor_reduce(eb[:, :], cmp_[:, :], AX.X, ALU.add))
            v.tensor_scalar(eb[:, :], eb[:, :], float(E - 1), None, ALU.min).then_inc(eb_ready, 1)
            link(v.tensor_scalar(npf[:, :], ends[0:1, E - 1:E], 0.5, 0.25, ALU.mult, ALU.add))
            link(v.tensor_copy(R.pairs[:, :], npf[:, :]))
            link(v.tensor_copy(R.ends[:, :], ends[0:1, :]))
            for n in range(N):
                last = v.scalar_tensor_tensor(posm[:, n, :], off[:, :], float(P), g.ps[:, 1, n * E:(n + 1) * E], ALU.mult, ALU.add)
            link(last)
            for n in range(N):
                select(posf[:, n * 8:(n + 1) * 8], posm, n)
            link.wait()
            link.mark(v.tensor_copy(posi[:, :], posf[:, :]))
            link(v.tensor_copy(R.pos[:, 0:N * 8], posf[:, :]))
            link.mark(v.tensor_scalar(slot_i[:, :], posi[:, :], P - 1, None, ALU.bitwise_and))
            link(v.tensor_scalar(blk_i[:, :], posi[:, :], 7, None, ALU.logical_shift_right))
            link.mark(v.tensor_copy(slot[:, :], slot_i[:, :]))
            link(v.tensor_copy(blk[:, :], blk_i[:, :]))
            for n, t in enumerate(tiles):
                if n:
                    dve.wait_ge(rows_used, n)
                v.tensor_tensor(OS[:, :, :], iota[:, :].unsqueeze(1).broadcast_to([P, 8, P]),
                                slot[:, n * 8:(n + 1) * 8].unsqueeze(2).broadcast_to([P, 8, P]), ALU.is_equal)
                link(v.tensor_tensor(OB[:, :, :], iota[:, 0:NB].unsqueeze(1).broadcast_to([P, 8, NB]),
                                     blk[:, n * 8:(n + 1) * 8].unsqueeze(2).broadcast_to([P, 8, NB]), ALU.is_equal))
                v.tensor_scalar(OB[:, :, :], OB[:, :, :], tok[:, t:t + 1], None, ALU.mult).then_inc(oh_ready, 1)
            dve.wait_ge(eb_ps, 1)
            v.tensor_copy(R.block_expert[:, :], g.ps[0:1, 3, 0:P])
            dve.wait_ge(rows_used, N)
            link(v.memset(R.rows[:, :], 0))
            link(v.tensor_copy(R.rows[:, 0:NB], g.ps[:, 4, 0:NB]))


def stage_experts(nc, g, name, layer, tiles, R):
    N = len(tiles)
    NB = n_blocks(N)
    io = g.io
    with ExitStack() as s:
        wgu, wd, w_loaded = R.wgu, R.wd, R.w_loaded
        idx = [g.sb(s, f"idx{b}", [P, 1], u32) for b in range(2)]
        xg = [g.sb(s, f"xg{b}", [P, D]) for b in range(2)]
        xT = [g.sb(s, f"xT{b}", [P, KD, P]) for b in range(2)]
        sg = [g.sb(s, f"sg{b}", [P, FF]) for b in range(2)]
        hm = [g.sb(s, f"hm{b}", [P, FF]) for b in range(2)]
        hmT = [g.sb(s, f"hmT{b}", [P, KF, P]) for b in range(2)]
        y = [g.sb(s, f"y{b}", [P, D]) for b in range(2)]
        tiny = g.sb(s, "tiny", [P, 3])
        tiny_made, = g.sems(name, "tiny_made")
        names = "gu_ps silu_done h_ready ht_ps ht_copied y_ps y_low y_high"
        M = dict(zip(names.split(), g.sems(name, names)))
        TW = {n: g.sems(name, f"{n}0 {n}1") for n in "idx_ready gathered xT_ps xT_copied y_stored passed".split()}
        block = s.enter_context(nc.Block())

        def gate_up(b, lhsT, rhs):
            for k in range(KD):
                last = nc.tensor.matmul(g.ps[:, 4 + b, :], lhsT(k), rhs(k), start=(k == 0), stop=(k == KD - 1))
            return last

        def turn_h(b):
            for f in range(KF):
                last = nc.tensor.transpose(g.ps[:, 4 + b, f * P:(f + 1) * P], hm[b][:, f * P:(f + 1) * P], g.ident[:, :])
            return last

        def down(b, bank, rhs):
            for o in range(2):
                for f in range(KF):
                    last = nc.tensor.matmul(g.ps[:, bank + o, :], hmT[b][:, f, :], rhs(f, o),
                                            start=(f == 0), stop=(f == KF - 1))
            return last

        @block.sync
        def _(sp):
            for b in range(2):
                sp.wait_ge(TW["gathered"][b], 16)
            for r in range(2, RING):
                load_expert(g, sp, layer, R, slice(r, r + 1), r)
            with sp.Fori(0, E // RING - 1) as i:
                for r in range(RING):
                    done = sp.value_load(R.ends[0:1, bass.ds(i * RING + r, 1)], min_val=1, max_val=NB)
                    sp.wait_ge(M["y_ps"], done)
                    load_expert(g, sp, layer, R, bass.ds(i * RING + (RING + r), 1), r)

        @block.gpsimd
        def _(pool):
            def gather(b):
                nc.gpsimd.indirect_dma_start(xg[b][:, :], None, g.h_rows, bass.IndirectOffsetOnAxis(ap=idx[b][:, 0:1], axis=0))\
                    .then_inc(TW["gathered"][b], 16)

            nc.gpsimd.memset(tiny[:, :], 0.0).then_inc(tiny_made, 1)
            pool.wait_ge(tiny_made, 1)
            for b in range(2):
                pool.sem_inc(TW["passed"][b], 1)
                pool.wait_ge(TW["idx_ready"][b], 1)
                gather(b)
            pairs = pool.value_load(R.pairs[0:1, 0:1], min_val=1, max_val=NB // 2)
            with pool.Fori(0, NB // 2) as i:
                with pool.If(i < pairs):
                    for b in range(2):
                        pool.wait_ge(TW["xT_ps"][b], i + 1)
                        pool.wait_ge(TW["idx_ready"][b], i + 2)
                        pool.wait_ge(TW["passed"][b], i + 1)
                        nc.gpsimd.tensor_tensor(tiny[:, 1 + b:2 + b], tiny[:, 0:1], tiny[:, 0:1], ALU.add).then_inc(TW["passed"][b], 1)
                        gather(b)

        @block.tensor
        def _(pe):
            def turn_x(b):
                cols = xg[b][:, :].rearrange("p (q k) -> p k q", k=KD)
                for k in range(KD):
                    last = nc.tensor.transpose(g.ps[:, 2 * b + k // 4, (k % 4) * P:(k % 4 + 1) * P], cols[:, k, :], g.ident[:, :])
                last.then_inc(TW["xT_ps"][b], 1)

            for b in range(2):
                pe.wait_ge(TW["gathered"][b], 16)
                turn_x(b)
            pairs = pe.value_load(R.pairs[0:1, 0:1], min_val=1, max_val=NB // 2)
            with pe.Fori(0, NB // 2) as i:
                with pe.If(i < pairs):
                    slot = []
                    for b in range(2):
                        e = pe.value_load(R.block_expert[0:1, bass.ds(i * 2 + b, 1)], min_val=0, max_val=E - 1)
                        slot.append(pe.snap(e & (RING - 1)))
                        pe.wait_ge(TW["xT_copied"][b], i + 1)
                        for r in range(RING):
                            pe.wait_ge(w_loaded[r], ((e + (RING - r)) >> 2) * 48 + 48)
                        gate_up(b, lambda k: xT[b][:, k, :],
                                lambda k: wgu[:, bass.ds(slot[b], 1), k, :].rearrange("p a n -> p (a n)")).then_inc(M["gu_ps"], 1)
                    for b in range(2):
                        pe.wait_ge(M["h_ready"], i * 2 + (b + 1))
                        turn_h(b).then_inc(M["ht_ps"], 1)
                        pe.wait_ge(TW["gathered"][b], i * 16 + 32)
                        if b == 0:
                            pe.wait_ge(M["y_low"], i * 2 + 1)
                            pe.wait_ge(M["y_high"], i * 2 + 1)
                        turn_x(b)
                    for b in range(2):
                        pe.wait_ge(M["ht_copied"], i * 2 + (b + 1))
                        if b == 1:
                            pe.wait_ge(TW["xT_copied"][0], i + 2)
                        down(b, 6 if b == 0 else 0, lambda f, o: wd[:, bass.ds(slot[b], 1), f, o * 512:(o + 1) * 512].rearrange("p a n -> p (a n)"))\
                            .then_inc(M["y_ps"], 1)

        @block.scalar
        def _(act):
            def silu(b, waited, at, done):
                act.wait_ge(waited, at)
                nc.scalar.activation(sg[b][:, :], g.ps[:, 4 + b, 0:FF], ACT.Silu).then_inc(done, 1)

            def take_ht(b, waited, at, done):
                act.wait_ge(waited, at)
                nc.scalar.activation(hmT[b][:, :, :].rearrange("p f r -> p (f r)"), g.ps[:, 4 + b, 0:FF], ACT.Copy).then_inc(done, 1)

            def take_x(b, at):
                act.wait_ge(TW["xT_ps"][b], at)
                nc.scalar.activation(xT[b][:, :, :].rearrange("p k r -> p (k r)"),
                                     g.ps[:, 2 * b:2 * b + 2, :].rearrange("p a c -> p (a c)"), ACT.Copy)\
                    .then_inc(TW["xT_copied"][b], 1)

            for r in range(RING):
                act.sem_inc(w_loaded[r], 48)
            act.sem_inc(M["y_low"], 1)
            for b in range(2):
                act.sem_inc(TW["y_stored"][b], 16)
                take_x(b, 1)
            pairs = act.value_load(R.pairs[0:1, 0:1], min_val=1, max_val=NB // 2)
            with act.Fori(0, NB // 2) as i:
                with act.If(i < pairs):
                    for b in range(2):
                        silu(b, M["gu_ps"], i * 2 + (b + 1), M["silu_done"])
                    for b in range(2):
                        take_ht(b, M["ht_ps"], i * 2 + (b + 1), M["ht_copied"])
                        take_x(b, i + 2)
                    for b in range(2):
                        act.wait_ge(M["y_ps"], i * 2 + (b + 1))
                        act.wait_ge(TW["y_stored"][b], i * 16 + 16)
                        nc.scalar.activation(y[b][:, 0:512], g.ps[:, 6 if b == 0 else 0, :], ACT.Copy).then_inc(M["y_low"], 1)
                        act.wait_ge(M["y_low"], i * 2 + (b + 2))
                        act.wait_ge(M["y_high"], i * 2 + (b + 2))
                        act.dma_start(g.y_rows[bass.ds(i * (2 * P) + b * P, P), :], y[b][:, :]).then_inc(TW["y_stored"][b], 16)
            for b in range(2):
                act.wait_ge(TW["y_stored"][b], pairs * 16 + 16)
                nc.scalar.activation(y[b][:, 0:1], y[b][:, 0:1], ACT.Copy)

        @block.vector
        def _(dve):
            def multiply(b, waited, at, done):
                dve.wait_ge(waited, at)
                nc.vector.tensor_tensor(hm[b][:, :], sg[b][:, :], g.ps[:, 4 + b, FF:2 * FF], ALU.mult).then_inc(done, 1)

            for b in range(2):
                nc.vector.tensor_copy(idx[b][:, :], R.rows[:, b:b + 1]).then_inc(TW["idx_ready"][b], 1)
            dve.sem_inc(M["y_high"], 1)
            for b in range(2):
                dve.wait_ge(TW["gathered"][b], 16)
                nc.vector.tensor_copy(idx[b][:, :], R.rows[:, 2 + b:3 + b]).then_inc(TW["idx_ready"][b], 1)
            pairs = dve.value_load(R.pairs[0:1, 0:1], min_val=1, max_val=NB // 2)
            with dve.Fori(0, NB // 2) as i:
                with dve.If(i < pairs):
                    for b in range(2):
                        multiply(b, M["silu_done"], i * 2 + (b + 1), M["h_ready"])
                    for b in range(2):
                        dve.wait_ge(TW["gathered"][b], i * 16 + 32)
                        nc.vector.tensor_copy(idx[b][:, :], R.rows[:, bass.ds(i * 2 + (4 + b), 1)]).then_inc(TW["idx_ready"][b], 1)
                    for b in range(2):
                        dve.wait_ge(M["y_ps"], i * 2 + (b + 1))
                        dve.wait_ge(TW["y_stored"][b], i * 16 + 16)
                        nc.vector.tensor_scalar(y[b][:, 512:D], g.ps[:, 7 if b == 0 else 1, :], 1.0, None, ALU.mult)\
                            .then_inc(M["y_high"], 1)


def program(nc, io):
    g = Core()
    g.io = io
    g.names = {}
    outer = ExitStack()
    with outer:
        def sb(stack, name, shape, dt=fp32):
            g.names[name] = g.names.get(name, 0) + 1
            return stack.enter_context(nc.sbuf_tensor(f"{name}_{g.names[name]}", shape, dt))

        def sem(name):
            return nc.alloc_semaphore(name)

        def recycle():
            nc.clear_and_free_semaphores(nc.allocated_since(g.kept))
            nc.all_engine_barrier()

        g.sb, g.sem = sb, sem
        g.sems = lambda stage, names: [sem(f"{stage}_{n}") for n in names.split()]
        g.mod_vecs = nc.dram_tensor("mod_vecs", [2, 2, 6, D], fp32).ap()
        g.h_rows = nc.dram_tensor("h_rows", [T, D], fp32).ap()
        g.x_rows = nc.dram_tensor("x_rows", [T, D], fp32).ap()
        g.ps = outer.enter_context(nc.psum_tensor("ps", [P, 8, 512], fp32))
        g.ident = sb(outer, "ident", [P, P])
        g.ones = sb(outer, "ones", [P, P])
        g.before = sb(outer, "before", [P, P])
        g.token_id = sb(outer, "token_id", [P, TT], i32)
        g.mask = sb(outer, "mask", [P, 2, P], i32)
        g.eps = sb(outer, "eps", [P, 1])
        hT = sb(outer, "hT", [P, KD, T])
        g.cT = sb(outer, "cT", [P, 16])
        g.y_rows = nc.dram_tensor("y_rows", [n_blocks(TT) * P, D], fp32).ap()
        g.ya_rows = nc.dram_tensor("ya_rows", [P, KD, T], fp32).ap()
        g.yb_rows = nc.dram_tensor("yb_rows", [P, KD, T], fp32).ap()
        settled = sem("settled")

        def hold(eng, n=1):
            eng.wait_ge(settled, n)
        g.hold = hold
        g.settled = settled

        stage_constants(nc, g)
        g.kept = nc.snapshot_sems()
        x0 = lambda t: tile_rows(io["ctx"][0], t) if t < CT else tile_rows(io["x"][0], t - CT)
        x_row = lambda t: tile_rows(g.x_rows, t)
        out_row = lambda t: tile_rows(io["out"][0], t - CT)
        every, latent = list(range(TT)), list(range(CT, TT))

        def moe(layer, X, tiles, **tail):
            name = f"moe{layer}"
            with ExitStack() as s:
                R = Core()
                R.gates = sb(s, "gates", [P, TT, TOPK])
                R.pos = sb(s, "pos", [P, TT * TOPK], u32)
                R.rows = sb(s, "rows", [P, n_blocks(TT) + 4], u32)
                R.ends = sb(s, "ends", [1, E], i32)
                R.block_expert = sb(s, "block_expert", [1, P], i32)
                R.pairs = sb(s, "pairs", [1, 1], i32)
                F = sb(s, "F", [P, TT, D])
                recycle()
                ring = ExitStack()
                R.wgu = sb(ring, "wgu", [P, RING, KD, 2 * FF])
                R.wd = sb(ring, "wd", [P, RING, KF, D])
                R.w_loaded = g.sems(name, " ".join(f"w_loaded{r}" for r in range(RING)))
                stage_route(nc, g, name + "r", layer, hT, tiles, R, F)
                stage_experts(nc, g, name + "e", layer, tiles, R)
                ring.close()
                recycle()
                stage_rows(nc, g, name + "x", tiles, hT, X, experts=(R, F), residual=(layer, 1), **tail)

        stage_modulation(nc, g, hT, x0)
        stage_lru(nc, g, hT)
        stage_attention(nc, g, "gla", hT, True)
        with ExitStack() as s:
            X = sb(s, "X", [P, TT, D])
            stage_rows(nc, g, "r0", every, hT, X, mix=(io["ab_w_out"][0], ((g.ya_rows, KD), (g.yb_rows, KD))),
                       residual=(0, 0), norm=(0, 1), load_x=x0, store_h=True)
            moe(0, X, every, norm=(1, 0), store_x=x_row, column_major=True)
        stage_attention(nc, g, "hgrn", hT, False)
        with ExitStack() as s:
            X = sb(s, "X", [P, TT, D])
            stage_rows(nc, g, "r1", latent, hT, X, mix=(io["c_w_out"][0], ((g.yb_rows, KD),)),
                       residual=(1, 0), norm=(1, 1), load_x=x_row, store_h=True)
            moe(1, X, latent, store_x=out_row)



_INPUTS = ["x", "c", "ctx", "c_ctx", "mod_w", "mod_b", "pre_gain", "post_gain", "ab_w_in", "ab_conv_w", "ab_conv_b",
           "ab_lru_wa", "ab_lru_ba", "ab_lru_wi", "ab_lru_bi", "ab_lru_lambda", "ab_gla_wa2", "ab_gla_ba", "ab_w_out",
           "c_w_in", "hgrn_lb_logits", "c_w_out", "moe_router", "moe_bias", "moe_w_gate", "moe_w_up", "moe_w_down",
           "moe_ws_gate", "moe_ws_up", "moe_ws_down"]


def kernel(**inputs):
    import numpy as np
    import concourse.bacc as bacc
    from concourse.bass_utils import run_bass_kernel_spmd

    nc = bacc.Bacc("TRN2", target_bir_lowering=False, num_devices=1)
    arrays, io = {}, {}
    for name in _INPUTS:
        a = np.ascontiguousarray(inputs[name])
        arrays[f"in_{name}"] = a
        io[name] = nc.dram_tensor(f"in_{name}", a.shape, mybir.dt.from_np(a.dtype), kind="ExternalInput").ap()
    io["out"] = nc.dram_tensor("out_0", (1, LAT, D), fp32, kind="ExternalOutput").ap()
    program(nc, io)
    r = run_bass_kernel_spmd(nc, [arrays], core_ids=[0])
    return r.results[0]["out_0"]
```
